# Optimizing a Trainium2 kernel written in Bass

```python
import math
import jax, jax.numpy as jnp
from jax import lax
import numpy as np

D_MODEL = 1024
BATCH = 1
SEQ = 1024
DEPTH = 1

CHUNK = 64
Q_BLOCK = 128
EPS = 1e-6

MIX_WIDTH = D_MODEL
SB_HEAD_DIM = 64
SB_HEADS = (MIX_WIDTH // 2) // SB_HEAD_DIM
SB_WIDTH = SB_HEADS * SB_HEAD_DIM
MLA_V = 64
MLA_HEADS = (MIX_WIDTH - SB_WIDTH) // MLA_V
MLA_WIDTH = MLA_HEADS * MLA_V
MLA_NOPE = 64
MLA_ROPE = 32
MLA_Q_RANK = 384
MLA_KV_RANK = 256
ROPE_THETA = 10000.0

IN_SPLITS = (SB_WIDTH, SB_WIDTH, SB_WIDTH, MLA_Q_RANK, MLA_KV_RANK, MLA_ROPE)
IN_WIDTH = sum(IN_SPLITS)

MEM_TOKENS = 256
MEM_HEADS = 4
MEM_HEAD_DIM = D_MODEL // MEM_HEADS

N_GROUPS = 4
EXPERTS_PER_GROUP = 4
N_EXPERTS = N_GROUPS * EXPERTS_PER_GROUP
EXPERT_TOP_K = 2
EXPERT_FF = 512

kernel_name = "hybrid_stickbreak_mla_mem_hmoe_layer"

def rms_norm(x, g):
    xf = x.astype(jnp.float32)
    y = xf * lax.rsqrt(jnp.mean(xf * xf, axis=-1, keepdims=True) + EPS)
    return (y * g.astype(jnp.float32)).astype(x.dtype)

def rope_tables(positions, rot_dim, dtype):
    half = rot_dim // 2
    inv_freq = ROPE_THETA ** (-(jnp.arange(half, dtype=jnp.float32) * 2.0 / rot_dim))
    ang = positions.astype(jnp.float32)[..., None] * inv_freq
    return jnp.cos(ang).astype(dtype), jnp.sin(ang).astype(dtype)

def apply_rope(x, cos, sin):
    half = x.shape[-1] // 2
    x1, x2 = x[..., :half], x[..., half:]
    return jnp.concatenate([x1 * cos - x2 * sin, x2 * cos + x1 * sin], axis=-1)

def stick_breaking_attention(q, k, v):
    S, dh = q.shape[2], q.shape[3]
    scale = dh ** -0.5
    outs = []
    for qb in range(S // Q_BLOCK):
        q0 = qb * Q_BLOCK
        L = q0 + Q_BLOCK
        z = jnp.einsum('bhqd,bhkd->bhqk', q[:, :, q0:L], k[:, :, :L]).astype(jnp.float32) * scale
        t_idx = q0 + jnp.arange(Q_BLOCK)[:, None]
        s_idx = jnp.arange(L)[None, :]
        past = s_idx < t_idx
        log_fail = jnp.where(past, jax.nn.log_sigmoid(-z), 0.0)
        between = lax.cumsum(log_fail, axis=3, reverse=True) - log_fail
        w = jnp.where(past, jnp.exp(jax.nn.log_sigmoid(z) + between), 0.0)
        outs.append(jnp.einsum('bhqk,bhkd->bhqd', w.astype(v.dtype), v[:, :, :L]))
    return jnp.concatenate(outs, axis=2)

def chunk_causal_attention(q, k, v):
    S, dk = q.shape[2], q.shape[3]
    scale = dk ** -0.5
    outs = []
    for qb in range(S // Q_BLOCK):
        q0 = qb * Q_BLOCK
        L = q0 + Q_BLOCK
        s = jnp.einsum('bhqd,bhkd->bhqk', q[:, :, q0:L], k[:, :, :L]).astype(jnp.float32) * scale
        t_chunk = (q0 + jnp.arange(Q_BLOCK))[:, None] // CHUNK
        s_chunk = jnp.arange(L)[None, :] // CHUNK
        s = jnp.where(s_chunk <= t_chunk, s, -jnp.inf)
        p = jax.nn.softmax(s, axis=-1)
        outs.append(jnp.einsum('bhqk,bhkd->bhqd', p.astype(v.dtype), v[:, :, :L]))
    return jnp.concatenate(outs, axis=2)

def setup_inputs(seed: int = 0) -> dict:
    key = jax.random.key(seed)
    ks = jax.random.split(key, 40)
    f32 = jnp.float32

    def w(i, shape, fan_in):
        return jax.random.normal(ks[i], shape, f32) * (fan_in ** -0.5)

    def gain(i, n):
        return 1.0 + 0.05 * jax.random.normal(ks[i], (n,), f32)

    x = jax.random.normal(ks[0], (BATCH, SEQ, D_MODEL), f32)
    mem = jax.random.normal(ks[1], (BATCH, MEM_TOKENS, D_MODEL), f32)
    offsets = jax.random.randint(ks[2], (BATCH, 1), 0, 4096, dtype=jnp.int32)
    positions = offsets + jnp.arange(SEQ, dtype=jnp.int32)[None, :]
    return {
        "x": x,
        "mem": mem,
        "positions": positions,
        "norm_mix_g": gain(3, D_MODEL),
        "w_in": w(4, (D_MODEL, IN_WIDTH), D_MODEL),
        "mla_q_norm_g": gain(5, MLA_Q_RANK),
        "w_uq": w(6, (MLA_Q_RANK, MLA_HEADS * (MLA_NOPE + MLA_ROPE)), MLA_Q_RANK),
        "mla_kv_norm_g": gain(7, MLA_KV_RANK),
        "w_ukv": w(8, (MLA_KV_RANK, MLA_HEADS * (MLA_NOPE + MLA_V)), MLA_KV_RANK),
        "mla_qn_g": gain(9, MLA_NOPE),
        "mla_qr_g": gain(10, MLA_ROPE),
        "mla_kn_g": gain(11, MLA_NOPE),
        "mla_kr_g": gain(12, MLA_ROPE),
        "sb_out_g": gain(13, SB_WIDTH),
        "mla_out_g": gain(14, MLA_WIDTH),
        "w_o": w(15, (MIX_WIDTH, D_MODEL), MIX_WIDTH),
        "norm_mem_g": gain(16, D_MODEL),
        "mem_src_g": gain(17, D_MODEL),
        "w_mq": w(18, (D_MODEL, D_MODEL), D_MODEL),
        "w_mkv": w(19, (D_MODEL, 2 * D_MODEL), D_MODEL),
        "mem_qhead_g": gain(20, MEM_HEAD_DIM),
        "mem_khead_g": gain(21, MEM_HEAD_DIM),
        "w_mo": w(22, (D_MODEL, D_MODEL), D_MODEL),
        "norm_moe_g": gain(23, D_MODEL),
        "w_group": w(24, (D_MODEL, N_GROUPS), D_MODEL),
        "b_group": 0.01 * jax.random.normal(ks[25], (N_GROUPS,), f32),
        "w_router": w(26, (D_MODEL, N_EXPERTS), D_MODEL),
        "b_router": 0.01 * jax.random.normal(ks[27], (N_EXPERTS,), f32),
        "w_gate": w(28, (N_EXPERTS, D_MODEL, EXPERT_FF), D_MODEL),
        "w_up": w(29, (N_EXPERTS, D_MODEL, EXPERT_FF), D_MODEL),
        "w_down": w(30, (N_EXPERTS, EXPERT_FF, D_MODEL), EXPERT_FF),
    }

def reference(x, mem, positions, norm_mix_g, w_in, mla_q_norm_g, w_uq, mla_kv_norm_g, w_ukv,
              mla_qn_g, mla_qr_g, mla_kn_g, mla_kr_g, sb_out_g, mla_out_g, w_o,
              norm_mem_g, mem_src_g, w_mq, w_mkv, mem_qhead_g, mem_khead_g, w_mo,
              norm_moe_g, w_group, b_group, w_router, b_router, w_gate, w_up, w_down):
    B, S, D = x.shape
    cos, sin = rope_tables(positions, MLA_ROPE, x.dtype)
    h = x
    for _ in range(DEPTH):
        hn = rms_norm(h, norm_mix_g)
        proj = hn @ w_in
        cuts = list(np.cumsum(IN_SPLITS)[:-1])
        sb_q, sb_k, sb_v, c_q, c_kv, k_rope = jnp.split(proj, cuts, axis=-1)

        to_heads = lambda t: t.reshape(B, S, SB_HEADS, SB_HEAD_DIM).transpose(0, 2, 1, 3)
        sb = stick_breaking_attention(to_heads(sb_q), to_heads(sb_k), to_heads(sb_v))
        sb = sb.transpose(0, 2, 1, 3).reshape(B, S, SB_WIDTH)

        q = (rms_norm(c_q, mla_q_norm_g) @ w_uq).reshape(B, S, MLA_HEADS, MLA_NOPE + MLA_ROPE)
        kv = (rms_norm(c_kv, mla_kv_norm_g) @ w_ukv).reshape(B, S, MLA_HEADS, MLA_NOPE + MLA_V)
        q_nope = rms_norm(q[..., :MLA_NOPE], mla_qn_g)
        q_rope = rms_norm(q[..., MLA_NOPE:], mla_qr_g)
        k_nope = rms_norm(kv[..., :MLA_NOPE], mla_kn_g)
        v_mla = kv[..., MLA_NOPE:]
        k_rope = rms_norm(k_rope, mla_kr_g)
        q_rope = apply_rope(q_rope, cos[:, :, None], sin[:, :, None])
        k_rope = apply_rope(k_rope, cos, sin)
        q_full = jnp.concatenate([q_nope, q_rope], axis=-1)
        k_full = jnp.concatenate(
            [k_nope, jnp.broadcast_to(k_rope[:, :, None], (B, S, MLA_HEADS, MLA_ROPE))], axis=-1)
        mla = chunk_causal_attention(q_full.transpose(0, 2, 1, 3), k_full.transpose(0, 2, 1, 3),
                                     v_mla.transpose(0, 2, 1, 3))
        mla = mla.transpose(0, 2, 1, 3).reshape(B, S, MLA_WIDTH)

        mixed = jnp.concatenate([rms_norm(sb, sb_out_g), rms_norm(mla, mla_out_g)], axis=-1)
        h = h + mixed @ w_o

        hq = rms_norm(h, norm_mem_g)
        mn = rms_norm(mem, mem_src_g)
        mq = rms_norm((hq @ w_mq).reshape(B, S, MEM_HEADS, MEM_HEAD_DIM), mem_qhead_g)
        mkv = (mn @ w_mkv).reshape(B, MEM_TOKENS, 2, MEM_HEADS, MEM_HEAD_DIM)
        mk = rms_norm(mkv[:, :, 0], mem_khead_g)
        mv = mkv[:, :, 1]
        sc = jnp.einsum('bshd,bmhd->bhsm', mq, mk).astype(jnp.float32) * (MEM_HEAD_DIM ** -0.5)
        p = jax.nn.softmax(sc, axis=-1).astype(mv.dtype)
        mo = jnp.einsum('bhsm,bmhd->bshd', p, mv).reshape(B, S, D)
        h = h + mo @ w_mo

        t = rms_norm(h, norm_moe_g).reshape(B * S, D)
        g_prob = jax.nn.softmax((t @ w_group).astype(jnp.float32) + b_group.astype(jnp.float32), axis=-1)
        g_idx = jnp.argmax(g_prob, axis=-1)
        g_w = jnp.take_along_axis(g_prob, g_idx[:, None], axis=-1)
        e_logits = ((t @ w_router).astype(jnp.float32) + b_router.astype(jnp.float32)
                    ).reshape(-1, N_GROUPS, EXPERTS_PER_GROUP)
        e_logits = jnp.take_along_axis(e_logits, g_idx[:, None, None], axis=1)[:, 0]
        e_prob = jax.nn.softmax(e_logits, axis=-1)
        top_p, top_i = lax.top_k(e_prob, EXPERT_TOP_K)
        weights = g_w * top_p / jnp.sum(top_p, axis=-1, keepdims=True)
        expert_id = g_idx[:, None] * EXPERTS_PER_GROUP + top_i
        gates = jnp.sum(jax.nn.one_hot(expert_id, N_EXPERTS, dtype=jnp.float32) * weights[..., None],
                        axis=1).astype(t.dtype)
        moe = jnp.zeros_like(t)
        for e in range(N_EXPERTS):
            he = jax.nn.silu(t @ w_gate[e]) * (t @ w_up[e])
            moe = moe + gates[:, e:e + 1] * (he @ w_down[e])
        h = h + moe.reshape(B, S, D)
    return h


_drawn_inputs = setup_inputs


def setup_inputs(seed=0):
    import zlib

    import numpy as np

    out = dict(_drawn_inputs(seed))
    spreads = {}
    factors = {'mla_qr_g': 2.835,
     'mla_kr_g': 3.291,
     'norm_mem_g': 8.0,
     'mem_src_g': 5.296,
     'mem_qhead_g': 8.0,
     'mem_khead_g': 8.0,
     'b_group': 47.807,
     'b_router': 58.6,
     'norm_moe_g': 7.026}
    for name, (base, spread) in spreads.items():
        noise = np.random.default_rng([zlib.crc32(name.encode()), seed]).standard_normal(out[name].shape)
        drawn = base * np.exp(spread * noise) if base else spread * noise
        out[name] = __import__('jax').numpy.asarray(drawn.astype(out[name].dtype))
    for name, factor in factors.items():
        out[name] = (out[name] * factor).astype(out[name].dtype)
    return out
```

```python
import math

import numpy as np
import concourse.bass as bass
from concourse import mybir
from contextlib import ExitStack

F32 = mybir.dt.float32
BF16 = mybir.dt.bfloat16
I32 = mybir.dt.int32
ACT = mybir.ActivationFunctionType
ALU = mybir.AluOpType
AX = mybir.AxisListType

P = 128
SEQ, DM, MEM = 1024, 1024, 256
T, DC, MT = SEQ // P, DM // P, MEM // P
EPS = 1e-6
HEADS, HD = 8, 64
PAIRS = HEADS // 2
NOPE, ROPE = 64, 32
QK = NOPE + ROPE
HALF = ROPE // 2
QR, KVR = 384, 256
SBW = HEADS * HD
MLA0 = 3 * SBW
MLAW = QR + KVR + ROPE
THETA = 10000.0
MH, MHD = 4, 256
NG, EG = 4, 4
NE, FF = NG * EG, 512
FC = FF // P
GRP = 4
SLOTS = (2 * SEQ) // P + NE
TAB = SLOTS + 2
BIG = 64.0


class Steps:

    def __init__(self, eng, own):
        self.eng, self.own, self.counts, self.last = eng, own, {}, None

    def __call__(self, ins, sem=None):
        sem = self.own if sem is None else sem
        self.counts[sem.name] = self.counts.get(sem.name, 0) + 1
        ins.then_inc(sem, 1)
        self.last = (sem, self.counts[sem.name])

    def settle(self):
        self.eng.wait_ge(*self.last)


def transposition_rounds():
    rounds = []

    def add(kind, key, engine, n=2):
        for half in range(n):
            rounds.append(((kind, key, half), engine))

    for m in range(MT):
        add("mem", m, "dve")
    for j in range(4):
        for t in (2 * j, 2 * j + 1):
            add("x", t, "dve")
        if j in (1, 2):
            add("mk", j - 1, "dve")
    for u in range(2 * HEADS):
        add("sb", u, "act", 4 * (u % 2) + 4)
    for i in range(T + 2):
        if i >= 2:
            add("qf", i - 2, "act")
            add("kf", i - 2, "act")
        if i < T:
            add("c", i, "dve")
    for u in range(2 * HEADS):
        add("mla", u, "act", 4 * (u % 2) + 4)
    for i in range(T + 2):
        if i < T:
            add("stats", i, "dve", 1)
        if 1 <= i <= T:
            add("mqT", i - 1, "act")
        if i < T:
            add("hT", i, "act")
        if 1 <= i <= T:
            add("pT", i - 1, "act")
        if i >= 2:
            add("tT", i - 2, "act")
            add("router", i - 2, "dve", 1)
    add("rank", 0, "dve", 1)
    return rounds


def moe_layer(nc, x, mem, positions, norm_mix_g, w_in, mla_q_norm_g, w_uq, mla_kv_norm_g, w_ukv,
              mla_qn_g, mla_qr_g, mla_kn_g, mla_kr_g, sb_out_g, mla_out_g, w_o, norm_mem_g,
              mem_src_g, w_mq, w_mkv, mem_qhead_g, mem_khead_g, w_mo, norm_moe_g, w_group, b_group,
              w_router, b_router, w_gate, w_up, w_down, out, debug=None):
    ROUNDS = transposition_rounds()
    ROUND = {key: i for i, (key, _) in enumerate(ROUNDS)}
    EMPTIED = []
    seen = {"act": 0, "dve": 0}
    for _, engine in ROUNDS:
        seen[engine] += 1
        EMPTIED.append((engine, seen[engine]))

    x2, mem2, out2 = x[0], mem[0], out[0]
    mkT_dram = nc.dram_tensor("mkT_spill", [P, DC * MEM], F32).ap()
    mv_dram = nc.dram_tensor("mv_spill", [P, MT * DM], F32).ap()
    tn_dram = nc.dram_tensor("tn_rows", [SEQ, DM], F32).ap()
    tok_dram = nc.dram_tensor("slot_tokens", [P * TAB, 1], I32).ap()
    y_dram = nc.dram_tensor("expert_rows", [SLOTS * P, DM], F32).ap()

    ctx = ExitStack()
    with ctx:
        def sem(name):
            return ctx.enter_context(nc.semaphore(name))

        def small(name, shape, dt=F32):
            return ctx.enter_context(nc.sbuf_tensor(name, shape, dt))

        ARENA = 50720
        arena = small("arena", [P, ARENA])
        psum = ctx.enter_context(nc.psum_tensor("psum", [P, 8, 512], F32))

        def cut(at, *dims):
            n = math.prod(dims)
            assert at + n <= ARENA
            v = arena[:, at:at + n]
            if len(dims) == 2:
                v = v.rearrange("p (a b) -> p a b", a=dims[0])
            elif len(dims) == 3:
                v = v.rearrange("p (a b c) -> p a b c", a=dims[0], b=dims[1])
            return v

        hnT = cut(0, DC, SEQ)
        mixT = cut(8192, DC, SEQ)
        XIN = 4
        xin = cut(8192, XIN, DM)
        mnT = cut(12288, DC, MEM)
        k_raw = cut(14336, MT, DM)
        w_mk = cut(16384, DC, DM)
        w_mv = cut(24576, DC, DM)
        w_qkv = cut(32768, DC, 3 * SBW)
        mv0 = cut(45056, MT, DM)
        mkT0 = cut(47104, DC, MEM)
        qz = cut(16384, HEADS, SEQ)
        kT = cut(24576, PAIRS, SEQ)
        v_sb = cut(28672, T, SBW)
        f_sb = cut(32768, 2, SEQ)
        g_sb = cut(34816, 2, SEQ)
        w_rows = cut(36864, 2, GRP, SEQ)
        wT_sb = cut(45056, 2, 512)
        fall = cut(46080, 2, SEQ + 1)
        zeros = cut(48640, 1)
        mqT_h = cut(16384, HEADS, SEQ)
        mkT_h = cut(24576, HEADS, SEQ)
        v_mla = cut(32768, T, SBW)
        w_c = cut(36864, DC, MLAW)
        w_q = cut(42240, 3, HEADS * QK)
        w_kv = cut(44544, 2, HEADS * P)
        cn = cut(46592, QR + KVR)
        cT = cut(47232, 5, P)
        qf = cut(47872, HEADS, QK)
        kf = cut(48640, HEADS, QK)
        sq = cut(49408, HEADS, QK)
        p_rows = cut(36864, 2, GRP, SEQ)
        pT_sb = cut(45056, 2, 512)
        wo_sb = cut(0, DC, DM)
        wmq_sb = cut(16384, DC, DM)
        wmo_sb = cut(24576, DC, DM)
        x_in = cut(32768, DM)
        h1 = cut(33792, 2, DM)
        h1T = cut(35840, DC, P)
        mq_sb = cut(36864, DM)
        mqT = cut(37888, DC, P)
        mp = cut(38912, MH, MEM)
        mpT = cut(39936, MH * MT, P)
        moT = cut(40960, DC, P)
        tn = cut(41984, DM)
        tT = cut(43008, DC, P)
        mix_sq = cut(44032, DC, P)
        moe_g = cut(45056, DM)
        mkT1 = cut(46080, DC, MEM)
        mv1 = cut(48128, MT, DM)
        junk = cut(50176, 544)
        junk_b = junk.bitcast(BF16)
        h2 = mixT
        wexp = [(cut(16384 + 12288 * b, DC, FF), cut(20480 + 12288 * b, DC, FF),
                 cut(24576 + 12288 * b, FC, DM)) for b in range(2)]
        xg = cut(40960, 2, DM)
        xT = cut(43008, 2, DC, P)
        silu = cut(45056, FF)
        hrow = cut(45568, FF)
        hTe = cut(46080, FC, P)
        ysb = cut(46592, 2, DM)
        rt = [cut(40960 + P * i, T, NE) for i in range(12)]
        y1 = cut(16384, 2, DM)
        y2 = cut(18432, 2, DM)
        yo = cut(20480, 2, DM)

        ident = small("ident", [P, P])
        before = small("before", [P, P])
        ones = small("ones", [P, P])
        cos = small("cos", [P, T, HALF])
        sin = small("sin", [P, T, HALF])
        rtmp = small("rtmp", [P, 5, P])
        pos_i = small("pos_i", [P, T], I32)
        posf = small("posf", [P, T])
        invf = small("invf", [P, HALF])
        gx = small("gx", [P, DC])
        gmem = small("gmem", [P, DC])
        gcq = small("gcq", [P, 5])
        gq96 = small("gq96", [P, QK])
        gk96 = small("gk96", [P, QK])
        gmh = small("gmh", [P, 4])
        gmix = small("gmix", [P, DC])
        ghq = small("ghq", [P, DC])
        kr = small("kr", [P, ROPE])
        ms = small("ms", [P, 16])
        rr = small("rr", [P, 16])
        mst = small("mst", [P, 32])
        rst = small("rst", [P, 32])
        nwt = small("nwt", [P, 32])
        mx = small("mx", [P, 4])
        nb = small("nb", [P, 4])
        rs = small("rs", [P, 4])
        ri = small("ri", [P, 4])
        st2 = small("st2", [P, 2])
        r2 = small("r2", [P, 2])
        r1 = small("r1", [P, 2])
        m1 = small("m1", [P, 1])
        m4 = small("m4", [P, MH])
        v4 = small("v4", [P, MH])
        sc = small("sc", [P, MH])
        mmx = small("mmx", [P, MH])
        mnb = small("mnb", [P, MH])
        mrs = small("mrs", [P, MH])
        mri = small("mri", [P, MH])
        m2 = small("m2", [P, 1])
        rt2 = small("rt2", [P, 1])
        wr = small("wr", [P, DC, NG + NE])
        br = small("br", [P, NG + NE])
        lg = small("lg", [P, T, NG + NE])
        rsm = cut(48640, 16, T)
        esm = cut(48768, 8, NE)
        s4 = cut(48896, 3, T, EG)
        io4 = small("io4", [P, EG])
        io16 = small("io16", [P, NE])
        slotf = small("slotf", [P, SLOTS])
        posk = small("posk", [P, 2, T], I32)
        adr = small("adr", [P, 3, 2 * T], I32)
        tok = small("tok", [P, T], I32)
        eidt = small("eidt", [P, SLOTS], I32)
        nitt = small("nitt", [P, 2], I32)
        idx_all = small("idx_all", [P, TAB], I32)
        idx = small("idx", [P, 2], I32)
        tiny = small("tiny", [P, 1])
        slot_cmp = junk[:, 0:SLOTS * NE].rearrange("p (s e) -> p s e", s=SLOTS)

        s_gain = sem("gains_loaded")
        s_pos = sem("positions_loaded")
        s_const = sem("constants_made")
        s_xin = [sem(f"input_tile_loaded{i}") for i in range(XIN)]
        s_wmk = [sem(f"w_mk_loaded{i}") for i in range(2)]
        s_wmv = sem("w_mv_loaded")
        s_wqkv = sem("w_qkv_loaded")
        s_sq = sem("mean_square_ready")
        s_rr = sem("rstd_ready")
        s_xn = sem("input_tile_normed")
        s_t = sem("transposition_bank_full")
        s_te = {"act": sem("transposition_bank_emptied_by_act"), "dve": sem("transposition_bank_emptied_by_dve")}
        s_mkv = sem("mem_kv_product")
        s_mkvo = sem("mem_kv_copied")
        s_mkn = sem("mem_k_normed")
        s_spill = sem("mem_kv_spilled")
        s_mk1 = sem("mem_kv_reloaded")
        s_qz = sem("query_zeros")
        s_pr = sem("sb_projection_product")
        s_proA = sem("sb_projection_copied_by_act")
        s_proD = sem("sb_projection_copied_by_dve")
        s_s = sem("sb_scores_full")
        s_f = sem("sb_fail_ready")
        s_g = sem("sb_take_ready")
        s_fm = sem("sb_fail_masked")
        s_gm = sem("sb_take_masked")
        s_w = sem("sb_weights_ready")
        s_pv = sem("sb_value_product")
        s_o = sem("sb_output_copied")
        s_wc = sem("w_c_loaded")
        s_wuq = sem("w_uq_loaded")
        s_p1 = sem("mla_down_product")
        s_csq = sem("mla_down_squares")
        s_cr = sem("mla_down_rstd")
        s_ce = sem("mla_down_normed")
        s_kre = sem("mla_rope_key_taken")
        s_p3 = sem("mla_up_product")
        s_q3 = sem("mla_up_copied")
        s_qkf = sem("mla_heads_ready")
        s_ms = sem("mla_scores_full")
        s_nb = sem("mla_maximum_ready")
        s_e = sem("mla_exp_ready")
        s_pn = sem("mla_probabilities_ready")
        s_mpv = sem("mla_value_product")
        s_mo = sem("mla_output_copied")
        s_wo = sem("w_o_loaded")
        s_wmq = sem("w_mq_loaded")
        s_wmo = sem("w_mo_loaded")
        s_wos = sem("w_o_scaled")
        s_wmqs = sem("w_mq_scaled")
        s_moeg = sem("moe_gain_loaded")
        s_x = sem("x_tile_loaded")
        s_msq = sem("mixed_squares")
        s_om = sem("mix_product")
        s_h1a = sem("sb_part_added")
        s_h1 = sem("h1_ready")
        s_h1q = sem("h1_mean_square")
        s_msc = sem("mem_scores_full")
        s_mnb = sem("mem_maximum_ready")
        s_me = sem("mem_exp_ready")
        s_mp = sem("mem_probabilities_ready")
        s_mq = sem("mem_query_product")
        s_mqo = sem("mem_query_copied")
        s_mqs = sem("mem_query_scale_ready")
        s_mot = sem("mem_output_product")
        s_moto = sem("mem_output_copied")
        s_mop = sem("mem_projection_product")
        s_h2 = sem("h2_ready")
        s_h2q = sem("h2_mean_square")
        s_tn = sem("moe_input_ready")
        s_tnd = sem("moe_input_stored")
        s_wr = sem("router_loaded")
        s_rm = sem("expert_choice_ready")
        s_tab0 = sem("token_table_cleared")
        s_ra = sem("token_addresses_ready")
        s_scat = sem("tokens_scattered")
        s_idx = sem("token_table_loaded")
        s_plan = sem("slot_plan_ready")
        s_wg = [sem(f"w_gate_loaded{b}") for b in range(2)]
        s_wu = [sem(f"w_up_loaded{b}") for b in range(2)]
        s_wd = [sem(f"w_down_loaded{b}") for b in range(2)]
        s_go = sem("gather_allowed")
        s_ic = sem("slot_indices_ready")
        s_xg = [sem(f"slot_rows_gathered{b}") for b in range(2)]
        s_xt = sem("slot_rows_transposed")
        s_xa = sem("slot_first_half_copied")
        s_xb = sem("slot_second_half_copied")
        s_gf = sem("gate_product")
        s_uf = sem("up_product")
        s_si = sem("silu_ready")
        s_h = sem("expert_hidden_ready")
        s_ht = sem("expert_hidden_transposed")
        s_hto = sem("expert_hidden_copied")
        s_y = sem("down_product")
        s_yo = sem("down_copied")
        s_ys = [sem(f"expert_rows_stored{b}") for b in range(2)]
        s_cg = [sem(f"chosen_rows_gathered{b}") for b in range(2)]
        s_co = sem("combined_ready")
        s_out = [sem(f"output_stored{b}") for b in range(2)]
        s_dve = sem("dve_own")
        s_act = sem("act_own")
        s_pool = sem("pool_own")
        s_dveL = sem("dve_own_in_slots")
        s_actL = sem("act_own_in_slots")

        block = ctx.enter_context(nc.Block())
        GAINS = 12

        def bank(i):
            return psum[:, i, :]

        def pair(i):
            return psum[:, 2 * i:2 * i + 2, :].rearrange("p a b -> p (a b)")

        def units():
            return [(h, g) for h in range(HEADS) for g in range(2)]

        @block.sync
        def _(sp):
            def rows(t):
                return slice(t * P, (t + 1) * P)

            def load_tile(n):
                src = mem2[rows(n), :] if n < MT else x2[rows(n - MT), :]
                if n >= XIN:
                    last = ROUND[("mem", n - XIN, 1)] if n - XIN < MT else ROUND[("x", n - XIN - MT, 1)]
                    sp.wait_ge(s_t, last + 1)
                sp.dma_start(xin[:, n % XIN, :], src).then_inc(s_xin[n % XIN], 16)

            def chunks(w, c0, c1):
                return w[:, c0:c1].rearrange("(k p) n -> p k n", p=P)

            def column(g, n):
                return g.rearrange("(c p) -> p c", p=n)

            load_tile(0)
            load_tile(1)
            for i in range(2):
                sp.dma_start(w_mk[:, 4 * i:4 * i + 4, :], chunks(w_mkv, 0, DM)[:, 4 * i:4 * i + 4, :]).then_inc(s_wmk[i], 16)
            load_tile(2)
            load_tile(3)
            sp.dma_start(w_mv, chunks(w_mkv, DM, 2 * DM)).then_inc(s_wmv, 16)
            sp.dma_start(w_qkv, chunks(w_in, 0, 3 * SBW)).then_inc(s_wqkv, 16)
            for n in range(4, MT + T):
                load_tile(n)
            for b in range(2):
                c = (2 + b) * SEQ
                sp.dma_start(y_dram[c:c + SEQ, :], x2).then_inc(s_ys[b], 16)
            sp.wait_ge(s_mkvo, 4)
            sp.dma_start(mv_dram, mv0.rearrange("p a b -> p (a b)")).then_inc(s_spill, 16)
            sp.wait_ge(s_te["dve"], EMPTIED[ROUND[("mk", 1, 1)]][1])
            sp.dma_start(mkT_dram, mkT0.rearrange("p a b -> p (a b)")).then_inc(s_spill, 16)
            sp.wait_ge(s_o, 2 * HEADS)
            sp.dma_start(w_c, chunks(w_in, MLA0, MLA0 + MLAW)).then_inc(s_wc, 16)
            sp.dma_start(w_q, chunks(w_uq, 0, HEADS * QK)).then_inc(s_wuq, 16)
            sp.dma_start(w_kv, chunks(w_ukv, 0, HEADS * P)).then_inc(s_wuq, 16)
            sp.wait_ge(s_p1, T)
            sp.dma_start(wo_sb, chunks(w_o, 0, DM)).then_inc(s_wo, 16)
            sp.wait_ge(s_t, ROUND[("kf", T - 1, 1)] + 1)
            sp.wait_ge(s_spill, 32)
            sp.dma_start(mkT1.rearrange("p a b -> p (a b)"), mkT_dram).then_inc(s_mk1, 16)
            sp.dma_start(mv1.rearrange("p a b -> p (a b)"), mv_dram).then_inc(s_mk1, 16)
            sp.wait_ge(s_mo, 2 * HEADS)
            sp.dma_start(x_in, x2[rows(0), :]).then_inc(s_x, 16)
            sp.dma_start(wmq_sb, chunks(w_mq, 0, DM)).then_inc(s_wmq, 16)
            sp.dma_start(moe_g, norm_moe_g.partition_broadcast(P)).then_inc(s_moeg, 16)
            sp.dma_start(wmo_sb, chunks(w_mo, 0, DM)).then_inc(s_wmo, 16)
            for i in range(T + 1):
                if i + 1 < T:
                    sp.wait_ge(s_h1a, i + 1)
                    sp.dma_start(x_in, x2[rows(i + 1), :]).then_inc(s_x, 16)
                if i >= 1:
                    sp.wait_ge(s_tn, i)
                    sp.dma_start(tn_dram[rows(i - 1), :], tn).then_inc(s_tnd, 16)

            sp.wait_ge(s_scat, 16 * 2 * T)
            sp.dma_start(idx_all[:, :], tok_dram.rearrange("(p s) o -> p (s o)", p=P)).then_inc(s_idx, 16)
            sp.wait_ge(s_plan, 1)
            n_it = sp.value_load(nitt[0:1, 0:1], min_val=1, max_val=SLOTS // 2)
            with sp.Fori(0, n_it) as k:
                for b in range(2):
                    e = sp.value_load(eidt[0:1, bass.ds(2 * k + b, 1)], min_val=0, max_val=NE - 1)
                    sp.wait_ge(s_gf, 2 * k + b + 1)
                    sp.dma_start(wexp[b][0], w_gate[bass.ds(e, 1), :, :].rearrange("e (k p) n -> p (e k) n", p=P)).then_inc(s_wg[b], 16)
                    sp.wait_ge(s_uf, 2 * k + b + 1)
                    sp.dma_start(wexp[b][1], w_up[bass.ds(e, 1), :, :].rearrange("e (k p) n -> p (e k) n", p=P)).then_inc(s_wu[b], 16)
                    sp.wait_ge(s_y, 2 * k + b + 1)
                    sp.dma_start(wexp[b][2], w_down[bass.ds(e, 1), :, :].rearrange("e (k p) n -> p (e k) n", p=P)).then_inc(s_wd[b], 16)
            for t in range(T):
                sp.wait_ge(s_co, t + 1)
                sp.dma_start(out2[rows(t), :], yo[:, t % 2, :]).then_inc(s_out[t % 2], 16)
            for b in range(2):
                sp.wait_ge(s_out[b], 16 * T // 2)

        @block.gpsimd
        def _(pool):
            do = Steps(pool, s_pool)
            INV = (np.float32(THETA) ** (-(np.arange(HALF, dtype=np.float32) * np.float32(2.0) / np.float32(ROPE)))).astype(np.float32)
            with nc.allow_non_contiguous_dma(reason="small gain vectors laid along the partitions"):
                for dst, src in ((gmem[:, :], mem_src_g.rearrange("(c p) -> p c", p=P)),
                                 (gx[:, :], norm_mix_g.rearrange("(c p) -> p c", p=P)),
                                 (gmh[:, 0:2], mem_qhead_g.rearrange("(c p) -> p c", p=P)),
                                 (gmh[:, 2:4], mem_khead_g.rearrange("(c p) -> p c", p=P)),
                                 (gcq[:, 0:3], mla_q_norm_g.rearrange("(c p) -> p c", p=P)),
                                 (gcq[:, 3:5], mla_kv_norm_g.rearrange("(c p) -> p c", p=P)),
                                 (gq96[:, 0:NOPE], mla_qn_g.partition_broadcast(P)),
                                 (gq96[:, NOPE:QK], mla_qr_g.partition_broadcast(P)),
                                 (gk96[:, 0:NOPE], mla_kn_g.partition_broadcast(P)),
                                 (gk96[:, NOPE:QK], mla_kr_g.partition_broadcast(P)),
                                 (gmix[:, 0:4], sb_out_g.rearrange("(c p) -> p c", p=P)),
                                 (gmix[:, 4:8], mla_out_g.rearrange("(c p) -> p c", p=P))):
                    pool.dma_start(dst, src).then_inc(s_gain, 16)
                pool.dma_start(ghq[:, :], norm_mem_g.rearrange("(c p) -> p c", p=P)).then_inc(s_pos, 16)
                pool.dma_start(pos_i[:, :], positions[0].rearrange("(t p) -> p t", p=P)).then_inc(s_pos, 16)
                pool.dma_start(wr[:, :, 0:NG], w_group.rearrange("(c p) e -> p c e", p=P)).then_inc(s_wr, 16)
                pool.dma_start(wr[:, :, NG:NG + NE], w_router.rearrange("(c p) e -> p c e", p=P)).then_inc(s_wr, 16)
                pool.dma_start(br[:, 0:NG], b_group.partition_broadcast(P)).then_inc(s_wr, 16)
                pool.dma_start(br[:, NG:NG + NE], b_router.partition_broadcast(P)).then_inc(s_wr, 16)
            do(pool.memset(ident[:, :], 0.0))
            do(pool.memset(ones[:, :], 1.0))
            do(pool.memset(idx_all[:, :], 0))
            for j in range(HALF):
                do(pool.memset(invf[:, j:j + 1], float(INV[j])))
            do.settle()
            do(pool.affine_select(out=ident[:, :], in_=ident[:, :], compare_op=ALU.not_equal, fill=1.0,
                                  base=0, pattern=[[-1, P]], channel_multiplier=1))
            do(pool.affine_select(out=before[:, :], in_=ones[:, :], compare_op=ALU.is_gt, fill=0.0,
                                  base=0, pattern=[[1, P]], channel_multiplier=-1))
            do(pool.iota(tok[:, :], pattern=[[P, T]], base=0, channel_multiplier=1))
            do(pool.iota(adr[:, 0, 0:NE], pattern=[[1, NE]], base=0, channel_multiplier=0))
            do(pool.iota(eidt[:, :], pattern=[[1, SLOTS]], base=0, channel_multiplier=0))
            do.settle()
            do(pool.tensor_copy(io16[:, :], adr[:, 0, 0:NE]))
            do(pool.tensor_copy(io4[:, :], adr[:, 0, 0:EG]))
            do(pool.tensor_copy(slotf[:, :], eidt[:, :]))
            do.settle()
            pool.dma_start(tok_dram.rearrange("(p s) o -> p (s o)", p=P), idx_all[:, :]).then_inc(s_tab0, 16)
            do(pool.memset(tiny[:, :], 0.0), s_const)

            pool.wait_ge(s_mkv, 4)
            pool.memset(qz[HD:P, 0:HEADS:2, :], 0.0).then_inc(s_qz, 1)
            pool.memset(qz[0:HD, 1:HEADS:2, :], 0.0).then_inc(s_qz, 1)
            pool.wait_ge(s_pr, 12)
            pool.wait_ge(s_spill, 32)
            for b in range(2):
                pool.memset(fall[:, b, SEQ:SEQ + 1], 1.0).then_inc(s_qz, 1)
            pool.memset(zeros, 0.0).then_inc(s_qz, 1)
            for u, (h, g) in enumerate(units()):
                for r in range(GRP):
                    n, t = GRP * u + r, GRP * g + r
                    for buf, full, masked, fill in ((f_sb, s_f, s_fm, 1.0), (g_sb, s_g, s_gm, 0.0)):
                        block_ = buf[:, n % 2, t * P:(t + 1) * P]
                        pool.wait_ge(full, n + 1)
                        pool.affine_select(out=block_, in_=block_, compare_op=ALU.is_gt, fill=fill, base=0,
                                           pattern=[[-1, P]], channel_multiplier=1).then_inc(masked, 1)

            pool.wait_ge(s_tab0, 16)
            pool.wait_ge(s_ra, 1)
            for j in range(2):
                for t in range(T):
                    c = j * T + t
                    pool.indirect_dma_start(out=tok_dram, out_offset=bass.IndirectOffsetOnAxis(ap=adr[:, 2, c:c + 1], axis=0),
                                            in_=tok[:, t:t + 1], in_offset=None,
                                            bounds_check=P * TAB - 1, oob_is_err=True).then_inc(s_scat, 16)
            pool.wait_ge(s_idx, 16)
            pool.wait_ge(s_tnd, 16 * T)
            pool.wait_ge(s_plan, 1)
            n_it = pool.value_load(nitt[0:1, 0:1], min_val=1, max_val=SLOTS // 2)

            def gather(b, column):
                pool.tensor_copy(idx[:, b:b + 1], idx_all[:, column]).then_inc(s_ic, 1)

            def fetch(b):
                pool.indirect_dma_start(out=xg[:, b, :], out_offset=None, in_=tn_dram,
                                        in_offset=bass.IndirectOffsetOnAxis(ap=idx[:, b:b + 1], axis=0)).then_inc(s_xg[b], 16)

            gather(0, slice(0, 1))
            pool.wait_ge(s_ic, 1)
            fetch(0)
            with pool.Fori(0, n_it) as k:
                for b in range(2):
                    nxt = 1 - b
                    column = pool.snap(2 * k + b + 1)
                    pool.wait_ge(s_xt, 2 * (2 * k + b) + 2)
                    gather(nxt, bass.ds(column, 1))
                    pool.wait_ge(s_ic, 2 * k + b + 2)
                    pool.sem_inc(s_go, 1)
                    fetch(nxt)
            all_slots = pool.snap(16 * n_it + 16)
            for b in range(2):
                pool.wait_ge(s_ys[b], all_slots)
            pool.wait_ge(s_xg[0], all_slots)
            pool.sem_inc(s_go, 1)
            for t in range(T):
                if t >= 2:
                    pool.wait_ge(s_co, t - 1)
                for j, buf in enumerate((y1, y2)):
                    pool.indirect_dma_start(out=buf[:, t % 2, :], out_offset=None, in_=y_dram,
                                            in_offset=bass.IndirectOffsetOnAxis(ap=posk[:, j, t:t + 1], axis=0)).then_inc(s_cg[t % 2], 16)

        @block.scalar
        def _(act):
            do = Steps(act, s_act)

            def empty(key, dst, src):
                i = ROUND[key]
                act.wait_ge(s_t, i + 1)
                do(act.activation(dst, src, ACT.Copy), s_te["act"])

            def squares(n):
                act.wait_ge(s_xin[n % XIN], 16 * (n // XIN + 1))
                do(act.activation(junk_b[:, 0:DM], xin[:, n % XIN, :], ACT.Square, scale=DM ** -0.5,
                                  accum_out=ms[:, n:n + 1]), s_sq)
                do.settle()

            act.wait_ge(s_rr, 1)
            for dst, src in ((sin, rtmp[:, 0, :]), (cos, rtmp[:, 1, :])):
                do(act.activation(dst[:, :, :].rearrange("p a b -> p (a b)"), src, ACT.Sin))
            for j in range(-1, 4):
                for n in (2 * j + 2, 2 * j + 3):
                    squares(n)
                for n in (2 * j + 2, 2 * j + 3):
                    act.wait_ge(s_rr, n // 2 + 2)
                    do(act.activation(xin[:, n % XIN, :], xin[:, n % XIN, :], ACT.Copy, scale=rr[:, n:n + 1]), s_xn)
                if j < 0:
                    continue
                act.wait_ge(s_mkv, j + 1)
                src = pair(1 + j % 3)
                if j < 2:
                    for h in range(MH):
                        do(act.activation(junk_b[:, 0:MHD], src[:, MHD * h:MHD * (h + 1)], ACT.Square,
                                          scale=MHD ** -0.5, accum_out=mst[:, MH * j + h:MH * j + h + 1]))
                        do.settle()
                    do(act.activation(k_raw[:, j, :], src, ACT.Copy), s_mkvo)
                else:
                    do(act.activation(mv0[:, j - 2, :], src, ACT.Copy), s_mkvo)
            for p in range(PAIRS):
                act.wait_ge(s_pr, 2 * p + 2)
                do(act.activation(kT[:, p, :], pair(1 + (4 + 2 * p + 1) % 3), ACT.Copy), s_proA)

            def take(u, r):
                g = u % 2
                n, L = GRP * u + r, P * (GRP * g + r + 1)
                src = pair(1 + n % 2)[:, 0:L]
                act.wait_ge(s_s, n + 1)
                if n >= 2:
                    act.wait_ge(s_w, n - 1)
                do(act.activation(f_sb[:, n % 2, 0:L], src, ACT.Sigmoid, scale=-(HD ** -0.5)), s_f)
                do(act.activation(g_sb[:, n % 2, 0:L], src, ACT.Sigmoid, scale=HD ** -0.5), s_g)

            def spread(kind, bufs, u, j, s_done):
                i = ROUND[(kind, u, j)]
                first = ROUND[(kind, 0, 0)]
                lo = P * max(0, j - GRP * (u % 2))
                if i - first >= 2:
                    act.wait_ge(s_done, i - first - 1)
                empty((kind, u, j), bufs[:, (i - first) % 2, lo:512], bank(i % 2)[:, lo:512])

            def attention(kind, bufs, s_done, one):
                act_units = 2 * HEADS
                for r in range(GRP):
                    one(0, r)
                for u in range(act_units):
                    nj = 4 * (u % 2) + 4
                    for j in range(nj):
                        if u + 1 < act_units and j % (nj // 4) == 0:
                            one(u + 1, j // (nj // 4))
                        spread(kind, bufs, u, j, s_done)

            act.wait_ge(s_proD, 8)
            attention("sb", wT_sb, s_pv, take)

            for i in range(T + 2):
                if i < T:
                    act.wait_ge(s_p1, i + 1)
                    for c, (a, b, src) in enumerate(((0, QR, bank(2)[:, 0:QR]), (QR, QR + KVR, bank(3)[:, 0:KVR]),
                                                     (0, ROPE, bank(3)[:, KVR:KVR + ROPE]))):
                        n = b - a
                        do(act.activation(junk_b[:, 0:n], src, ACT.Square, scale=n ** -0.5,
                                          accum_out=mst[:, c:c + 1]), s_csq if c == 2 else None)
                        do.settle()
                    act.wait_ge(s_cr, i + 1)
                    do(act.activation(cn[:, 0:QR], bank(2)[:, 0:QR], ACT.Copy, scale=rst[:, 0:1]))
                    act.wait_ge(s_kre, i + 1)
                    do(act.activation(cn[:, QR:QR + KVR], bank(3)[:, 0:KVR], ACT.Copy, scale=rst[:, 1:2]), s_ce)
                if i >= 2:
                    for kind, dst in (("qf", mqT_h), ("kf", mkT_h)):
                        for half in range(2):
                            key = (kind, i - 2, half)
                            empty(key, dst[0:QK, 4 * half:4 * half + 4, (i - 2) * P:(i - 1) * P],
                                  bank(ROUND[key] % 2)[0:QK, :].rearrange("p (a b) -> p a b", a=4))
                if 1 <= i <= T:
                    act.wait_ge(s_p3, i)
                    if i >= 2:
                        act.wait_ge(s_t, ROUND[("kf", i - 2, 1)] + 1)
                    for half in range(2):
                        hs = slice(4 * half, 4 * half + 4)
                        src = bank(4 + half)[:, 0:4 * QK].rearrange("p (a b) -> p a b", a=4)
                        kv = bank(6 + half).rearrange("p (a b) -> p a b", a=4)
                        do(act.activation(qf[:, hs, :], src, ACT.Copy))
                        do(act.activation(kf[:, hs, 0:NOPE], kv[:, :, 0:NOPE], ACT.Copy))
                        do(act.activation(v_mla[:, i - 1, 4 * half * HD:(4 * half + 4) * HD].rearrange("p (a b) -> p a b", a=4),
                                          kv[:, :, NOPE:NOPE + HD], ACT.Copy), s_q3)

            def exps(u, r):
                n, g = GRP * u + r, u % 2
                L = P * (GRP * g + r + 1)
                act.wait_ge(s_nb, n + 1)
                if u >= 2:
                    act.wait_ge(s_t, ROUND[("mla", u - 2, 4 * g + 3)] + 1)
                if n >= 4:
                    act.wait_ge(s_pn, n - 3)
                do(act.activation(p_rows[:, u % 2, r, 0:L], pair(1 + n % 2)[:, 0:L], ACT.Exp, scale=QK ** -0.5,
                                  bias=nb[:, n % 4:n % 4 + 1], accum_out=rs[:, n % 4:n % 4 + 1]), s_e)

            attention("mla", pT_sb, s_mpv, exps)

            def wide(key2, dst):
                for half in range(2):
                    key = (*key2, half)
                    empty(key, dst[:, 4 * half:4 * half + 4, :].rearrange("p a b -> p (a b)"), bank(ROUND[key] % 2))

            for i in range(T + 2):
                if 1 <= i <= T:
                    wide(("mqT", i - 1), mqT)
                if i < T:
                    act.wait_ge(s_h1, i + 1)
                    do(act.activation(junk_b[:, 0:DM], h1[:, i % 2, :], ACT.Square, scale=DM ** -0.5,
                                      accum_out=m1[:, 0:1]), s_h1q)
                    wide(("hT", i), h1T)
                if 1 <= i <= T:
                    act.wait_ge(s_mnb, i)
                    if i >= 2:
                        act.wait_ge(s_t, ROUND[("pT", i - 2, 1)] + 1)
                    for h in range(MH):
                        do(act.activation(mp[:, h, :], pair(3)[:, MEM * h:MEM * (h + 1)], ACT.Exp, scale=sc[:, h:h + 1],
                                          bias=mnb[:, h:h + 1], accum_out=mrs[:, h:h + 1]), s_me)
                if i < T:
                    act.wait_ge(s_mq, i + 1)
                    for h in range(MH):
                        do(act.activation(junk_b[:, 0:MHD], pair(1)[:, MHD * h:MHD * (h + 1)], ACT.Square,
                                          scale=MHD ** -0.5, accum_out=m4[:, h:h + 1]))
                        do.settle()
                    do(act.activation(mq_sb, pair(1), ACT.Copy), s_mqo)
                if 1 <= i <= T:
                    wide(("pT", i - 1), mpT)
                    act.wait_ge(s_mot, i)
                    do(act.activation(moT.rearrange("p a b -> p (a b)"), pair(2), ACT.Copy), s_moto)
                if i >= 2:
                    wide(("tT", i - 2), tT)
                if 1 <= i <= T:
                    act.wait_ge(s_h2, i)
                    do(act.activation(junk_b[:, 0:DM].rearrange("p (a b) -> p a b", a=DC), h2[:, :, (i - 1) * P:i * P],
                                      ACT.Square, scale=DM ** -0.5, accum_out=m2[:, 0:1]), s_h2q)

            act.wait_ge(s_rm, 1)
            do(act.activation(s4[:, 2, :, :], s4[:, 1, :, :], ACT.Exp), s_rm)
            do(act.activation(rsm[:, 8, :], rsm[:, 7, :], ACT.Exp), s_rm)

            act.wait_ge(s_plan, 1)
            n_it = act.value_load(nitt[0:1, 0:1], min_val=1, max_val=SLOTS // 2)

            def rows_out(b, count, copied):
                act.wait_ge(s_xt, count)
                act.activation(xT[:, b, 4:8, :].rearrange("p a b -> p (a b)"), bank(1), ACT.Copy).then_inc(s_xb, 1)

            for b in range(2):
                act.wait_ge(s_ys[b], 16)
            act.sem_inc(s_yo, 2)
            rows_out(0, 4, None)
            with act.Fori(0, n_it) as k:
                for b in range(2):
                    s = 2 * k + b
                    act.wait_ge(s_gf, s + 3)
                    act.wait_ge(s_h, s + 1)
                    act.activation(silu, bank(2), ACT.Silu).then_inc(s_si, 1)
                    rows_out(1 - b, 2 * s + 6, None)
                    act.wait_ge(s_y, s + 3)
                    act.wait_ge(s_ys[b], 16 * k + 16)
                    act.activation(ysb[:, b, :], pair(2 + b), ACT.Copy).then_inc(s_yo, 1)
                    act.wait_ge(s_yo, s + 3)
                    act.dma_start(y_dram[bass.ds(s * P, P), :], ysb[:, b, :]).then_inc(s_ys[b], 16)

        @block.vector
        def _(dve):
            do = Steps(dve, s_dve)

            def one(ins, sem_=None):
                do(ins, sem_)
                do.settle()

            def rsqrt(y, v, sem_=None):
                n = v.shape[-1]
                w = nwt[:, 0:n]
                one(dve.tensor_scalar(w.bitcast(I32), v.bitcast(I32), 1, None, ALU.logical_shift_right))
                one(dve.tensor_scalar(y.bitcast(I32), w.bitcast(I32), -1.0, float(0x5F3759DF), ALU.mult, ALU.add))
                for step in range(3):
                    one(dve.tensor_tensor(w, y, y, ALU.mult))
                    one(dve.tensor_tensor(w, w, v, ALU.mult))
                    one(dve.tensor_scalar(w, w, -0.5, 1.5, ALU.mult, ALU.add))
                    one(dve.tensor_tensor(y, y, w, ALU.mult), sem_ if step == 2 else None)

            def rotate(dst, src, t):
                n = src.shape[1]
                c = cos[:, t, :].unsqueeze(1).to_broadcast([P, n, HALF])
                s = sin[:, t, :].unsqueeze(1).to_broadcast([P, n, HALF])
                a, b = src[:, :, 0:HALF], src[:, :, HALF:ROPE]
                v = [rtmp[:, i, 0:n * HALF].rearrange("p (a b) -> p a b", a=n) for i in range(4)]
                do(dve.tensor_tensor(v[0], a, c, ALU.mult))
                do(dve.tensor_tensor(v[1], b, s, ALU.mult))
                do(dve.tensor_tensor(v[2], b, c, ALU.mult))
                one(dve.tensor_tensor(v[3], a, s, ALU.mult))
                do(dve.tensor_tensor(dst[:, :, 0:HALF], v[0], v[1], ALU.subtract))
                one(dve.tensor_tensor(dst[:, :, HALF:ROPE], v[2], v[3], ALU.add))

            dve.wait_ge(s_pos, 32)
            dve.wait_ge(s_const, 1)
            one(dve.tensor_copy(posf[:, :], pos_i[:, :]))
            ang, cyc, tmp = rtmp[:, 0, :], rtmp[:, 1, :], rtmp[:, 2, :]
            a3 = ang.rearrange("p (a b) -> p a b", a=T)
            one(dve.tensor_tensor(a3, posf[:, :].unsqueeze(2).to_broadcast([P, T, HALF]),
                                  invf[:, :].unsqueeze(1).to_broadcast([P, T, HALF]), ALU.mult))
            one(dve.tensor_scalar(tmp, ang, 1.0 / (2 * math.pi), None, ALU.mult))
            one(dve.tensor_copy(cyc.bitcast(I32), tmp))
            one(dve.tensor_copy(tmp, cyc.bitcast(I32)))
            TWO_PI = (6.28125, 0.0019350051879882812, 3.019916e-07)
            for part in TWO_PI:
                one(dve.scalar_tensor_tensor(out=ang, in0=tmp, scalar=-part, in1=ang, op0=ALU.mult, op1=ALU.add))
            PI = float(np.nextafter(np.float32(math.pi), np.float32(0)))

            def wrap(v, w):
                one(dve.tensor_scalar(w, v, PI, -2 * math.pi, ALU.is_gt, ALU.mult))
                one(dve.tensor_tensor(v, v, w, ALU.add))
                one(dve.tensor_scalar(w, v, -PI, 2 * math.pi, ALU.is_lt, ALU.mult))
                one(dve.tensor_tensor(v, v, w, ALU.add))
                one(dve.tensor_scalar(v, v, PI, -PI, ALU.min, ALU.max))

            wrap(ang, tmp)
            one(dve.tensor_scalar(cyc, ang, math.pi / 2, None, ALU.add))
            wrap(cyc, tmp)
            dve.wait_ge(s_gain, 16 * GAINS)
            one(dve.tensor_tensor(gmh[:, 0:2], gmh[:, 0:2], gmh[:, 2:4], ALU.mult), s_rr)

            def rstds(pair_):
                dve.wait_ge(s_sq, 2 * pair_ + 2)
                c = slice(2 * pair_, 2 * pair_ + 2)
                one(dve.tensor_scalar(ms[:, c], ms[:, c], EPS, None, ALU.add))
                rsqrt(rr[:, c], ms[:, c], s_rr)

            def turned(key, dst, gain):
                i = ROUND[key]
                n = dst.shape[1]
                dve.wait_ge(s_t, i + 1)
                do(dve.tensor_tensor(dst, bank(i % 2)[:, 0:n * P].rearrange("p (a b) -> p a b", a=n),
                                     gain.unsqueeze(2).to_broadcast([P, n, P]), ALU.mult), s_te["dve"])

            rstds(0)
            for m in range(MT):
                for half in range(2):
                    hs = slice(4 * half, 4 * half + 4)
                    turned(("mem", m, half), mnT[:, hs, m * P:(m + 1) * P], gmem[:, hs])

            for j in range(4):
                rstds(j + 1)
                for t in (2 * j, 2 * j + 1):
                    for half in range(2):
                        hs = slice(4 * half, 4 * half + 4)
                        turned(("x", t, half), hnT[:, hs, t * P:(t + 1) * P], gx[:, hs])
                if j in (0, 1):
                    dve.wait_ge(s_mkvo, j + 1)
                    c = slice(MH * j, MH * j + MH)
                    one(dve.tensor_scalar(mst[:, c], mst[:, c], EPS, None, ALU.add))
                    rsqrt(rst[:, c], mst[:, c])
                    kv = k_raw[:, j, :].rearrange("p (a b) -> p a b", a=MH)
                    do(dve.tensor_tensor(kv, kv, rst[:, c].unsqueeze(2).to_broadcast([P, MH, MHD]), ALU.mult), s_mkn)
                if j in (1, 2):
                    m = j - 1
                    for half in range(2):
                        key = ("mk", m, half)
                        dve.wait_ge(s_t, ROUND[key] + 1)
                        src = bank(ROUND[key] % 2).rearrange("p (h c m) -> p h c m", h=2, c=2)
                        for c in range(2):
                            dst = mkT0[:, 4 * half + c:4 * half + 4:2, m * P:(m + 1) * P]
                            do(dve.tensor_scalar(dst, src[:, :, c, :], gmh[:, c:c + 1], None, ALU.mult),
                               s_te["dve"] if c else None)

            dve.wait_ge(s_qz, 2)
            for p in range(PAIRS):
                dve.wait_ge(s_pr, 2 * p + 1)
                src = pair(1 + (4 + 2 * p) % 3)
                do(dve.tensor_copy(qz[0:HD, 2 * p, :], src[0:HD, :]))
                do(dve.tensor_copy(qz[HD:P, 2 * p + 1, :], src[HD:P, :]), s_proD)
            for c in range(4):
                dve.wait_ge(s_pr, 9 + c)
                do(dve.tensor_copy(v_sb[:, 2 * c:2 * c + 2, :].rearrange("p a b -> p (a b)"),
                                   pair(1 + (12 + c) % 3)), s_proD)

            def out_rows(u, s_prod, s_copied, chunk0):
                h, g = divmod(u, 2)
                rows = slice(HD * (h % 2), HD * (h % 2) + HD)
                dve.wait_ge(s_prod, prod_count(u))
                do(dve.tensor_copy(mixT[rows, chunk0 + h // 2, 512 * g:512 * (g + 1)], bank(6 + u % 2)[rows, :]), s_copied)

            dve.wait_ge(s_qz, 5)
            for u in range(2 * HEADS):
                g = u % 2
                for r in range(GRP):
                    n, L = GRP * u + r, P * (GRP * g + r + 1)
                    dve.wait_ge(s_fm, n + 1)
                    b = n % 2
                    one(dve.tensor_tensor_scan(fall[:, b, SEQ - L:SEQ][:, ::-1], f_sb[:, b, 0:L][:, ::-1],
                                               zeros.to_broadcast([P, L]), 1.0, ALU.mult, ALU.add))
                    dve.wait_ge(s_gm, n + 1)
                    if u >= 2 and r == 0:
                        dve.wait_ge(s_t, ROUND[("sb", u - 2, 4 * g + 3)] + 1)
                    do(dve.tensor_tensor(w_rows[:, u % 2, r, 0:L], g_sb[:, b, 0:L],
                                         fall[:, b, SEQ - L + 1:SEQ + 1], ALU.mult), s_w)
                if u >= 1:
                    out_rows(u - 1, s_pv, s_o, 0)
            out_rows(2 * HEADS - 1, s_pv, s_o, 0)

            def mla_down(i):
                dve.wait_ge(s_csq, i + 1)
                one(dve.tensor_scalar(mst[:, 0:3], mst[:, 0:3], EPS, None, ALU.add))
                rsqrt(rst[:, 0:3], mst[:, 0:3], s_cr)
                one(dve.scalar_tensor_tensor(out=kr[:, :], in0=bank(3)[:, KVR:KVR + ROPE], scalar=rst[:, 2:3],
                                             in1=gk96[:, NOPE:QK], op0=ALU.mult, op1=ALU.mult), s_kre)

            def mla_turn(i):
                turned(("c", i, 0), cT[:, 0:3, :], gcq[:, 0:3])
                turned(("c", i, 1), cT[:, 3:5, :], gcq[:, 3:5])

            def mla_heads(t, kr_t):
                dve.wait_ge(s_q3, 2 * t + 2)
                do(dve.tensor_tensor(sq, qf, qf, ALU.mult))
                do.settle()
                do(dve.tensor_reduce(mst[:, 8:16], sq[:, :, 0:NOPE], AX.X, ALU.add))
                one(dve.tensor_reduce(mst[:, 16:24], sq[:, :, NOPE:QK], AX.X, ALU.add))
                one(dve.tensor_tensor(sq[:, :, 0:NOPE], kf[:, :, 0:NOPE], kf[:, :, 0:NOPE], ALU.mult))
                one(dve.tensor_reduce(mst[:, 24:32], sq[:, :, 0:NOPE], AX.X, ALU.add))
                do(dve.tensor_scalar(mst[:, 8:16], mst[:, 8:16], 1.0 / NOPE, EPS, ALU.mult, ALU.add))
                do(dve.tensor_scalar(mst[:, 16:24], mst[:, 16:24], 1.0 / ROPE, EPS, ALU.mult, ALU.add))
                one(dve.tensor_scalar(mst[:, 24:32], mst[:, 24:32], 1.0 / NOPE, EPS, ALU.mult, ALU.add))
                rsqrt(rst[:, 8:32], mst[:, 8:32])

                def spread(c, n):
                    return rst[:, c:c + HEADS].unsqueeze(2).to_broadcast([P, HEADS, n])

                do(dve.tensor_tensor(qf[:, :, 0:NOPE], qf[:, :, 0:NOPE], spread(8, NOPE), ALU.mult))
                do(dve.tensor_tensor(qf[:, :, NOPE:QK], qf[:, :, NOPE:QK], spread(16, ROPE), ALU.mult))
                one(dve.tensor_tensor(kf[:, :, 0:NOPE], kf[:, :, 0:NOPE], spread(24, NOPE), ALU.mult))
                do(dve.tensor_tensor(qf, qf, gq96[:, :].unsqueeze(1).to_broadcast([P, HEADS, QK]), ALU.mult))
                one(dve.tensor_tensor(kf[:, :, 0:NOPE], kf[:, :, 0:NOPE],
                                      gk96[:, 0:NOPE].unsqueeze(1).to_broadcast([P, HEADS, NOPE]), ALU.mult))
                rotate(qf[:, :, NOPE:QK], qf[:, :, NOPE:QK], t)
                do(dve.tensor_copy(kf[:, :, NOPE:QK], krs[:, t % 2, :].unsqueeze(1).to_broadcast([P, HEADS, ROPE])), s_qkf)

            krs = rtmp[:, 4, 0:2 * ROPE].rearrange("p (a b) -> p a b", a=2)
            for i in range(T + 1):
                if i < T:
                    mla_down(i)
                    rotate(krs[:, i % 2, :].unsqueeze(1), kr[:, :].unsqueeze(1), i)
                    mla_turn(i)
                if i >= 1:
                    mla_heads(i - 1, None)

            def maximum(n):
                u, r = divmod(n, GRP)
                t = GRP * (u % 2) + r
                L = P * (t + 1)
                src = pair(1 + n % 2)
                dve.wait_ge(s_ms, n + 1)
                one(dve.memset(src[0:64, L - 64:L], -1e30))
                one(dve.tensor_reduce(mx[:, n % 4:n % 4 + 1], src[:, 0:L], AX.X, ALU.max))
                do(dve.tensor_scalar(nb[:, n % 4:n % 4 + 1], mx[:, n % 4:n % 4 + 1], -(QK ** -0.5), None, ALU.mult), s_nb)

            def scale_rows(n):
                u, r = divmod(n, GRP)
                L = P * (GRP * (u % 2) + r + 1)
                dve.wait_ge(s_e, n + 1)
                one(dve.reciprocal(ri[:, n % 4:n % 4 + 1], rs[:, n % 4:n % 4 + 1]))
                row = p_rows[:, u % 2, r, 0:L]
                do(dve.tensor_scalar(row, row, ri[:, n % 4:n % 4 + 1], None, ALU.mult), s_pn)

            for n in range(8 * HEADS + 1):
                if n < 8 * HEADS:
                    maximum(n)
                if n >= 1:
                    scale_rows(n - 1)
                if n >= 5 and n % 4 == 1:
                    out_rows(n // 4 - 1, s_mpv, s_mo, 4) if False else None
                if n >= 8 and n % 4 == 3:
                    out_rows(n // 4 - 2, s_mpv, s_mo, 4)
            for u in range(2 * HEADS - 2, 2 * HEADS):
                out_rows(u, s_mpv, s_mo, 4)

            dve.wait_ge(s_wo, 16)
            for c in range(DC):
                do(dve.tensor_scalar(wo_sb[:, c, :], wo_sb[:, c, :], gmix[:, c:c + 1], None, ALU.mult), s_wos)

            def mixed_squares(i):
                m = mixT[:, :, i * P:(i + 1) * P]
                do(dve.tensor_tensor(mix_sq, m, m, ALU.mult), s_msq)

            dve.wait_ge(s_mo, 2 * HEADS)
            mixed_squares(0)
            dve.wait_ge(s_moeg, 16)
            for i in range(T + 2):
                if i < T:
                    i_ = ROUND[("stats", i, 0)]
                    dve.wait_ge(s_t, i_ + 1)
                    one(dve.tensor_scalar(st2[:, :], bank(i_ % 2)[:, 0:2], 1.0 / SBW, EPS, ALU.mult, ALU.add), s_te["dve"])
                    rsqrt(r2[:, :], st2[:, :])
                    if i == 0:
                        dve.wait_ge(s_wmq, 16)
                        for c in range(DC):
                            do(dve.tensor_scalar(wmq_sb[:, c, :], wmq_sb[:, c, :], ghq[:, c:c + 1], None, ALU.mult), s_wmqs)
                    dve.wait_ge(s_x, 16 * (i + 1))
                    dve.wait_ge(s_om, 2 * i + 1)
                    one(dve.scalar_tensor_tensor(out=h1[:, i % 2, :], in0=pair(1), scalar=r2[:, 0:1], in1=x_in,
                                                 op0=ALU.mult, op1=ALU.add), s_h1a)
                    dve.wait_ge(s_om, 2 * i + 2)
                    one(dve.scalar_tensor_tensor(out=h1[:, i % 2, :], in0=pair(2), scalar=r2[:, 1:2], in1=h1[:, i % 2, :],
                                                 op0=ALU.mult, op1=ALU.add), s_h1)
                if 1 <= i <= T:
                    dve.wait_ge(s_msc, i)
                    one(dve.tensor_reduce(mmx[:, :], pair(3).rearrange("p (a b) -> p a b", a=MH), AX.X, ALU.max))
                    one(dve.tensor_tensor(mmx[:, :], mmx[:, :], sc[:, :], ALU.mult))
                    do(dve.tensor_scalar(mnb[:, :], mmx[:, :], -1.0, None, ALU.mult), s_mnb)
                if i < T:
                    dve.wait_ge(s_h1q, i + 1)
                    one(dve.tensor_scalar(r1[:, 1:2], m1[:, :], EPS, None, ALU.add))
                    rsqrt(r1[:, 0:1], r1[:, 1:2])
                    one(dve.tensor_tensor(r1[:, 1:2], r1[:, 0:1], r1[:, 0:1], ALU.mult))
                if 1 <= i <= T:
                    dve.wait_ge(s_me, MH * i)
                    one(dve.reciprocal(mri[:, :], mrs[:, :]))
                    do(dve.tensor_tensor(mp, mp, mri[:, :].unsqueeze(2).to_broadcast([P, MH, MEM]), ALU.mult), s_mp)
                if i < T:
                    dve.wait_ge(s_mqo, i + 1)
                    one(dve.tensor_scalar(v4[:, :], m4[:, :], r1[:, 1:2], EPS, ALU.mult, ALU.add))
                    rsqrt(sc[:, :], v4[:, :])
                    one(dve.tensor_scalar(sc[:, :], sc[:, :], r1[:, 0:1], MHD ** -0.5, ALU.mult, ALU.mult), s_mqs)
                if i >= 2:
                    j = ROUND[("router", i - 2, 0)]
                    dve.wait_ge(s_t, j + 1)
                    if i == 2:
                        dve.wait_ge(s_wr, 64)
                    do(dve.tensor_tensor(lg[:, i - 2, :], bank(j % 2)[:, 0:NG + NE], br[:, :], ALU.add), s_te["dve"])
                if 1 <= i <= T:
                    dve.wait_ge(s_mop, i)
                    h2v = h2[:, :, (i - 1) * P:i * P]
                    one(dve.tensor_tensor(h2v, pair(3).rearrange("p (a b) -> p a b", a=DC),
                                          h1[:, (i - 1) % 2, :].rearrange("p (a b) -> p a b", a=DC), ALU.add), s_h2)
                    dve.wait_ge(s_h2q, i)
                    one(dve.tensor_scalar(m2[:, :], m2[:, :], EPS, None, ALU.add))
                    rsqrt(rt2[:, :], m2[:, :])
                    if i >= 2:
                        dve.wait_ge(s_t, ROUND[("tT", i - 2, 1)] + 1)
                        dve.wait_ge(s_tnd, 16 * (i - 1))
                    do(dve.scalar_tensor_tensor(out=tn.rearrange("p (a b) -> p a b", a=DC), in0=h2v, scalar=rt2[:, 0:1],
                                                in1=moe_g.rearrange("p (a b) -> p a b", a=DC), op0=ALU.mult, op1=ALU.mult), s_tn)
                if i + 1 < T:
                    dve.wait_ge(s_t, ROUND[("stats", i, 0)] + 1)
                    mixed_squares(i + 1)

            do.settle()
            gl = lg[:, :, 0:NG]
            el = lg[:, :, NG:NG + NE].rearrange("p t (g e) -> p t g e", g=NG)

            def over(v, n):
                return v.unsqueeze(2).to_broadcast([P, T, n])

            def along(v, n=T):
                return v.unsqueeze(1).to_broadcast([P, n, v.shape[-1]])

            def first_of(best, values, index):
                eq = s4[:, 0, :, :]
                one(dve.tensor_tensor(eq, values, over(best, EG), ALU.is_equal))
                one(dve.tensor_scalar(eq, eq, -BIG, BIG, ALU.mult, ALU.add))
                one(dve.tensor_tensor(eq, eq, along(io4[:, :]), ALU.add))
                one(dve.tensor_reduce(index, eq, AX.X, ALU.min))

            gmax, gid, top1, i1, top2, i2 = (rsm[:, c, :] for c in range(6))
            one(dve.tensor_reduce(gmax, gl, AX.X, ALU.max))
            one(dve.tensor_tensor(s4[:, 1, :, :], gl, over(gmax, NG), ALU.subtract))
            first_of(gmax, gl, gid)
            oh, sel = s4[:, 0, :, :], rt[0][:, :, 0:EG]
            one(dve.tensor_tensor(oh, along(io4[:, :]), over(gid, NG), ALU.is_equal))
            for g in range(NG):
                dst = rt[1][:, :, 0:EG] if g else sel
                one(dve.tensor_tensor(dst, el[:, :, g, :], oh[:, :, g:g + 1].to_broadcast([P, T, EG]), ALU.mult))
                if g:
                    one(dve.tensor_tensor(sel, sel, rt[1][:, :, 0:EG], ALU.add))
            one(dve.tensor_reduce(top1, sel, AX.X, ALU.max))
            first_of(top1, sel, i1)
            one(dve.tensor_tensor(oh, along(io4[:, :]), over(i1, EG), ALU.is_equal))
            one(dve.tensor_scalar(oh, oh, -3e38, None, ALU.mult))
            one(dve.tensor_tensor(sel, sel, oh, ALU.add))
            one(dve.tensor_reduce(top2, sel, AX.X, ALU.max))
            first_of(top2, sel, i2)
            one(dve.tensor_tensor(rsm[:, 7, :], top2, top1, ALU.subtract), s_rm)
            for c in (3, 5):
                one(dve.scalar_tensor_tensor(out=rsm[:, c, :], in0=gid, scalar=float(EG), in1=rsm[:, c, :],
                                             op0=ALU.mult, op1=ALU.add))
            one(dve.tensor_tensor(rt[2], along(io16[:, :]), over(i1, NE), ALU.is_equal))
            one(dve.tensor_tensor(rt[3], along(io16[:, :]), over(i2, NE), ALU.is_equal))
            one(dve.tensor_tensor(rt[4], rt[2], rt[3], ALU.add), s_rm)
            dve.wait_ge(s_rm, 4)
            one(dve.tensor_reduce(rsm[:, 9, :], s4[:, 2, :, :], AX.X, ALU.add))
            one(dve.tensor_scalar(rsm[:, 10, :], rsm[:, 8, :], 1.0, None, ALU.add))
            one(dve.tensor_tensor(rsm[:, 9, :], rsm[:, 9, :], rsm[:, 10, :], ALU.mult))
            one(dve.reciprocal(rsm[:, 11, :], rsm[:, 9, :]))
            one(dve.tensor_tensor(rsm[:, 12, :], rsm[:, 11, :], rsm[:, 8, :], ALU.mult))
            j = ROUND[("rank", 0, 0)]
            dve.wait_ge(s_t, j + 1)
            one(dve.tensor_copy(rt[5].rearrange("p t e -> p (t e)"), bank(j % 2)[:, 0:T * NE]))
            one(dve.tensor_copy(rt[6].rearrange("p t e -> p (t e)"), bank(j % 2)[:, T * NE:2 * T * NE]), s_te["dve"])
            base, tiles, ends = esm[:, 0, :], esm[:, 1, :], esm[:, 2, :]
            one(dve.tensor_scalar(base, rt[6][:, 0, :], 0.0, None, ALU.mult))
            for t in range(T):
                one(dve.tensor_tensor(rt[5][:, t, :], rt[5][:, t, :], base, ALU.add))
                one(dve.tensor_tensor(base, base, rt[6][:, t, :], ALU.add))
            one(dve.tensor_scalar(tiles, base, 0.0, None, ALU.is_gt))
            for c in range(1, T):
                one(dve.scalar_tensor_tensor(out=tiles, in0=base, scalar=float(P * c), in1=tiles, op0=ALU.is_gt, op1=ALU.add))
            one(dve.tensor_tensor_scan(ends, ones[:, 0:NE], tiles, 0.0, ALU.mult, ALU.add))
            one(dve.tensor_tensor(esm[:, 3, :], ends, tiles, ALU.subtract))
            one(dve.tensor_scalar(esm[:, 3, :], esm[:, 3, :], float(P), None, ALU.mult))
            one(dve.tensor_tensor(rt[5], rt[5], along(esm[:, 3, :]), ALU.add))
            for c in range(2):
                one(dve.tensor_tensor(rt[7], rt[5], rt[2 + c], ALU.mult))
                one(dve.tensor_reduce(rsm[:, 13 + c, :], rt[7], AX.X, ALU.add))
                one(dve.tensor_copy(posk[:, c, :], rsm[:, 13 + c, :]))
            flat = posk[:, :, :].rearrange("p c t -> p (c t)")
            one(dve.tensor_scalar(adr[:, 0, :], flat, P - 1, None, ALU.bitwise_and))
            one(dve.tensor_scalar(adr[:, 1, :], flat, 7, None, ALU.logical_shift_right))
            one(dve.tensor_scalar(adr[:, 0, :], adr[:, 0, :], float(TAB), None, ALU.mult))
            one(dve.tensor_tensor(adr[:, 2, :], adr[:, 0, :], adr[:, 1, :], ALU.add), s_ra)
            one(dve.tensor_tensor(slot_cmp, slotf[:, :].unsqueeze(2).to_broadcast([P, SLOTS, NE]), along(ends, SLOTS), ALU.is_ge))
            one(dve.tensor_reduce(junk[:, 512:512 + SLOTS], slot_cmp, AX.X, ALU.add))
            one(dve.tensor_scalar(junk[:, 512:512 + SLOTS], junk[:, 512:512 + SLOTS], float(NE - 1), None, ALU.min))
            one(dve.tensor_copy(eidt[:, :], junk[:, 512:512 + SLOTS]))
            one(dve.tensor_scalar(esm[:, 4, 0:1], ends[:, NE - 1:NE], 1.0, None, ALU.add))
            one(dve.tensor_copy(nitt[:, 1:2], esm[:, 4, 0:1]))
            one(dve.tensor_scalar(nitt[:, 0:1], nitt[:, 1:2], 1, None, ALU.logical_shift_right), s_plan)

            n_it = dve.value_load(nitt[0:1, 0:1], min_val=1, max_val=SLOTS // 2)

            def rows_out(b, count):
                dve.wait_ge(s_xt, count)
                dve.tensor_copy(xT[:, b, 0:4, :].rearrange("p a b -> p (a b)"), bank(0)).then_inc(s_xa, 1)

            dve.sem_inc(s_h, 1)
            dve.sem_inc(s_hto, 1)
            rows_out(0, 3)
            with dve.Fori(0, n_it) as k:
                for b in range(2):
                    s = 2 * k + b
                    dve.wait_ge(s_si, s + 1)
                    dve.wait_ge(s_uf, s + 3)
                    dve.wait_ge(s_ht, s + 1)
                    dve.tensor_tensor(hrow, silu, bank(3), ALU.mult).then_inc(s_h, 1)
                    rows_out(1 - b, 2 * s + 5)
                    dve.wait_ge(s_ht, s + 2)
                    dve.tensor_copy(hTe.rearrange("p a b -> p (a b)"), bank(0)).then_inc(s_hto, 1)

            for t in range(T):
                dve.wait_ge(s_cg[t % 2], 32 * (t // 2 + 1))
                if t >= 2:
                    dve.wait_ge(s_out[t % 2], 16 * (t // 2))
                o3 = yo[:, t % 2, :].rearrange("p (a b) -> p a b", a=DC)
                one(dve.scalar_tensor_tensor(out=o3, in0=y1[:, t % 2, :].rearrange("p (a b) -> p a b", a=DC),
                                             scalar=rsm[:, 11, t:t + 1], in1=h2[:, :, t * P:(t + 1) * P], op0=ALU.mult, op1=ALU.add))
                one(dve.scalar_tensor_tensor(out=yo[:, t % 2, :], in0=y2[:, t % 2, :], scalar=rsm[:, 12, t:t + 1],
                                             in1=yo[:, t % 2, :], op0=ALU.mult, op1=ALU.add), s_co)

        @block.tensor
        def _(pe):
            def begin(key):
                i = ROUND[key]
                if i >= 2:
                    engine, count = EMPTIED[i - 2]
                    pe.wait_ge(s_te[engine], count)
                return bank(i % 2)

            def turn(key, blocks):
                dst = begin(key)
                at = 0
                for src in blocks:
                    rows = src.shape[-1]
                    mm = pe.transpose(dst[0:rows, at:at + P], src, ident[:, :])
                    at += P
                mm.then_inc(s_t, 1)

            def product(dst, pairs_, sem_=None):
                n = len(pairs_)
                for i, (a, b) in enumerate(pairs_):
                    mm = pe.matmul(dst, a, b, start=(i == 0), stop=(i == n - 1))
                if sem_ is not None:
                    mm.then_inc(sem_, 1)

            def halves(pair_, lhs, rhs, sem_, n=DC):
                for half in range(2):
                    product(bank(2 * pair_ + half), [(lhs(k), rhs(k, half)) for k in range(n)],
                            sem_ if half else None)

            pe.wait_ge(s_const, 1)
            for m in range(MT):
                pe.wait_ge(s_xn, m + 1)
                for half in range(2):
                    turn(("mem", m, half), [xin[:, m, (4 * half + c) * P:(4 * half + c + 1) * P] for c in range(4)])
            pe.wait_ge(s_te["dve"], EMPTIED[ROUND[("mem", 1, 1)]][1])
            for j in range(4):
                m = j % 2
                w = w_mk if j < 2 else w_mv
                if j == 3:
                    pe.wait_ge(s_mkvo, 1)
                for half in range(2):
                    if j == 0:
                        pass
                    if j == 2 and half == 0:
                        pe.wait_ge(s_wmv, 16)
                    for k in range(DC):
                        if j == 0 and half == 0 and k % 4 == 0:
                            pe.wait_ge(s_wmk[k // 4], 16)
                        mm = pe.matmul(bank(2 * (1 + j % 3) + half), mnT[:, k, m * P:(m + 1) * P],
                                       w[:, k, 512 * half:512 * half + 512], start=(k == 0), stop=(k == DC - 1))
                mm.then_inc(s_mkv, 1)
                for t in (2 * j, 2 * j + 1):
                    pe.wait_ge(s_xn, MT + t + 1)
                    for half in range(2):
                        turn(("x", t, half), [xin[:, (MT + t) % XIN, (4 * half + c) * P:(4 * half + c + 1) * P] for c in range(4)])
                if j in (1, 2):
                    pe.wait_ge(s_mkn, j)
                    for half in range(2):
                        turn(("mk", j - 1, half), [k_raw[:, j - 1, (4 * half + c) * P:(4 * half + c + 1) * P] for c in range(4)])

            pe.wait_ge(s_te["dve"], EMPTIED[ROUND[("x", T - 1, 1)]][1])
            pe.wait_ge(s_wqkv, 16)

            def projection_free(use):
                if use < 3 + 4 and use - 3 < 4:
                    pe.wait_ge(s_mkvo, use - 3 + 1)
                else:
                    o = use - 3 - 4
                    if o < 8:
                        pe.wait_ge(s_proA if o % 2 else s_proD, o // 2 + 1)
                    else:
                        pe.wait_ge(s_proD, 4 + o - 8 + 1)

            for p in range(PAIRS):
                for c in range(2):
                    use = 4 + 2 * p + c
                    projection_free(use)
                    col = c * SBW + p * P
                    halves(1 + use % 3, lambda k: w_qkv[:, k, col:col + P],
                           lambda k, half: hnT[:, k, 512 * half:512 * half + 512], s_pr)
            for c in range(4):
                use = 12 + c
                projection_free(use)
                for half in range(2):
                    t = 2 * c + half
                    product(bank(2 * (1 + use % 3) + half),
                            [(hnT[:, k, t * P:(t + 1) * P], w_qkv[:, k, 2 * SBW:3 * SBW]) for k in range(DC)],
                            s_pr if half else None)

            def attention(kind, rows, bufs, s_full, s_free, s_ready, s_prod, s_copied, scores, value):
                first = ROUND[(kind, 0, 0)]

                def weigh(u, j):
                    i = ROUND[(kind, u, j)]
                    g = u % 2
                    lo = P * max(0, j - GRP * g)
                    pe.wait_ge(s_te["act"], EMPTIED[i][1])
                    if j == 0 and u >= 2:
                        pe.wait_ge(s_copied, u - 1)
                    pe.matmul(bank(6 + u % 2)[:, lo:512], value(u // 2, j), bufs[:, (i - first) % 2, lo:512],
                              start=(j == 0), stop=(j == GRP * g + 3)).then_inc(s_prod, 1)

                def score(n):
                    u, r = divmod(n, GRP)
                    h, g = divmod(u, 2)
                    t = GRP * g + r
                    L = P * (t + 1)
                    if n >= 2:
                        pe.wait_ge(s_free, n - 1)
                    lhs, rhs = scores(h, t)
                    for at in range(0, L, 512):
                        end = min(L, at + 512)
                        mm = pe.matmul(pair(1 + n % 2)[:, at:end], lhs, rhs(at, end), start=True, stop=True)
                    mm.then_inc(s_full, 1)

                for n in range(GRP):
                    score(n)
                for u in range(2 * HEADS):
                    g = u % 2
                    nj = 4 * g + 4
                    for j in range(nj):
                        if u + 1 < 2 * HEADS and j % (nj // 4) == 0:
                            score(GRP * (u + 1) + j // (nj // 4))
                        pe.wait_ge(s_ready, GRP * (u + 1))
                        r0 = max(0, j - GRP * g)
                        dst = begin((kind, u, j))
                        for r in range(r0, GRP):
                            mm = pe.transpose(dst[:, r * P:(r + 1) * P], rows[:, u % 2, r, j * P:(j + 1) * P], ident[:, :])
                        mm.then_inc(s_t, 1)
                        if j >= 1:
                            weigh(u, j - 1)
                    weigh(u, nj - 1)

            pe.wait_ge(s_proA, 4)
            pe.wait_ge(s_proD, 8)
            attention("sb", w_rows, wT_sb, s_s, s_g, s_w, s_pv, s_o,
                      lambda h, t: (qz[:, h, t * P:(t + 1) * P], lambda a, b: kT[:, h // 2, a:b]),
                      lambda h, j: v_sb[:, j, P * (h // 2):P * (h // 2 + 1)])

            pe.wait_ge(s_o, 2 * HEADS)
            pe.wait_ge(s_g, 8 * HEADS)
            for i in range(T + 2):
                if i < T:
                    if i == 0:
                        pe.wait_ge(s_wc, 16)
                    else:
                        pe.wait_ge(s_ce, i)
                        pe.wait_ge(s_kre, i)
                    lhs = [hnT[:, k, i * P:(i + 1) * P] for k in range(DC)]
                    product(bank(2)[:, 0:QR], [(lhs[k], w_c[:, k, 0:QR]) for k in range(DC)])
                    product(bank(3)[:, 0:KVR + ROPE], [(lhs[k], w_c[:, k, QR:MLAW]) for k in range(DC)], s_p1)
                if 1 <= i <= T:
                    if i == 1:
                        pe.wait_ge(s_wuq, 32)
                    else:
                        pe.wait_ge(s_q3, 2 * (i - 1))
                    pe.wait_ge(s_te["dve"], EMPTIED[ROUND[("c", i - 1, 1)]][1])
                    for half in range(2):
                        product(bank(4 + half)[:, 0:4 * QK],
                                [(cT[:, k, :], w_q[:, k, 4 * QK * half:4 * QK * (half + 1)]) for k in range(3)])
                    for half in range(2):
                        product(bank(6 + half), [(cT[:, 3 + k, :], w_kv[:, k, 512 * half:512 * half + 512]) for k in range(2)],
                                s_p3 if half else None)
                if i >= 2:
                    pe.wait_ge(s_qkf, i - 1)
                    for kind, src in (("qf", qf), ("kf", kf)):
                        for half in range(2):
                            turn((kind, i - 2, half), [src[:, 4 * half + c, :] for c in range(4)])
                if i < T:
                    pe.wait_ge(s_ce, i + 1)
                    turn(("c", i, 0), [cn[:, c * P:(c + 1) * P] for c in range(3)])
                    turn(("c", i, 1), [cn[:, c * P:(c + 1) * P] for c in range(3, 5)])

            pe.wait_ge(s_te["act"], EMPTIED[ROUND[("kf", T - 1, 1)]][1])
            attention("mla", p_rows, pT_sb, s_ms, s_e, s_pn, s_mpv, s_mo,
                      lambda h, t: (mqT_h[0:QK, h, t * P:(t + 1) * P], lambda a, b: mkT_h[0:QK, h, a:b]),
                      lambda h, j: v_mla[:, j, P * (h // 2):P * (h // 2 + 1)])

            pe.wait_ge(s_mo, 2 * HEADS)
            for i in range(T + 2):
                if i < T:
                    pe.wait_ge(s_msq, i + 1)
                    dst = begin(("stats", i, 0))
                    for c in range(2):
                        product(dst[:, c:c + 1], [(mix_sq[:, 4 * c + k, :], ones[:, 0:1]) for k in range(4)],
                                s_t if c else None)
                    if i == 0:
                        pe.wait_ge(s_wos, DC)
                    else:
                        pe.wait_ge(s_mqo, i)
                    lhs = lambda c: mixT[:, c, i * P:(i + 1) * P]
                    halves(1, lambda k: lhs(k), lambda k, half: wo_sb[:, k, 512 * half:512 * half + 512], s_om, 4)
                    if i >= 2:
                        pe.wait_ge(s_moto, i - 1)
                    halves(2, lambda k: lhs(4 + k), lambda k, half: wo_sb[:, 4 + k, 512 * half:512 * half + 512], s_om, 4)
                if 1 <= i <= T:
                    pe.wait_ge(s_mqo, i)
                    for half in range(2):
                        turn(("mqT", i - 1, half), [mq_sb[:, (4 * half + c) * P:(4 * half + c + 1) * P] for c in range(4)])
                    if i == 1:
                        pe.wait_ge(s_mk1, 32)
                    else:
                        pe.wait_ge(s_h2, i - 1)
                    pe.wait_ge(s_te["act"], EMPTIED[ROUND[("mqT", i - 1, 1)]][1])
                    for h in range(MH):
                        product(pair(3)[:, MEM * h:MEM * (h + 1)],
                                [(mqT[:, 2 * h + c, :], mkT1[:, 2 * h + c, :]) for c in range(2)],
                                s_msc if h == MH - 1 else None)
                if i < T:
                    pe.wait_ge(s_h1, i + 1)
                    for half in range(2):
                        turn(("hT", i, half), [h1[:, i % 2, (4 * half + c) * P:(4 * half + c + 1) * P] for c in range(4)])
                    if i == 0:
                        pe.wait_ge(s_wmqs, DC)
                    pe.wait_ge(s_te["act"], EMPTIED[ROUND[("hT", i, 1)]][1])
                    halves(1, lambda k: h1T[:, k, :], lambda k, half: wmq_sb[:, k, 512 * half:512 * half + 512], s_mq)
                if 1 <= i <= T:
                    pe.wait_ge(s_mp, i)
                    for half in range(2):
                        turn(("pT", i - 1, half), [mp[:, 2 * half + c // 2, (c % 2) * P:(c % 2 + 1) * P] for c in range(4)])
                    pe.wait_ge(s_te["act"], EMPTIED[ROUND[("pT", i - 1, 1)]][1])
                    for c in range(DC):
                        h = c // 2
                        product(pair(2)[:, c * P:(c + 1) * P],
                                [(mv1[:, m, c * P:(c + 1) * P], mpT[:, 2 * h + m, :]) for m in range(MT)],
                                s_mot if c == DC - 1 else None)
                if i >= 2:
                    for half in range(2):
                        pe.wait_ge(s_tn, i - 1)
                        turn(("tT", i - 2, half), [tn[:, (4 * half + c) * P:(4 * half + c + 1) * P] for c in range(4)])
                    if i == 2:
                        pe.wait_ge(s_wr, 64)
                    pe.wait_ge(s_te["act"], EMPTIED[ROUND[("tT", i - 2, 1)]][1])
                    dst = begin(("router", i - 2, 0))
                    product(dst[:, 0:NG + NE], [(tT[:, k, :], wr[:, k, :]) for k in range(DC)], s_t)
                if 1 <= i <= T:
                    if i == 1:
                        pe.wait_ge(s_wmo, 16)
                    pe.wait_ge(s_moto, i)
                    pe.wait_ge(s_me, MH * i)
                    halves(3, lambda k: moT[:, k, :], lambda k, half: wmo_sb[:, k, 512 * half:512 * half + 512], s_mop)

            pe.wait_ge(s_rm, 4)
            dst = begin(("rank", 0, 0))
            marks = rt[4].rearrange("p t e -> p (t e)")
            pe.matmul(dst[:, 0:T * NE], before[:, :], marks, start=True, stop=True)
            pe.matmul(dst[:, T * NE:2 * T * NE], ones[:, :], marks, start=True, stop=True).then_inc(s_t, 1)

            pe.wait_ge(s_plan, 1)
            n_it = pe.value_load(nitt[0:1, 0:1], min_val=1, max_val=SLOTS // 2)
            for s_ in (s_gf, s_uf, s_y, s_xt):
                pe.sem_inc(s_, 2)
            pe.sem_inc(s_ht, 1)

            def rows_in(b, loads, copied_a, copied_b):
                pe.wait_ge(s_xg[b], loads)
                for half, (copied, count) in enumerate(((s_hto, copied_a), (s_xb, copied_b))):
                    if count is not None:
                        pe.wait_ge(copied, count)
                    for c in range(4):
                        at = (4 * half + c) * P
                        mm = pe.transpose(bank(half)[:, c * P:(c + 1) * P], xg[:, b, at:at + P], ident[:, :])
                    mm.then_inc(s_xt, 1)

            rows_in(0, 16, None, None)
            with pe.Fori(0, n_it) as k:
                for b in range(2):
                    s = 2 * k + b
                    pe.wait_ge(s_xa, s + 1)
                    pe.wait_ge(s_xb, s + 1)
                    pe.wait_ge(s_h, s + 1)
                    pe.wait_ge(s_wg[b], 16 * k + 16)
                    product(bank(2), [(xT[:, b, c, :], wexp[b][0][:, c, :]) for c in range(DC)], s_gf)
                    pe.wait_ge(s_wu[b], 16 * k + 16)
                    product(bank(3), [(xT[:, b, c, :], wexp[b][1][:, c, :]) for c in range(DC)], s_uf)
                    rows_in(1 - b, 16 * k + 16 * (1 + b), s + 1, s + 1)
                    pe.wait_ge(s_h, s + 2)
                    pe.wait_ge(s_xa, s + 2)
                    for c in range(FC):
                        mm = pe.transpose(bank(0)[:, c * P:(c + 1) * P], hrow[:, c * P:(c + 1) * P], ident[:, :])
                    mm.then_inc(s_ht, 1)
                    pe.wait_ge(s_hto, s + 2)
                    pe.wait_ge(s_wd[b], 16 * k + 16)
                    pe.wait_ge(s_yo, s + 1)
                    halves(2 + b, lambda c: hTe[:, c, :],
                           lambda c, half: wexp[b][2][:, c, 512 * half:512 * half + 512], s_y, FC)


def prod_count(u):
    return 12 * (u // 2) + (4 if u % 2 == 0 else 12)


_INS = ["x", "mem", "positions", "norm_mix_g", "w_in", "mla_q_norm_g", "w_uq", "mla_kv_norm_g", "w_ukv",
        "mla_qn_g", "mla_qr_g", "mla_kn_g", "mla_kr_g", "sb_out_g", "mla_out_g", "w_o", "norm_mem_g",
        "mem_src_g", "w_mq", "w_mkv", "mem_qhead_g", "mem_khead_g", "w_mo", "norm_moe_g", "w_group",
        "b_group", "w_router", "b_router", "w_gate", "w_up", "w_down"]


def kernel(**inputs):
    import numpy as _np
    import concourse.bacc as _bacc
    from concourse import mybir as _mybir
    from concourse.bass_utils import run_bass_kernel_spmd as _run

    nc = _bacc.Bacc("TRN2", target_bir_lowering=False, num_devices=1)
    arrays, args = {}, []
    for name in _INS:
        a = _np.ascontiguousarray(inputs[name])
        arrays[f"in_{name}"] = a
        args.append(nc.dram_tensor(f"in_{name}", a.shape, _mybir.dt.from_np(a.dtype), kind="ExternalInput").ap())
    out = nc.dram_tensor("layer_out", (1, SEQ, DM), F32, kind="ExternalOutput").ap()
    moe_layer(nc, *args, out)
    r = _run(nc, [arrays], core_ids=[0])
    return r.results[0]["layer_out"]
```

```python
import math

import numpy as np
import concourse.bass as bass
from concourse import mybir
from contextlib import ExitStack

F32 = mybir.dt.float32
BF16 = mybir.dt.bfloat16
I32 = mybir.dt.int32
ACT = mybir.ActivationFunctionType
ALU = mybir.AluOpType
AX = mybir.AxisListType

P = 128
SEQ, DM, MEM = 1024, 1024, 256
T, DC, MT = SEQ // P, DM // P, MEM // P
EPS = 1e-6
HEADS, HD = 8, 64
PAIRS = HEADS // 2
NOPE, ROPE = 64, 32
QK = NOPE + ROPE
HALF = ROPE // 2
QR, KVR = 384, 256
SBW = HEADS * HD
MLA0 = 3 * SBW
MLAW = QR + KVR + ROPE
THETA = 10000.0
MH, MHD = 4, 256
NG, EG = 4, 4
NE, FF = NG * EG, 512
FC = FF // P
GRP = 4
UNITS = [(h, g) for g in (1, 0) for h in range(HEADS)]
SLOTS = (2 * SEQ) // P + NE
TAB = SLOTS + 2
BIG = 64.0


class Steps:

    def __init__(self, eng, own):
        self.eng, self.own, self.counts, self.last = eng, own, {}, None

    def __call__(self, ins, sem=None):
        sem = self.own if sem is None else sem
        self.counts[sem.name] = self.counts.get(sem.name, 0) + 1
        ins.then_inc(sem, 1)
        self.last = (sem, self.counts[sem.name])

    def settle(self):
        self.eng.wait_ge(*self.last)


def blocks(u):
    return GRP * (UNITS[u][1] + 1)


def transposition_rounds():
    rounds = []

    def add(kind, key, engine, n=2):
        for half in range(n):
            rounds.append(((kind, key, half), engine))

    for m in range(MT):
        add("mem", m, "dve")
    for j in range(4):
        for t in (2 * j, 2 * j + 1):
            add("x", t, "dve")
        if j in (1, 2):
            add("mk", j - 1, "dve")
    for u in range(2 * HEADS):
        add("sb", u, "act", blocks(u))
    for i in range(T + 2):
        if i >= 2:
            add("qf", i - 2, "act")
            add("kf", i - 2, "act")
        if i < T:
            add("c", i, "dve")
    for u in range(2 * HEADS):
        add("mla", u, "act", blocks(u))
    for i in range(T + 2):
        if i < T:
            add("stats", i, "dve", 1)
        if 1 <= i <= T:
            add("mqT", i - 1, "act")
        if i < T:
            add("hT", i, "act")
        if 1 <= i <= T:
            add("pT", i - 1, "act")
        if i >= 2:
            add("tT", i - 2, "act")
            add("router", i - 2, "dve", 1)
    add("rank", 0, "dve", 1)
    add("table", 0, "dve", 1)
    return rounds


def moe_layer(nc, x, mem, positions, norm_mix_g, w_in, mla_q_norm_g, w_uq, mla_kv_norm_g, w_ukv,
              mla_qn_g, mla_qr_g, mla_kn_g, mla_kr_g, sb_out_g, mla_out_g, w_o, norm_mem_g,
              mem_src_g, w_mq, w_mkv, mem_qhead_g, mem_khead_g, w_mo, norm_moe_g, w_group, b_group,
              w_router, b_router, w_gate, w_up, w_down, out, debug=None):
    ROUNDS = transposition_rounds()
    ROUND = {key: i for i, (key, _) in enumerate(ROUNDS)}
    EMPTIED = []
    seen = {"act": 0, "dve": 0}
    for _, engine in ROUNDS:
        seen[engine] += 1
        EMPTIED.append((engine, seen[engine]))

    x2, mem2, out2 = x[0], mem[0], out[0]
    mkT_dram = nc.dram_tensor("mkT_spill", [P, DC * MEM], F32).ap()
    mv_dram = nc.dram_tensor("mv_spill", [P, MT * DM], F32).ap()
    tn_dram = nc.dram_tensor("tn_rows", [SEQ, DM], F32).ap()
    y_dram = nc.dram_tensor("expert_rows", [SLOTS * P, DM], F32).ap()

    ctx = ExitStack()
    with ctx:
        def sem(name):
            return ctx.enter_context(nc.semaphore(name))

        def small(name, shape, dt=F32):
            return ctx.enter_context(nc.sbuf_tensor(name, shape, dt))

        ARENA = 50720
        arena = small("arena", [P, ARENA])
        psum = ctx.enter_context(nc.psum_tensor("psum", [P, 8, 512], F32))

        def cut(at, *dims):
            n = math.prod(dims)
            assert at + n <= ARENA
            v = arena[:, at:at + n]
            if len(dims) == 2:
                v = v.rearrange("p (a b) -> p a b", a=dims[0])
            elif len(dims) == 3:
                v = v.rearrange("p (a b c) -> p a b c", a=dims[0], b=dims[1])
            return v

        hnT = cut(0, DC, SEQ)
        mixT = cut(8192, DC, SEQ)
        XIN = 4
        xin = cut(8192, XIN, DM)
        mnT = cut(12288, DC, MEM)
        k_raw = cut(14336, MT, DM)
        w_mk = cut(16384, DC, DM)
        w_mv = cut(24576, DC, DM)
        w_qkv = cut(32768, DC, 3 * SBW)
        mv0 = cut(45056, MT, DM)
        mkT0 = cut(47104, DC, MEM)
        qz = cut(16384, HEADS, SEQ)
        kT = cut(24576, PAIRS, SEQ)
        v_sb = cut(28672, T, SBW)
        f_sb = cut(32768, 2, SEQ)
        g_sb = cut(34816, 2, SEQ)
        w_rows = cut(36864, 2, GRP, SEQ)
        wT_sb = cut(45056, 2, 512)
        fall = cut(46080, 2, SEQ + 1)
        zeros = cut(48640, 1)
        mqT_h = cut(16384, HEADS, SEQ)
        mkT_h = cut(24576, HEADS, SEQ)
        v_mla = cut(32768, T, SBW)
        w_c = cut(36864, DC, MLAW)
        w_q = cut(42240, 3, HEADS * QK)
        w_kv = cut(44544, 2, HEADS * P)
        cn = cut(46592, QR + KVR)
        cT = cut(47232, 5, P)
        qf = cut(47872, HEADS, QK)
        kf = cut(48640, HEADS, QK)
        sq = cut(49408, HEADS, QK)
        p_rows = cut(36864, 2, GRP, SEQ)
        pT_sb = cut(45056, 2, 512)
        wo_sb = cut(0, DC, DM)
        wmq_sb = cut(16384, DC, DM)
        wmo_sb = cut(24576, DC, DM)
        x_in = cut(32768, DM)
        h1 = cut(33792, 2, DM)
        h1T = cut(35840, DC, P)
        mq_sb = cut(36864, DM)
        mqT = cut(37888, DC, P)
        mp = cut(38912, MH, MEM)
        mpT = cut(39936, MH * MT, P)
        moT = cut(40960, DC, P)
        tn = cut(41984, DM)
        tT = cut(43008, DC, P)
        mix_sq = cut(44032, DC, P)
        moe_g = cut(45056, DM)
        mkT1 = cut(46080, DC, MEM)
        mv1 = cut(48128, MT, DM)
        junk = cut(50176, 544)
        junk_b = junk.bitcast(BF16)
        h2 = mixT
        wexp = [(cut(16384 + 12288 * b, DC, FF), cut(20480 + 12288 * b, DC, FF),
                 cut(24576 + 12288 * b, FC, DM)) for b in range(2)]
        xg = cut(40960, 2, DM)
        xT = cut(43008, 2, DC, P)
        silu = cut(45056, FF)
        hrow = cut(45568, FF)
        hTe = cut(46080, FC, P)
        ysb = cut(46592, 2, DM)
        rt = [cut(40960 + P * i, T, NE) for i in range(12)]
        onehot = cut(42496, 2 * T, P)
        token_at = cut(44544, 2 * T, TAB)
        y1 = cut(16384, 2, DM)
        y2 = cut(18432, 2, DM)
        yo = cut(20480, 2, DM)

        ident = small("ident", [P, P])
        before = small("before", [P, P])
        ones = small("ones", [P, P])
        cos = small("cos", [P, T, HALF])
        sin = small("sin", [P, T, HALF])
        rtmp = small("rtmp", [P, 5, P])
        mix_sum = rtmp[:, 0:2, :]
        lane = rtmp[:, 2, :]
        slot_no = rtmp[:, 3, 0:TAB]
        pos_i = small("pos_i", [P, T], I32)
        posf = small("posf", [P, T])
        invf = small("invf", [P, HALF])
        gx = small("gx", [P, DC])
        gmem = small("gmem", [P, DC])
        gcq = small("gcq", [P, 5])
        gq96 = small("gq96", [P, QK])
        gk96 = small("gk96", [P, QK])
        gmh = small("gmh", [P, 4])
        gmix = small("gmix", [P, DC])
        ghq = small("ghq", [P, DC])
        kr = small("kr", [P, ROPE])
        ms = small("ms", [P, 16])
        rr = small("rr", [P, 16])
        mst = small("mst", [P, 32])
        rst = small("rst", [P, 32])
        nwt = small("nwt", [P, 32])
        mx = small("mx", [P, 4])
        nb = small("nb", [P, 4])
        rs = small("rs", [P, 4])
        ri = small("ri", [P, 4])
        st2 = small("st2", [P, 2])
        r2 = small("r2", [P, 2])
        r1 = small("r1", [P, 2])
        m1 = small("m1", [P, 1])
        m4 = small("m4", [P, MH])
        v4 = small("v4", [P, MH])
        sc = small("sc", [P, MH])
        mmx = small("mmx", [P, MH])
        mnb = small("mnb", [P, MH])
        mrs = small("mrs", [P, MH])
        mri = small("mri", [P, MH])
        m2 = small("m2", [P, 1])
        rt2 = small("rt2", [P, 1])
        wr = small("wr", [P, DC, NG + NE])
        br = small("br", [P, NG + NE])
        lg = small("lg", [P, T, NG + NE])
        rsm = cut(48640, 16, T)
        esm = cut(48768, 8, NE)
        s4 = cut(48896, 3, T, EG)
        io4 = small("io4", [P, EG])
        io16 = small("io16", [P, NE])
        slotf = small("slotf", [P, SLOTS])
        posk = small("posk", [P, 2, T], I32)
        adr = small("adr", [P, 2, 2 * T], I32)
        adrf = small("adrf", [P, 2, 2 * T])
        tokf = small("tokf", [P, T])
        thr = small("thr", [P, T - 1])
        nums = small("nums", [P, 2 * NE], I32)
        eidt = small("eidt", [P, SLOTS], I32)
        nitt = small("nitt", [P, 2], I32)
        idx_all = small("idx_all", [P, TAB], I32)
        idx = small("idx", [P, 2], I32)
        tiny = small("tiny", [P, 1])
        slot_cmp = junk[:, 0:SLOTS * NE].rearrange("p (s e) -> p s e", s=SLOTS)

        s_gain = sem("gains_loaded")
        s_pos = sem("positions_loaded")
        s_gcol = sem("input_gains_loaded")
        s_ang = sem("angles_ready")
        s_rot = sem("rotary_tables_ready")
        s_const = sem("constants_made")
        s_xin = [sem(f"input_tile_loaded{i}") for i in range(XIN)]
        s_wmk = [sem(f"w_mk_loaded{i}") for i in range(2)]
        s_wmv = sem("w_mv_loaded")
        s_wqkv = sem("w_qkv_loaded")
        s_sq = sem("mean_square_ready")
        s_rr = sem("rstd_ready")
        s_xn = sem("input_tile_normed")
        s_t = sem("transposition_bank_full")
        s_te = {"act": sem("transposition_bank_emptied_by_act"), "dve": sem("transposition_bank_emptied_by_dve")}
        s_mkv = sem("mem_kv_product")
        s_mkvo = sem("mem_kv_copied")
        s_mkn = sem("mem_k_normed")
        s_spill = sem("mem_kv_spilled")
        s_mk1 = sem("mem_kv_reloaded")
        s_qz = sem("query_zeros")
        s_pr = sem("sb_projection_product")
        s_proA = sem("sb_projection_copied_by_act")
        s_proD = sem("sb_projection_copied_by_dve")
        s_s = sem("sb_scores_full")
        s_f = sem("sb_fail_ready")
        s_g = sem("sb_take_ready")
        s_fm = sem("sb_fail_masked")
        s_gm = sem("sb_take_masked")
        s_w = sem("sb_weights_ready")
        s_pv = sem("sb_value_product")
        s_o = sem("sb_output_copied")
        s_wc = sem("w_c_loaded")
        s_wuq = sem("w_uq_loaded")
        s_p1 = sem("mla_down_product")
        s_csq = sem("mla_down_squares")
        s_cr = sem("mla_down_rstd")
        s_ce = sem("mla_down_normed")
        s_kre = sem("mla_rope_key_taken")
        s_p3 = sem("mla_up_product")
        s_q3 = sem("mla_up_copied")
        s_qkf = sem("mla_heads_ready")
        s_ms = sem("mla_scores_full")
        s_nb = sem("mla_maximum_ready")
        s_e = sem("mla_exp_ready")
        s_pn = sem("mla_probabilities_ready")
        s_mpv = sem("mla_value_product")
        s_mo = sem("mla_output_copied")
        s_wo = sem("w_o_loaded")
        s_wmq = sem("w_mq_loaded")
        s_wmo = sem("w_mo_loaded")
        s_wos = sem("w_o_scaled")
        s_wmqs = sem("w_mq_scaled")
        s_moeg = sem("moe_gain_loaded")
        s_x = sem("x_tile_loaded")
        s_msq = sem("mixed_squares")
        s_om = sem("mix_product")
        s_h1a = sem("sb_part_added")
        s_h1 = sem("h1_ready")
        s_h1q = sem("h1_mean_square")
        s_msc = sem("mem_scores_full")
        s_mnb = sem("mem_maximum_ready")
        s_me = sem("mem_exp_ready")
        s_mp = sem("mem_probabilities_ready")
        s_mq = sem("mem_query_product")
        s_mqo = sem("mem_query_copied")
        s_mqs = sem("mem_query_scale_ready")
        s_mot = sem("mem_output_product")
        s_moto = sem("mem_output_copied")
        s_mop = sem("mem_projection_product")
        s_h2 = sem("h2_ready")
        s_h2q = sem("h2_mean_square")
        s_tn = sem("moe_input_ready")
        s_tnd = sem("moe_input_stored")
        s_wr = sem("router_loaded")
        s_rm = sem("expert_choice_ready")
        s_lane = sem("table_numbers_made")
        s_ab = sem("token_marks_ready")
        s_idx = sem("token_table_ready")
        s_plan = sem("slot_plan_ready")
        s_wg = [sem(f"w_gate_loaded{b}") for b in range(2)]
        s_wu = [sem(f"w_up_loaded{b}") for b in range(2)]
        s_wd = [sem(f"w_down_loaded{b}") for b in range(2)]
        s_go = sem("gather_allowed")
        s_ic = sem("slot_indices_ready")
        s_xg = [sem(f"slot_rows_gathered{b}") for b in range(2)]
        s_xt = sem("slot_rows_transposed")
        s_xa = sem("slot_first_half_copied")
        s_xb = sem("slot_second_half_copied")
        s_gf = sem("gate_product")
        s_uf = sem("up_product")
        s_si = sem("silu_ready")
        s_h = sem("expert_hidden_ready")
        s_ht = sem("expert_hidden_transposed")
        s_hto = sem("expert_hidden_copied")
        s_y = sem("down_product")
        s_yo = sem("down_copied")
        s_ys = [sem(f"expert_rows_stored{b}") for b in range(2)]
        s_cg = [sem(f"chosen_rows_gathered{b}") for b in range(2)]
        s_co = sem("combined_ready")
        s_out = [sem(f"output_stored{b}") for b in range(2)]
        s_dve = sem("dve_own")
        s_act = sem("act_own")
        s_pool = sem("pool_own")
        s_dveL = sem("dve_own_in_slots")
        s_actL = sem("act_own_in_slots")

        block = ctx.enter_context(nc.Block())
        GAINS = 10

        def bank(i):
            return psum[:, i, :]

        def pair(i):
            return psum[:, 2 * i:2 * i + 2, :].rearrange("p a b -> p (a b)")

        @block.sync
        def _(sp):
            def rows(t):
                return slice(t * P, (t + 1) * P)

            def load_tile(n):
                src = mem2[rows(n), :] if n < MT else x2[rows(n - MT), :]
                if n >= XIN:
                    last = ROUND[("mem", n - XIN, 1)] if n - XIN < MT else ROUND[("x", n - XIN - MT, 1)]
                    sp.wait_ge(s_t, last + 1)
                sp.dma_start(xin[:, n % XIN, :], src).then_inc(s_xin[n % XIN], 16)

            def chunks(w, c0, c1):
                return w[:, c0:c1].rearrange("(k p) n -> p k n", p=P)

            def load(b, e, part):
                src = (w_gate, w_up, w_down)[part][bass.ds(e, 1), :, :].rearrange("e (k p) n -> p (e k) n", p=P)
                sp.dma_start(wexp[b][part], src).then_inc((s_wg, s_wu, s_wd)[part][b], 16)

            load_tile(0)
            load_tile(1)
            for i in range(2):
                sp.dma_start(w_mk[:, 4 * i:4 * i + 4, :], chunks(w_mkv, 0, DM)[:, 4 * i:4 * i + 4, :]).then_inc(s_wmk[i], 16)
            load_tile(2)
            load_tile(3)
            sp.dma_start(w_mv, chunks(w_mkv, DM, 2 * DM)).then_inc(s_wmv, 16)
            sp.dma_start(w_qkv, chunks(w_in, 0, 3 * SBW)).then_inc(s_wqkv, 16)
            for n in range(4, MT + T):
                load_tile(n)
            for b in range(2):
                c = (2 + b) * SEQ
                sp.dma_start(y_dram[c:c + SEQ, :], x2).then_inc(s_ys[b], 16)
            sp.wait_ge(s_mkvo, 4)
            sp.dma_start(mv_dram, mv0.rearrange("p a b -> p (a b)")).then_inc(s_spill, 16)
            sp.wait_ge(s_te["dve"], EMPTIED[ROUND[("mk", 1, 1)]][1])
            sp.dma_start(mkT_dram, mkT0.rearrange("p a b -> p (a b)")).then_inc(s_spill, 16)
            sp.wait_ge(s_o, 2 * HEADS)
            sp.dma_start(w_c, chunks(w_in, MLA0, MLA0 + MLAW)).then_inc(s_wc, 16)
            sp.dma_start(w_q, chunks(w_uq, 0, HEADS * QK)).then_inc(s_wuq, 16)
            sp.dma_start(w_kv, chunks(w_ukv, 0, HEADS * P)).then_inc(s_wuq, 16)
            sp.wait_ge(s_p1, T)
            sp.dma_start(wo_sb, chunks(w_o, 0, DM)).then_inc(s_wo, 16)
            sp.wait_ge(s_t, ROUND[("kf", T - 1, 1)] + 1)
            sp.wait_ge(s_spill, 32)
            sp.dma_start(mkT1.rearrange("p a b -> p (a b)"), mkT_dram).then_inc(s_mk1, 16)
            sp.dma_start(mv1.rearrange("p a b -> p (a b)"), mv_dram).then_inc(s_mk1, 16)
            sp.wait_ge(s_mo, 2 * HEADS)
            sp.dma_start(x_in, x2[rows(0), :]).then_inc(s_x, 16)
            sp.dma_start(wmq_sb, chunks(w_mq, 0, DM)).then_inc(s_wmq, 16)
            sp.dma_start(moe_g, norm_moe_g.partition_broadcast(P)).then_inc(s_moeg, 16)
            sp.dma_start(wmo_sb, chunks(w_mo, 0, DM)).then_inc(s_wmo, 16)
            for i in range(T + 1):
                if i + 1 < T:
                    sp.wait_ge(s_h1a, i + 1)
                    sp.dma_start(x_in, x2[rows(i + 1), :]).then_inc(s_x, 16)
                if i >= 1:
                    sp.wait_ge(s_tn, i)
                    sp.dma_start(tn_dram[rows(i - 1), :], tn).then_inc(s_tnd, 16)
                if i == T - 1:
                    sp.wait_ge(s_mq, T)
                    load(0, 0, 0)
                    load(0, 0, 1)
            sp.wait_ge(s_mop, T)
            load(0, 0, 2)
            sp.wait_ge(s_plan, 1)
            e = sp.value_load(eidt[0:1, 1:2], min_val=0, max_val=NE - 1)
            for part in range(3):
                load(1, e, part)
            n_it = sp.value_load(nitt[0:1, 0:1], min_val=NE // 2, max_val=SLOTS // 2)
            with sp.Fori(1, n_it) as k:
                for b in range(2):
                    e = sp.value_load(eidt[0:1, bass.ds(2 * k + b, 1)], min_val=0, max_val=NE - 1)
                    for part, used in enumerate((s_gf, s_uf, s_y)):
                        sp.wait_ge(used, 2 * k + b - 1)
                        load(b, e, part)
            for t in range(T):
                sp.wait_ge(s_co, t + 1)
                sp.dma_start(out2[rows(t), :], yo[:, t % 2, :]).then_inc(s_out[t % 2], 16)
            for b in range(2):
                sp.wait_ge(s_out[b], 16 * T // 2)

        @block.gpsimd
        def _(pool):
            do = Steps(pool, s_pool)
            INV = (np.float32(THETA) ** (-(np.arange(HALF, dtype=np.float32) * np.float32(2.0) / np.float32(ROPE)))).astype(np.float32)
            do(pool.memset(ident[:, :], 0.0))
            do(pool.memset(ones[:, :], 1.0))
            for j in range(HALF):
                do(pool.memset(invf[:, j:j + 1], float(INV[j])))
            do.settle()
            do(pool.affine_select(out=ident[:, :], in_=ident[:, :], compare_op=ALU.not_equal, fill=1.0,
                                  base=0, pattern=[[-1, P]], channel_multiplier=1))
            do(pool.affine_select(out=before[:, :], in_=ones[:, :], compare_op=ALU.is_gt, fill=0.0,
                                  base=0, pattern=[[1, P]], channel_multiplier=-1))
            do(pool.iota(nums[:, 0:NE], pattern=[[1, NE]], base=0, channel_multiplier=0))
            do(pool.iota(nums[:, NE:NE + T - 1], pattern=[[P, T - 1]], base=P, channel_multiplier=0))
            do(pool.iota(nums[:, NE + T:NE + 2 * T], pattern=[[P, T]], base=0, channel_multiplier=1))
            do(pool.iota(eidt[:, :], pattern=[[1, SLOTS]], base=0, channel_multiplier=0))
            do.settle()
            do(pool.tensor_copy(io16[:, :], nums[:, 0:NE]))
            do(pool.tensor_copy(io4[:, :], nums[:, 0:EG]))
            do(pool.tensor_copy(thr[:, :], nums[:, NE:NE + T - 1]))
            do(pool.tensor_copy(tokf[:, :], nums[:, NE + T:NE + 2 * T]))
            do(pool.tensor_copy(slotf[:, :], eidt[:, :]))
            do.settle()
            do(pool.memset(tiny[:, :], 0.0), s_const)

            pool.wait_ge(s_mkv, 4)
            pool.memset(qz[HD:P, 0:HEADS:2, :], 0.0).then_inc(s_qz, 1)
            pool.memset(qz[0:HD, 1:HEADS:2, :], 0.0).then_inc(s_qz, 1)
            pool.wait_ge(s_pr, 12)
            pool.wait_ge(s_spill, 32)
            for b in range(2):
                pool.memset(fall[:, b, SEQ:SEQ + 1], 1.0).then_inc(s_qz, 1)
            pool.memset(zeros, 0.0).then_inc(s_qz, 1)
            for u, (h, g) in enumerate(UNITS):
                for r in range(GRP):
                    n, t = GRP * u + r, GRP * g + r
                    for buf, full, masked, fill in ((f_sb, s_f, s_fm, 1.0), (g_sb, s_g, s_gm, 0.0)):
                        block_ = buf[:, n % 2, t * P:(t + 1) * P]
                        pool.wait_ge(full, n + 1)
                        pool.affine_select(out=block_, in_=block_, compare_op=ALU.is_gt, fill=fill, base=0,
                                           pattern=[[-1, P]], channel_multiplier=1).then_inc(masked, 1)

            pool.wait_ge(s_qkf, T)
            whole = rtmp[:, 4, :].bitcast(I32)
            do(pool.iota(whole, pattern=[[1, P]], base=0, channel_multiplier=0))
            do.settle()
            do(pool.tensor_copy(lane, whole), s_lane)
            do(pool.tensor_copy(slot_no, whole[:, 0:TAB]), s_lane)

            pool.wait_ge(s_idx, 1)
            pool.wait_ge(s_tnd, 16 * T)

            def pick(b, column):
                pool.tensor_copy(idx[:, b:b + 1], idx_all[:, column]).then_inc(s_ic, 1)

            def fetch(b):
                pool.indirect_dma_start(out=xg[:, b, :], out_offset=None, in_=tn_dram,
                                        in_offset=bass.IndirectOffsetOnAxis(ap=idx[:, b:b + 1], axis=0)).then_inc(s_xg[b], 16)

            for b in range(2):
                pick(b, slice(b, b + 1))
                pool.wait_ge(s_ic, b + 1)
                fetch(b)

            def refetch(s, b):
                column = pool.snap(s + 1)
                pool.wait_ge(s_xt, 2 * s)
                pick(b, bass.ds(column, 1))
                pool.wait_ge(s_ic, s + 2)
                pool.sem_inc(s_go, 1)
                fetch(b)

            pool.wait_ge(s_plan, 1)
            n_it = pool.value_load(nitt[0:1, 0:1], min_val=NE // 2, max_val=SLOTS // 2)
            pool.wait_ge(s_xt, 2)
            pick(0, slice(2, 3))
            pool.wait_ge(s_ic, 3)
            fetch(0)
            with pool.Fori(1, n_it) as k:
                refetch(2 * k, 1)
                refetch(2 * k + 1, 0)
            all_slots = pool.snap(16 * n_it + 16)
            for b in range(2):
                pool.wait_ge(s_ys[b], all_slots)
            pool.wait_ge(s_xg[0], all_slots)
            pool.sem_inc(s_go, 1)
            for t in range(T):
                if t >= 2:
                    pool.wait_ge(s_co, t - 1)
                for j, buf in enumerate((y1, y2)):
                    pool.indirect_dma_start(out=buf[:, t % 2, :], out_offset=None, in_=y_dram,
                                            in_offset=bass.IndirectOffsetOnAxis(ap=posk[:, j, t:t + 1], axis=0)).then_inc(s_cg[t % 2], 16)

        @block.scalar
        def _(act):
            do = Steps(act, s_act)

            with nc.allow_non_contiguous_dma(reason="small gain vectors laid along the partitions"):
                for n, (dst, src) in enumerate(((gmem[:, :], mem_src_g.rearrange("(c p) -> p c", p=P)),
                                 (gx[:, :], norm_mix_g.rearrange("(c p) -> p c", p=P)),
                                 (gmh[:, 0:2], mem_qhead_g.rearrange("(c p) -> p c", p=P)),
                                 (gmh[:, 2:4], mem_khead_g.rearrange("(c p) -> p c", p=P)),
                                 (gcq[:, 0:3], mla_q_norm_g.rearrange("(c p) -> p c", p=P)),
                                 (gcq[:, 3:5], mla_kv_norm_g.rearrange("(c p) -> p c", p=P)),
                                 (gq96[:, 0:NOPE], mla_qn_g.partition_broadcast(P)),
                                 (gq96[:, NOPE:QK], mla_qr_g.partition_broadcast(P)),
                                 (gk96[:, 0:NOPE], mla_kn_g.partition_broadcast(P)),
                                 (gk96[:, NOPE:QK], mla_kr_g.partition_broadcast(P)),
                                 (gmix[:, 0:4], sb_out_g.rearrange("(c p) -> p c", p=P)),
                                 (gmix[:, 4:8], mla_out_g.rearrange("(c p) -> p c", p=P)))):
                    act.dma_start(dst, src).then_inc(s_gcol if n < 2 else s_gain, 16)
                act.dma_start(ghq[:, :], norm_mem_g.rearrange("(c p) -> p c", p=P)).then_inc(s_pos, 16)
                act.dma_start(pos_i[:, :], positions[0].rearrange("(t p) -> p t", p=P)).then_inc(s_pos, 16)
                act.dma_start(wr[:, :, 0:NG], w_group.rearrange("(c p) e -> p c e", p=P)).then_inc(s_wr, 16)
                act.dma_start(wr[:, :, NG:NG + NE], w_router.rearrange("(c p) e -> p c e", p=P)).then_inc(s_wr, 16)
                act.dma_start(br[:, 0:NG], b_group.partition_broadcast(P)).then_inc(s_wr, 16)
                act.dma_start(br[:, NG:NG + NE], b_router.partition_broadcast(P)).then_inc(s_wr, 16)

            def empty(key, dst, src):
                i = ROUND[key]
                act.wait_ge(s_t, i + 1)
                do(act.activation(dst, src, ACT.Copy), s_te["act"])

            def squares(n):
                act.wait_ge(s_xin[n % XIN], 16 * (n // XIN + 1))
                do(act.activation(junk_b[:, 0:DM], xin[:, n % XIN, :], ACT.Square, scale=DM ** -0.5,
                                  accum_out=ms[:, n:n + 1]), s_sq)
                do.settle()

            for j in range(-1, 4):
                for n in (2 * j + 2, 2 * j + 3):
                    squares(n)
                for n in (2 * j + 2, 2 * j + 3):
                    act.wait_ge(s_rr, n // 2 + 1)
                    do(act.activation(xin[:, n % XIN, :], xin[:, n % XIN, :], ACT.Copy, scale=rr[:, n:n + 1]), s_xn)
                if j < 0:
                    continue
                act.wait_ge(s_mkv, j + 1)
                src = pair(1 + j % 3)
                if j < 2:
                    for h in range(MH):
                        do(act.activation(junk_b[:, 0:MHD], src[:, MHD * h:MHD * (h + 1)], ACT.Square,
                                          scale=MHD ** -0.5, accum_out=mst[:, MH * j + h:MH * j + h + 1]))
                        do.settle()
                    do(act.activation(k_raw[:, j, :], src, ACT.Copy), s_mkvo)
                else:
                    do(act.activation(mv0[:, j - 2, :], src, ACT.Copy), s_mkvo)
            for p in range(PAIRS):
                act.wait_ge(s_pr, 2 * p + 2)
                do(act.activation(kT[:, p, :], pair(1 + (4 + 2 * p + 1) % 3), ACT.Copy), s_proA)

            act.wait_ge(s_ang, 1)
            for dst, src in ((sin, rtmp[:, 0, :]), (cos, rtmp[:, 1, :])):
                do(act.activation(dst[:, :, :].rearrange("p a b -> p (a b)"), src, ACT.Sin), s_rot)

            def take(u, r):
                g = UNITS[u][1]
                n, L = GRP * u + r, P * (GRP * g + r + 1)
                src = pair(1 + n % 2)[:, 0:L]
                act.wait_ge(s_s, n + 1)
                if n >= 2:
                    act.wait_ge(s_w, n - 1)
                do(act.activation(f_sb[:, n % 2, 0:L], src, ACT.Sigmoid, scale=-(HD ** -0.5)), s_f)
                do(act.activation(g_sb[:, n % 2, 0:L], src, ACT.Sigmoid, scale=HD ** -0.5), s_g)

            def spread(kind, bufs, u, j, s_done):
                i = ROUND[(kind, u, j)]
                first = ROUND[(kind, 0, 0)]
                lo = P * max(0, j - GRP * UNITS[u][1])
                if i - first >= 2:
                    act.wait_ge(s_done, i - first - 1)
                empty((kind, u, j), bufs[:, (i - first) % 2, lo:512], bank(i % 2)[:, lo:512])

            def attention(kind, bufs, s_done, one):
                act_units = 2 * HEADS
                for r in range(GRP):
                    one(0, r)
                for u in range(act_units):
                    for j in range(blocks(u)):
                        spread(kind, bufs, u, j, s_done)
                        if u + 1 < act_units and j < GRP:
                            one(u + 1, j)

            act.wait_ge(s_proD, 8)
            attention("sb", wT_sb, s_pv, take)

            for i in range(T + 2):
                if i < T:
                    act.wait_ge(s_p1, i + 1)
                    for c, (a, b, src) in enumerate(((0, QR, bank(2)[:, 0:QR]), (QR, QR + KVR, bank(3)[:, 0:KVR]),
                                                     (0, ROPE, bank(3)[:, KVR:KVR + ROPE]))):
                        n = b - a
                        do(act.activation(junk_b[:, 0:n], src, ACT.Square, scale=n ** -0.5,
                                          accum_out=mst[:, c:c + 1]), s_csq if c == 2 else None)
                        do.settle()
                    act.wait_ge(s_cr, i + 1)
                    do(act.activation(cn[:, 0:QR], bank(2)[:, 0:QR], ACT.Copy, scale=rst[:, 0:1]))
                    act.wait_ge(s_kre, i + 1)
                    do(act.activation(cn[:, QR:QR + KVR], bank(3)[:, 0:KVR], ACT.Copy, scale=rst[:, 1:2]), s_ce)
                if i >= 2:
                    for kind, dst in (("qf", mqT_h), ("kf", mkT_h)):
                        for half in range(2):
                            key = (kind, i - 2, half)
                            empty(key, dst[0:QK, 4 * half:4 * half + 4, (i - 2) * P:(i - 1) * P],
                                  bank(ROUND[key] % 2)[0:QK, :].rearrange("p (a b) -> p a b", a=4))
                if 1 <= i <= T:
                    act.wait_ge(s_p3, i)
                    if i >= 2:
                        act.wait_ge(s_t, ROUND[("kf", i - 2, 1)] + 1)
                    for half in range(2):
                        hs = slice(4 * half, 4 * half + 4)
                        src = bank(4 + half)[:, 0:4 * QK].rearrange("p (a b) -> p a b", a=4)
                        kv = bank(6 + half).rearrange("p (a b) -> p a b", a=4)
                        do(act.activation(qf[:, hs, :], src, ACT.Copy))
                        do(act.activation(kf[:, hs, 0:NOPE], kv[:, :, 0:NOPE], ACT.Copy))
                        do(act.activation(v_mla[:, i - 1, 4 * half * HD:(4 * half + 4) * HD].rearrange("p (a b) -> p a b", a=4),
                                          kv[:, :, NOPE:NOPE + HD], ACT.Copy), s_q3)

            def exps(u, r):
                n, g = GRP * u + r, UNITS[u][1]
                L = P * (GRP * g + r + 1)
                act.wait_ge(s_nb, n + 1)
                if u >= 2:
                    act.wait_ge(s_t, ROUND[("mla", u - 2, blocks(u - 2) - 1)] + 1)
                if n >= 4:
                    act.wait_ge(s_pn, n - 3)
                do(act.activation(p_rows[:, u % 2, r, 0:L], pair(1 + n % 2)[:, 0:L], ACT.Exp, scale=QK ** -0.5,
                                  bias=nb[:, n % 4:n % 4 + 1], accum_out=rs[:, n % 4:n % 4 + 1]), s_e)

            attention("mla", pT_sb, s_mpv, exps)

            def wide(key2, dst):
                for half in range(2):
                    key = (*key2, half)
                    empty(key, dst[:, 4 * half:4 * half + 4, :].rearrange("p a b -> p (a b)"), bank(ROUND[key] % 2))

            for i in range(T + 2):
                if 1 <= i <= T:
                    wide(("mqT", i - 1), mqT)
                if i < T:
                    act.wait_ge(s_h1, i + 1)
                    do(act.activation(junk_b[:, 0:DM], h1[:, i % 2, :], ACT.Square, scale=DM ** -0.5,
                                      accum_out=m1[:, 0:1]), s_h1q)
                    wide(("hT", i), h1T)
                if 1 <= i <= T:
                    act.wait_ge(s_mnb, i)
                    if i >= 2:
                        act.wait_ge(s_t, ROUND[("pT", i - 2, 1)] + 1)
                    for h in range(MH):
                        do(act.activation(mp[:, h, :], pair(3)[:, MEM * h:MEM * (h + 1)], ACT.Exp, scale=sc[:, h:h + 1],
                                          bias=mnb[:, h:h + 1], accum_out=mrs[:, h:h + 1]), s_me)
                if i < T:
                    act.wait_ge(s_mq, i + 1)
                    for h in range(MH):
                        do(act.activation(junk_b[:, 0:MHD], pair(1)[:, MHD * h:MHD * (h + 1)], ACT.Square,
                                          scale=MHD ** -0.5, accum_out=m4[:, h:h + 1]))
                        do.settle()
                    do(act.activation(mq_sb, pair(1), ACT.Copy), s_mqo)
                if 1 <= i <= T:
                    wide(("pT", i - 1), mpT)
                    act.wait_ge(s_mot, i)
                    do(act.activation(moT.rearrange("p a b -> p (a b)"), pair(2), ACT.Copy), s_moto)
                if i >= 2:
                    wide(("tT", i - 2), tT)
                if 1 <= i <= T:
                    act.wait_ge(s_h2, i)
                    do(act.activation(junk_b[:, 0:DM].rearrange("p (a b) -> p a b", a=DC), h2[:, :, (i - 1) * P:i * P],
                                      ACT.Square, scale=DM ** -0.5, accum_out=m2[:, 0:1]), s_h2q)

            act.wait_ge(s_rm, 1)
            do(act.activation(s4[:, 2, :, :], s4[:, 1, :, :], ACT.Exp), s_rm)
            do(act.activation(rsm[:, 8, :], rsm[:, 7, :], ACT.Exp), s_rm)

            act.wait_ge(s_plan, 1)
            n_it = act.value_load(nitt[0:1, 0:1], min_val=NE // 2, max_val=SLOTS // 2)
            for b in range(2):
                act.wait_ge(s_ys[b], 16)
            act.sem_inc(s_yo, 2)

            def rows_out(s, b):
                act.wait_ge(s_xt, 2 * s + 2)
                act.activation(xT[:, b, 4:8, :].rearrange("p a b -> p (a b)"), bank(1), ACT.Copy).then_inc(s_xb, 1)

            def gate_out(s):
                act.wait_ge(s_gf, s + 1)
                act.activation(silu, bank(2), ACT.Silu).then_inc(s_si, 1)

            def down_out(s, b, stored):
                act.wait_ge(s_y, s + 1)
                act.wait_ge(s_ys[b], stored)
                act.activation(ysb[:, b, :], pair(2 + b), ACT.Copy).then_inc(s_yo, 1)
                act.wait_ge(s_yo, s + 3)
                act.dma_start(y_dram[bass.ds(s * P, P), :], ysb[:, b, :]).then_inc(s_ys[b], 16)

            def slot(s, b, stored):
                act.wait_ge(s_h, s)
                gate_out(s)
                rows_out(s + 1, 1 - b)
                down_out(s - 1, 1 - b, stored)

            rows_out(0, 0)
            gate_out(0)
            rows_out(1, 1)
            slot(1, 1, 16)
            with act.Fori(1, n_it) as k:
                slot(2 * k, 0, 16 * k)
                slot(2 * k + 1, 1, 16 * k + 16)
            down_out(2 * n_it - 1, 1, 16 * n_it)

        @block.vector
        def _(dve):
            do = Steps(dve, s_dve)

            def one(ins, sem_=None):
                do(ins, sem_)
                do.settle()

            def rsqrt(y, v, sem_=None):
                n = v.shape[-1]
                w = nwt[:, 0:n]
                one(dve.tensor_scalar(w.bitcast(I32), v.bitcast(I32), 1, None, ALU.logical_shift_right))
                one(dve.tensor_scalar(y.bitcast(I32), w.bitcast(I32), -1.0, float(0x5F3759DF), ALU.mult, ALU.add))
                for step in range(3):
                    one(dve.tensor_tensor(w, y, y, ALU.mult))
                    one(dve.tensor_tensor(w, w, v, ALU.mult))
                    one(dve.tensor_scalar(w, w, -0.5, 1.5, ALU.mult, ALU.add))
                    one(dve.tensor_tensor(y, y, w, ALU.mult), sem_ if step == 2 else None)

            def rotate(dst, src, t):
                n = src.shape[1]
                c = cos[:, t, :].unsqueeze(1).to_broadcast([P, n, HALF])
                s = sin[:, t, :].unsqueeze(1).to_broadcast([P, n, HALF])
                a, b = src[:, :, 0:HALF], src[:, :, HALF:ROPE]
                v = [rtmp[:, i, 0:n * HALF].rearrange("p (a b) -> p a b", a=n) for i in range(4)]
                do(dve.tensor_tensor(v[0], a, c, ALU.mult))
                do(dve.tensor_tensor(v[1], b, s, ALU.mult))
                do(dve.tensor_tensor(v[2], b, c, ALU.mult))
                one(dve.tensor_tensor(v[3], a, s, ALU.mult))
                do(dve.tensor_tensor(dst[:, :, 0:HALF], v[0], v[1], ALU.subtract))
                one(dve.tensor_tensor(dst[:, :, HALF:ROPE], v[2], v[3], ALU.add))


            def rstds(pair_):
                dve.wait_ge(s_sq, 2 * pair_ + 2)
                c = slice(2 * pair_, 2 * pair_ + 2)
                one(dve.tensor_scalar(ms[:, c], ms[:, c], EPS, None, ALU.add))
                rsqrt(rr[:, c], ms[:, c], s_rr)

            def turned(key, dst, gain):
                i = ROUND[key]
                n = dst.shape[1]
                dve.wait_ge(s_t, i + 1)
                do(dve.tensor_tensor(dst, bank(i % 2)[:, 0:n * P].rearrange("p (a b) -> p a b", a=n),
                                     gain.unsqueeze(2).to_broadcast([P, n, P]), ALU.mult), s_te["dve"])

            rstds(0)
            dve.wait_ge(s_gcol, 32)
            for m in range(MT):
                for half in range(2):
                    hs = slice(4 * half, 4 * half + 4)
                    turned(("mem", m, half), mnT[:, hs, m * P:(m + 1) * P], gmem[:, hs])

            for j in range(4):
                rstds(j + 1)
                for t in (2 * j, 2 * j + 1):
                    for half in range(2):
                        hs = slice(4 * half, 4 * half + 4)
                        turned(("x", t, half), hnT[:, hs, t * P:(t + 1) * P], gx[:, hs])
                if j in (0, 1):
                    dve.wait_ge(s_mkvo, j + 1)
                    c = slice(MH * j, MH * j + MH)
                    one(dve.tensor_scalar(mst[:, c], mst[:, c], EPS, None, ALU.add))
                    rsqrt(rst[:, c], mst[:, c])
                    kv = k_raw[:, j, :].rearrange("p (a b) -> p a b", a=MH)
                    do(dve.tensor_tensor(kv, kv, rst[:, c].unsqueeze(2).to_broadcast([P, MH, MHD]), ALU.mult), s_mkn)
                if j == 1:
                    dve.wait_ge(s_gain, 16 * GAINS)
                    one(dve.tensor_tensor(gmh[:, 0:2], gmh[:, 0:2], gmh[:, 2:4], ALU.mult))
                if j in (1, 2):
                    m = j - 1
                    for half in range(2):
                        key = ("mk", m, half)
                        dve.wait_ge(s_t, ROUND[key] + 1)
                        src = bank(ROUND[key] % 2).rearrange("p (h c m) -> p h c m", h=2, c=2)
                        for c in range(2):
                            dst = mkT0[:, 4 * half + c:4 * half + 4:2, m * P:(m + 1) * P]
                            do(dve.tensor_scalar(dst, src[:, :, c, :], gmh[:, c:c + 1], None, ALU.mult),
                               s_te["dve"] if c else None)

            dve.wait_ge(s_qz, 2)
            for p in range(PAIRS):
                dve.wait_ge(s_pr, 2 * p + 1)
                src = pair(1 + (4 + 2 * p) % 3)
                do(dve.tensor_copy(qz[0:HD, 2 * p, :], src[0:HD, :]))
                do(dve.tensor_copy(qz[HD:P, 2 * p + 1, :], src[HD:P, :]), s_proD)
            for c in range(4):
                dve.wait_ge(s_pr, 9 + c)
                do(dve.tensor_copy(v_sb[:, 2 * c:2 * c + 2, :].rearrange("p a b -> p (a b)"),
                                   pair(1 + (12 + c) % 3)), s_proD)


            dve.wait_ge(s_pos, 32)
            dve.wait_ge(s_const, 1)
            one(dve.tensor_copy(posf[:, :], pos_i[:, :]))
            ang, cyc, tmp = rtmp[:, 0, :], rtmp[:, 1, :], rtmp[:, 2, :]
            a3 = ang.rearrange("p (a b) -> p a b", a=T)
            one(dve.tensor_tensor(a3, posf[:, :].unsqueeze(2).to_broadcast([P, T, HALF]),
                                  invf[:, :].unsqueeze(1).to_broadcast([P, T, HALF]), ALU.mult))
            one(dve.tensor_scalar(tmp, ang, 1.0 / (2 * math.pi), None, ALU.mult))
            one(dve.tensor_copy(cyc.bitcast(I32), tmp))
            one(dve.tensor_copy(tmp, cyc.bitcast(I32)))
            TWO_PI = (6.28125, 0.0019350051879882812, 3.019916e-07)
            for part in TWO_PI:
                one(dve.scalar_tensor_tensor(out=ang, in0=tmp, scalar=-part, in1=ang, op0=ALU.mult, op1=ALU.add))
            PI = float(np.nextafter(np.float32(math.pi), np.float32(0)))

            def wrap(v, w, sem_=None):
                one(dve.tensor_scalar(w, v, PI, -2 * math.pi, ALU.is_gt, ALU.mult))
                one(dve.tensor_tensor(v, v, w, ALU.add))
                one(dve.tensor_scalar(w, v, -PI, 2 * math.pi, ALU.is_lt, ALU.mult))
                one(dve.tensor_tensor(v, v, w, ALU.add))
                one(dve.tensor_scalar(v, v, PI, -PI, ALU.min, ALU.max), sem_)

            wrap(ang, tmp)
            one(dve.tensor_scalar(cyc, ang, math.pi / 2, None, ALU.add))
            wrap(cyc, tmp, s_ang)

            def out_rows(u, s_prod, s_copied, chunk0):
                h, g = UNITS[u]
                rows = slice(HD * (h % 2), HD * (h % 2) + HD)
                dve.wait_ge(s_prod, prod_count(u))
                do(dve.tensor_copy(mixT[rows, chunk0 + h // 2, 512 * g:512 * (g + 1)], bank(6 + u % 2)[rows, :]), s_copied)

            dve.wait_ge(s_qz, 5)
            for u in range(2 * HEADS):
                g = UNITS[u][1]
                for r in range(GRP):
                    n, L = GRP * u + r, P * (GRP * g + r + 1)
                    dve.wait_ge(s_fm, n + 1)
                    b = n % 2
                    one(dve.tensor_tensor_scan(fall[:, b, SEQ - L:SEQ][:, ::-1], f_sb[:, b, 0:L][:, ::-1],
                                               zeros.to_broadcast([P, L]), 1.0, ALU.mult, ALU.add))
                    dve.wait_ge(s_gm, n + 1)
                    if u >= 2 and r == 0:
                        dve.wait_ge(s_t, ROUND[("sb", u - 2, blocks(u - 2) - 1)] + 1)
                    do(dve.tensor_tensor(w_rows[:, u % 2, r, 0:L], g_sb[:, b, 0:L],
                                         fall[:, b, SEQ - L + 1:SEQ + 1], ALU.mult), s_w)
                if u >= 1:
                    out_rows(u - 1, s_pv, s_o, 0)
            out_rows(2 * HEADS - 1, s_pv, s_o, 0)

            def mla_down(i):
                dve.wait_ge(s_csq, i + 1)
                one(dve.tensor_scalar(mst[:, 0:3], mst[:, 0:3], EPS, None, ALU.add))
                rsqrt(rst[:, 0:3], mst[:, 0:3], s_cr)
                one(dve.scalar_tensor_tensor(out=kr[:, :], in0=bank(3)[:, KVR:KVR + ROPE], scalar=rst[:, 2:3],
                                             in1=gk96[:, NOPE:QK], op0=ALU.mult, op1=ALU.mult), s_kre)

            def mla_turn(i):
                turned(("c", i, 0), cT[:, 0:3, :], gcq[:, 0:3])
                turned(("c", i, 1), cT[:, 3:5, :], gcq[:, 3:5])

            def mla_heads(t, kr_t):
                dve.wait_ge(s_q3, 2 * t + 2)
                do(dve.tensor_tensor(sq, qf, qf, ALU.mult))
                do.settle()
                do(dve.tensor_reduce(mst[:, 8:16], sq[:, :, 0:NOPE], AX.X, ALU.add))
                one(dve.tensor_reduce(mst[:, 16:24], sq[:, :, NOPE:QK], AX.X, ALU.add))
                one(dve.tensor_tensor(sq[:, :, 0:NOPE], kf[:, :, 0:NOPE], kf[:, :, 0:NOPE], ALU.mult))
                one(dve.tensor_reduce(mst[:, 24:32], sq[:, :, 0:NOPE], AX.X, ALU.add))
                do(dve.tensor_scalar(mst[:, 8:16], mst[:, 8:16], 1.0 / NOPE, EPS, ALU.mult, ALU.add))
                do(dve.tensor_scalar(mst[:, 16:24], mst[:, 16:24], 1.0 / ROPE, EPS, ALU.mult, ALU.add))
                one(dve.tensor_scalar(mst[:, 24:32], mst[:, 24:32], 1.0 / NOPE, EPS, ALU.mult, ALU.add))
                rsqrt(rst[:, 8:32], mst[:, 8:32])

                def spread(c, n):
                    return rst[:, c:c + HEADS].unsqueeze(2).to_broadcast([P, HEADS, n])

                do(dve.tensor_tensor(qf[:, :, 0:NOPE], qf[:, :, 0:NOPE], spread(8, NOPE), ALU.mult))
                do(dve.tensor_tensor(qf[:, :, NOPE:QK], qf[:, :, NOPE:QK], spread(16, ROPE), ALU.mult))
                one(dve.tensor_tensor(kf[:, :, 0:NOPE], kf[:, :, 0:NOPE], spread(24, NOPE), ALU.mult))
                do(dve.tensor_tensor(qf, qf, gq96[:, :].unsqueeze(1).to_broadcast([P, HEADS, QK]), ALU.mult))
                one(dve.tensor_tensor(kf[:, :, 0:NOPE], kf[:, :, 0:NOPE],
                                      gk96[:, 0:NOPE].unsqueeze(1).to_broadcast([P, HEADS, NOPE]), ALU.mult))
                rotate(qf[:, :, NOPE:QK], qf[:, :, NOPE:QK], t)
                do(dve.tensor_copy(kf[:, :, NOPE:QK], krs[:, t % 2, :].unsqueeze(1).to_broadcast([P, HEADS, ROPE])), s_qkf)

            krs = rtmp[:, 4, 0:2 * ROPE].rearrange("p (a b) -> p a b", a=2)
            for i in range(T + 1):
                if i < T:
                    mla_down(i)
                    rotate(krs[:, i % 2, :].unsqueeze(1), kr[:, :].unsqueeze(1), i)
                    mla_turn(i)
                if i >= 1:
                    mla_heads(i - 1, None)

            def maximum(n):
                u, r = divmod(n, GRP)
                t = GRP * UNITS[u][1] + r
                L = P * (t + 1)
                src = pair(1 + n % 2)
                dve.wait_ge(s_ms, n + 1)
                one(dve.memset(src[0:64, L - 64:L], -1e30))
                one(dve.tensor_reduce(mx[:, n % 4:n % 4 + 1], src[:, 0:L], AX.X, ALU.max))
                do(dve.tensor_scalar(nb[:, n % 4:n % 4 + 1], mx[:, n % 4:n % 4 + 1], -(QK ** -0.5), None, ALU.mult), s_nb)

            def scale_rows(n):
                u, r = divmod(n, GRP)
                L = P * (GRP * UNITS[u][1] + r + 1)
                dve.wait_ge(s_e, n + 1)
                one(dve.reciprocal(ri[:, n % 4:n % 4 + 1], rs[:, n % 4:n % 4 + 1]))
                row = p_rows[:, u % 2, r, 0:L]
                do(dve.tensor_scalar(row, row, ri[:, n % 4:n % 4 + 1], None, ALU.mult), s_pn)

            for n in range(8 * HEADS):
                maximum(n)
                if n % GRP >= 1:
                    scale_rows(n - 1)
                if n % GRP == GRP - 1:
                    scale_rows(n)
                if n >= 8 and n % 4 == 3:
                    out_rows(n // 4 - 2, s_mpv, s_mo, 4)
            for u in range(2 * HEADS - 2, 2 * HEADS):
                out_rows(u, s_mpv, s_mo, 4)

            dve.wait_ge(s_wo, 16)
            for c in range(DC):
                do(dve.tensor_scalar(wo_sb[:, c, :], wo_sb[:, c, :], gmix[:, c:c + 1], None, ALU.mult), s_wos)

            def mixed_squares(i):
                m = mixT[:, :, i * P:(i + 1) * P]
                one(dve.tensor_tensor(mix_sq, m, m, ALU.mult))
                do(dve.tensor_reduce(mix_sum, mix_sq.rearrange("p (g c) t -> p g t c", g=2), AX.X, ALU.add), s_msq)

            dve.wait_ge(s_mo, 2 * HEADS)
            mixed_squares(0)
            dve.wait_ge(s_moeg, 16)
            for i in range(T + 2):
                if i < T:
                    i_ = ROUND[("stats", i, 0)]
                    dve.wait_ge(s_t, i_ + 1)
                    one(dve.tensor_scalar(st2[:, :], bank(i_ % 2)[:, 0:2], 1.0 / SBW, EPS, ALU.mult, ALU.add), s_te["dve"])
                    rsqrt(r2[:, :], st2[:, :])
                    if i == 0:
                        dve.wait_ge(s_wmq, 16)
                        for c in range(DC):
                            do(dve.tensor_scalar(wmq_sb[:, c, :], wmq_sb[:, c, :], ghq[:, c:c + 1], None, ALU.mult), s_wmqs)
                    dve.wait_ge(s_x, 16 * (i + 1))
                    dve.wait_ge(s_om, 2 * i + 1)
                    one(dve.scalar_tensor_tensor(out=h1[:, i % 2, :], in0=pair(1), scalar=r2[:, 0:1], in1=x_in,
                                                 op0=ALU.mult, op1=ALU.add), s_h1a)
                    dve.wait_ge(s_om, 2 * i + 2)
                    one(dve.scalar_tensor_tensor(out=h1[:, i % 2, :], in0=pair(2), scalar=r2[:, 1:2], in1=h1[:, i % 2, :],
                                                 op0=ALU.mult, op1=ALU.add), s_h1)
                if i + 1 < T:
                    mixed_squares(i + 1)
                if 1 <= i <= T:
                    dve.wait_ge(s_msc, i)
                    one(dve.tensor_reduce(mmx[:, :], pair(3).rearrange("p (a b) -> p a b", a=MH), AX.X, ALU.max))
                    one(dve.tensor_tensor(mmx[:, :], mmx[:, :], sc[:, :], ALU.mult))
                    do(dve.tensor_scalar(mnb[:, :], mmx[:, :], -1.0, None, ALU.mult), s_mnb)
                if i < T:
                    dve.wait_ge(s_h1q, i + 1)
                    one(dve.tensor_scalar(r1[:, 1:2], m1[:, :], EPS, None, ALU.add))
                    rsqrt(r1[:, 0:1], r1[:, 1:2])
                    one(dve.tensor_tensor(r1[:, 1:2], r1[:, 0:1], r1[:, 0:1], ALU.mult))
                if 1 <= i <= T:
                    dve.wait_ge(s_me, MH * i)
                    one(dve.reciprocal(mri[:, :], mrs[:, :]))
                    do(dve.tensor_tensor(mp, mp, mri[:, :].unsqueeze(2).to_broadcast([P, MH, MEM]), ALU.mult), s_mp)
                if i < T:
                    dve.wait_ge(s_mqo, i + 1)
                    one(dve.tensor_scalar(v4[:, :], m4[:, :], r1[:, 1:2], EPS, ALU.mult, ALU.add))
                    rsqrt(sc[:, :], v4[:, :])
                    one(dve.tensor_scalar(sc[:, :], sc[:, :], r1[:, 0:1], MHD ** -0.5, ALU.mult, ALU.mult), s_mqs)
                if i >= 2:
                    j = ROUND[("router", i - 2, 0)]
                    dve.wait_ge(s_t, j + 1)
                    if i == 2:
                        dve.wait_ge(s_wr, 64)
                    do(dve.tensor_tensor(lg[:, i - 2, :], bank(j % 2)[:, 0:NG + NE], br[:, :], ALU.add), s_te["dve"])
                if 1 <= i <= T:
                    dve.wait_ge(s_mop, i)
                    h2v = h2[:, :, (i - 1) * P:i * P]
                    one(dve.tensor_tensor(h2v, pair(3).rearrange("p (a b) -> p a b", a=DC),
                                          h1[:, (i - 1) % 2, :].rearrange("p (a b) -> p a b", a=DC), ALU.add), s_h2)
                    dve.wait_ge(s_h2q, i)
                    one(dve.tensor_scalar(m2[:, :], m2[:, :], EPS, None, ALU.add))
                    rsqrt(rt2[:, :], m2[:, :])
                    if i >= 2:
                        dve.wait_ge(s_t, ROUND[("tT", i - 2, 1)] + 1)
                        dve.wait_ge(s_tnd, 16 * (i - 1))
                    do(dve.scalar_tensor_tensor(out=tn.rearrange("p (a b) -> p a b", a=DC), in0=h2v, scalar=rt2[:, 0:1],
                                                in1=moe_g.rearrange("p (a b) -> p a b", a=DC), op0=ALU.mult, op1=ALU.mult), s_tn)

            do.settle()
            gl = lg[:, :, 0:NG]
            el = lg[:, :, NG:NG + NE].rearrange("p t (g e) -> p t g e", g=NG)

            def over(v, n):
                return v.unsqueeze(2).to_broadcast([P, T, n])

            def along(v, n=T):
                return v.unsqueeze(1).to_broadcast([P, n, v.shape[-1]])

            def first_of(best, values, index):
                eq = s4[:, 0, :, :]
                one(dve.tensor_tensor(eq, values, over(best, EG), ALU.is_equal))
                one(dve.tensor_scalar(eq, eq, -BIG, BIG, ALU.mult, ALU.add))
                one(dve.tensor_tensor(eq, eq, along(io4[:, :]), ALU.add))
                one(dve.tensor_reduce(index, eq, AX.X, ALU.min))

            gmax, gid, top1, i1, top2, i2 = (rsm[:, c, :] for c in range(6))
            one(dve.tensor_reduce(gmax, gl, AX.X, ALU.max))
            one(dve.tensor_tensor(s4[:, 1, :, :], gl, over(gmax, NG), ALU.subtract))
            first_of(gmax, gl, gid)
            oh, sel = s4[:, 0, :, :], rt[0][:, :, 0:EG]
            one(dve.tensor_tensor(oh, along(io4[:, :]), over(gid, NG), ALU.is_equal))
            for g in range(NG):
                dst = rt[1][:, :, 0:EG] if g else sel
                one(dve.tensor_tensor(dst, el[:, :, g, :], oh[:, :, g:g + 1].to_broadcast([P, T, EG]), ALU.mult))
                if g:
                    one(dve.tensor_tensor(sel, sel, rt[1][:, :, 0:EG], ALU.add))
            one(dve.tensor_reduce(top1, sel, AX.X, ALU.max))
            first_of(top1, sel, i1)
            one(dve.tensor_tensor(oh, along(io4[:, :]), over(i1, EG), ALU.is_equal))
            one(dve.tensor_scalar(oh, oh, -3e38, None, ALU.mult))
            one(dve.tensor_tensor(sel, sel, oh, ALU.add))
            one(dve.tensor_reduce(top2, sel, AX.X, ALU.max))
            first_of(top2, sel, i2)
            one(dve.tensor_tensor(rsm[:, 7, :], top2, top1, ALU.subtract), s_rm)
            for c in (3, 5):
                one(dve.scalar_tensor_tensor(out=rsm[:, c, :], in0=gid, scalar=float(EG), in1=rsm[:, c, :],
                                             op0=ALU.mult, op1=ALU.add))
            one(dve.tensor_tensor(rt[2], along(io16[:, :]), over(i1, NE), ALU.is_equal))
            one(dve.tensor_tensor(rt[3], along(io16[:, :]), over(i2, NE), ALU.is_equal))
            one(dve.tensor_tensor(rt[4], rt[2], rt[3], ALU.add), s_rm)
            dve.wait_ge(s_rm, 4)
            one(dve.tensor_reduce(rsm[:, 9, :], s4[:, 2, :, :], AX.X, ALU.add))
            one(dve.tensor_scalar(rsm[:, 10, :], rsm[:, 8, :], 1.0, None, ALU.add))
            one(dve.tensor_tensor(rsm[:, 9, :], rsm[:, 9, :], rsm[:, 10, :], ALU.mult))
            one(dve.reciprocal(rsm[:, 11, :], rsm[:, 9, :]))
            one(dve.tensor_tensor(rsm[:, 12, :], rsm[:, 11, :], rsm[:, 8, :], ALU.mult))
            j = ROUND[("rank", 0, 0)]
            dve.wait_ge(s_t, j + 1)
            one(dve.tensor_copy(rt[5].rearrange("p t e -> p (t e)"), bank(j % 2)[:, 0:T * NE]))
            one(dve.tensor_copy(rt[6].rearrange("p t e -> p (t e)"), bank(j % 2)[:, T * NE:2 * T * NE]), s_te["dve"])
            tiles, ends, total = esm[:, 1, :], esm[:, 2, :], None
            a, b_ = rt[6], rt[7]
            for step in (1, 2, 4):
                do(dve.tensor_copy(b_[:, 0:step, :], a[:, 0:step, :]))
                one(dve.tensor_tensor(b_[:, step:T, :], a[:, step:T, :], a[:, 0:T - step, :], ALU.add))
                a, b_ = b_, a
            do(dve.tensor_tensor(rt[5][:, 1:T, :], rt[5][:, 1:T, :], a[:, 0:T - 1, :], ALU.add))
            over_ = rt[0][:, 0:T - 1, :].rearrange("p c e -> p e c")
            one(dve.tensor_tensor(over_, a[:, T - 1, :].unsqueeze(2).to_broadcast([P, NE, T - 1]),
                                  along(thr[:, :], NE), ALU.is_gt))
            one(dve.tensor_reduce(tiles, over_, AX.X, ALU.add))
            one(dve.tensor_scalar(tiles, tiles, 1.0, None, ALU.add))
            one(dve.tensor_tensor_scan(ends, ones[:, 0:NE], tiles, 0.0, ALU.mult, ALU.add))
            one(dve.tensor_tensor(esm[:, 3, :], ends, tiles, ALU.subtract))
            one(dve.tensor_scalar(esm[:, 3, :], esm[:, 3, :], float(P), None, ALU.mult))
            one(dve.tensor_tensor(rt[5], rt[5], along(esm[:, 3, :]), ALU.add))
            do(dve.tensor_tensor(rt[6], rt[5], rt[2], ALU.mult))
            one(dve.tensor_tensor(rt[7], rt[5], rt[3], ALU.mult))
            do(dve.tensor_reduce(rsm[:, 13, :], rt[6], AX.X, ALU.add))
            one(dve.tensor_reduce(rsm[:, 14, :], rt[7], AX.X, ALU.add))
            flat = posk[:, :, :].rearrange("p c t -> p (c t)")
            one(dve.tensor_copy(flat, rsm[:, 13:15, :].rearrange("p c t -> p (c t)")))
            do(dve.tensor_scalar(adr[:, 0, :], flat, P - 1, None, ALU.bitwise_and))
            one(dve.tensor_scalar(adr[:, 1, :], flat, 7, None, ALU.logical_shift_right))
            one(dve.tensor_copy(adrf[:, :, :], adr[:, :, :]))
            dve.wait_ge(s_lane, 2)
            dve.wait_ge(s_tnd, 16 * T)
            for c in range(2 * T):
                do(dve.tensor_scalar(onehot[:, c, :], lane, adrf[:, 0, c:c + 1], None, ALU.is_equal))
                do(dve.tensor_scalar(token_at[:, c, :], slot_no, adrf[:, 1, c:c + 1], tokf[:, c % T:c % T + 1],
                                     ALU.is_equal, ALU.mult), s_ab)
            one(dve.tensor_tensor(slot_cmp, slotf[:, :].unsqueeze(2).to_broadcast([P, SLOTS, NE]), along(ends, SLOTS), ALU.is_ge))
            one(dve.tensor_reduce(junk[:, 512:512 + SLOTS], slot_cmp, AX.X, ALU.add))
            one(dve.tensor_scalar(junk[:, 512:512 + SLOTS], junk[:, 512:512 + SLOTS], float(NE - 1), None, ALU.min))
            one(dve.tensor_copy(eidt[:, :], junk[:, 512:512 + SLOTS]))
            one(dve.tensor_scalar(esm[:, 4, 0:1], ends[:, NE - 1:NE], 1.0, None, ALU.add))
            one(dve.tensor_copy(nitt[:, 1:2], esm[:, 4, 0:1]))
            one(dve.tensor_scalar(nitt[:, 0:1], nitt[:, 1:2], 1, None, ALU.logical_shift_right), s_plan)
            j = ROUND[("table", 0, 0)]
            dve.wait_ge(s_t, j + 1)
            one(dve.tensor_copy(idx_all[:, :], bank(j % 2)[:, 0:TAB]), s_idx)

            n_it = dve.value_load(nitt[0:1, 0:1], min_val=NE // 2, max_val=SLOTS // 2)

            def rows_out(s, b):
                dve.wait_ge(s_xt, 2 * s + 1)
                dve.tensor_copy(xT[:, b, 0:4, :].rearrange("p a b -> p (a b)"), bank(0)).then_inc(s_xa, 1)

            def hidden(s):
                dve.wait_ge(s_si, s + 1)
                dve.wait_ge(s_uf, s + 1)
                dve.tensor_tensor(hrow, silu, bank(3), ALU.mult).then_inc(s_h, 1)

            def hidden_out(s):
                dve.wait_ge(s_ht, s + 1)
                dve.tensor_copy(hTe.rearrange("p a b -> p (a b)"), bank(0)).then_inc(s_hto, 1)

            def slot(s, b):
                hidden_out(s - 1)
                hidden(s)
                rows_out(s + 1, 1 - b)

            rows_out(0, 0)
            hidden(0)
            rows_out(1, 1)
            slot(1, 1)
            with dve.Fori(1, n_it) as k:
                for b in range(2):
                    slot(2 * k + b, b)
            hidden_out(2 * n_it - 1)

            for t in range(T):
                dve.wait_ge(s_cg[t % 2], 32 * (t // 2 + 1))
                if t >= 2:
                    dve.wait_ge(s_out[t % 2], 16 * (t // 2))
                o3 = yo[:, t % 2, :].rearrange("p (a b) -> p a b", a=DC)
                one(dve.scalar_tensor_tensor(out=o3, in0=y1[:, t % 2, :].rearrange("p (a b) -> p a b", a=DC),
                                             scalar=rsm[:, 11, t:t + 1], in1=h2[:, :, t * P:(t + 1) * P], op0=ALU.mult, op1=ALU.add))
                one(dve.scalar_tensor_tensor(out=yo[:, t % 2, :], in0=y2[:, t % 2, :], scalar=rsm[:, 12, t:t + 1],
                                             in1=yo[:, t % 2, :], op0=ALU.mult, op1=ALU.add), s_co)

        @block.tensor
        def _(pe):
            def begin(key):
                i = ROUND[key]
                if i >= 2:
                    engine, count = EMPTIED[i - 2]
                    pe.wait_ge(s_te[engine], count)
                return bank(i % 2)

            def turn(key, blocks):
                dst = begin(key)
                at = 0
                for src in blocks:
                    rows = src.shape[-1]
                    mm = pe.transpose(dst[0:rows, at:at + P], src, ident[:, :])
                    at += P
                mm.then_inc(s_t, 1)

            def product(dst, pairs_, sem_=None):
                n = len(pairs_)
                for i, (a, b) in enumerate(pairs_):
                    mm = pe.matmul(dst, a, b, start=(i == 0), stop=(i == n - 1))
                if sem_ is not None:
                    mm.then_inc(sem_, 1)

            def halves(pair_, lhs, rhs, sem_, n=DC):
                for half in range(2):
                    product(bank(2 * pair_ + half), [(lhs(k), rhs(k, half)) for k in range(n)],
                            sem_ if half else None)

            pe.wait_ge(s_const, 1)
            for m in range(MT):
                pe.wait_ge(s_xn, m + 1)
                for half in range(2):
                    turn(("mem", m, half), [xin[:, m, (4 * half + c) * P:(4 * half + c + 1) * P] for c in range(4)])
            pe.wait_ge(s_te["dve"], EMPTIED[ROUND[("mem", 1, 1)]][1])
            for j in range(4):
                m = j % 2
                w = w_mk if j < 2 else w_mv
                if j == 3:
                    pe.wait_ge(s_mkvo, 1)
                for half in range(2):
                    if j == 0:
                        pass
                    if j == 2 and half == 0:
                        pe.wait_ge(s_wmv, 16)
                    for k in range(DC):
                        if j == 0 and half == 0 and k % 4 == 0:
                            pe.wait_ge(s_wmk[k // 4], 16)
                        mm = pe.matmul(bank(2 * (1 + j % 3) + half), mnT[:, k, m * P:(m + 1) * P],
                                       w[:, k, 512 * half:512 * half + 512], start=(k == 0), stop=(k == DC - 1))
                mm.then_inc(s_mkv, 1)
                for t in (2 * j, 2 * j + 1):
                    pe.wait_ge(s_xn, MT + t + 1)
                    for half in range(2):
                        turn(("x", t, half), [xin[:, (MT + t) % XIN, (4 * half + c) * P:(4 * half + c + 1) * P] for c in range(4)])
                if j in (1, 2):
                    pe.wait_ge(s_mkn, j)
                    for half in range(2):
                        turn(("mk", j - 1, half), [k_raw[:, j - 1, (4 * half + c) * P:(4 * half + c + 1) * P] for c in range(4)])

            pe.wait_ge(s_te["dve"], EMPTIED[ROUND[("x", T - 1, 1)]][1])
            pe.wait_ge(s_wqkv, 16)

            def projection_free(use):
                if use < 3 + 4 and use - 3 < 4:
                    pe.wait_ge(s_mkvo, use - 3 + 1)
                else:
                    o = use - 3 - 4
                    if o < 8:
                        pe.wait_ge(s_proA if o % 2 else s_proD, o // 2 + 1)
                    else:
                        pe.wait_ge(s_proD, 4 + o - 8 + 1)

            for p in range(PAIRS):
                for c in range(2):
                    use = 4 + 2 * p + c
                    projection_free(use)
                    col = c * SBW + p * P
                    halves(1 + use % 3, lambda k: w_qkv[:, k, col:col + P],
                           lambda k, half: hnT[:, k, 512 * half:512 * half + 512], s_pr)
            for c in range(4):
                use = 12 + c
                projection_free(use)
                for half in range(2):
                    t = 2 * c + half
                    product(bank(2 * (1 + use % 3) + half),
                            [(hnT[:, k, t * P:(t + 1) * P], w_qkv[:, k, 2 * SBW:3 * SBW]) for k in range(DC)],
                            s_pr if half else None)

            def attention(kind, rows, bufs, s_full, s_free, s_ready, s_prod, s_copied, scores, value):
                first = ROUND[(kind, 0, 0)]

                def weigh(u, j):
                    i = ROUND[(kind, u, j)]
                    h, g = UNITS[u]
                    lo = P * max(0, j - GRP * g)
                    pe.wait_ge(s_te["act"], EMPTIED[i][1])
                    if j == 0 and u >= 2:
                        pe.wait_ge(s_copied, u - 1)
                    pe.matmul(bank(6 + u % 2)[:, lo:512], value(h, j), bufs[:, (i - first) % 2, lo:512],
                              start=(j == 0), stop=(j == GRP * g + 3)).then_inc(s_prod, 1)

                def score(n):
                    u, r = divmod(n, GRP)
                    h, g = UNITS[u]
                    t = GRP * g + r
                    L = P * (t + 1)
                    if n >= 2:
                        pe.wait_ge(s_free, n - 1)
                    lhs, rhs = scores(h, t)
                    for at in range(0, L, 512):
                        end = min(L, at + 512)
                        mm = pe.matmul(pair(1 + n % 2)[:, at:end], lhs, rhs(at, end), start=True, stop=True)
                    mm.then_inc(s_full, 1)

                for n in range(GRP):
                    score(n)
                for u in range(2 * HEADS):
                    g, nj = UNITS[u][1], blocks(u)
                    for j in range(nj):
                        if u + 1 < 2 * HEADS and j < GRP:
                            score(GRP * (u + 1) + j)
                        pe.wait_ge(s_ready, GRP * (u + 1))
                        r0 = max(0, j - GRP * g)
                        dst = begin((kind, u, j))
                        for r in range(r0, GRP):
                            mm = pe.transpose(dst[:, r * P:(r + 1) * P], rows[:, u % 2, r, j * P:(j + 1) * P], ident[:, :])
                        mm.then_inc(s_t, 1)
                        if j >= 1:
                            weigh(u, j - 1)
                    weigh(u, nj - 1)

            pe.wait_ge(s_proA, 4)
            pe.wait_ge(s_proD, 8)
            attention("sb", w_rows, wT_sb, s_s, s_g, s_w, s_pv, s_o,
                      lambda h, t: (qz[:, h, t * P:(t + 1) * P], lambda a, b: kT[:, h // 2, a:b]),
                      lambda h, j: v_sb[:, j, P * (h // 2):P * (h // 2 + 1)])

            pe.wait_ge(s_o, 2 * HEADS)
            pe.wait_ge(s_g, 8 * HEADS)
            for i in range(T + 2):
                if i < T:
                    if i == 0:
                        pe.wait_ge(s_wc, 16)
                    else:
                        pe.wait_ge(s_ce, i)
                        pe.wait_ge(s_kre, i)
                    lhs = [hnT[:, k, i * P:(i + 1) * P] for k in range(DC)]
                    product(bank(2)[:, 0:QR], [(lhs[k], w_c[:, k, 0:QR]) for k in range(DC)])
                    product(bank(3)[:, 0:KVR + ROPE], [(lhs[k], w_c[:, k, QR:MLAW]) for k in range(DC)], s_p1)
                if 1 <= i <= T:
                    if i == 1:
                        pe.wait_ge(s_wuq, 32)
                    else:
                        pe.wait_ge(s_q3, 2 * (i - 1))
                    pe.wait_ge(s_te["dve"], EMPTIED[ROUND[("c", i - 1, 1)]][1])
                    for half in range(2):
                        product(bank(4 + half)[:, 0:4 * QK],
                                [(cT[:, k, :], w_q[:, k, 4 * QK * half:4 * QK * (half + 1)]) for k in range(3)])
                    for half in range(2):
                        product(bank(6 + half), [(cT[:, 3 + k, :], w_kv[:, k, 512 * half:512 * half + 512]) for k in range(2)],
                                s_p3 if half else None)
                if i >= 2:
                    pe.wait_ge(s_qkf, i - 1)
                    for kind, src in (("qf", qf), ("kf", kf)):
                        for half in range(2):
                            turn((kind, i - 2, half), [src[:, 4 * half + c, :] for c in range(4)])
                if i < T:
                    pe.wait_ge(s_ce, i + 1)
                    turn(("c", i, 0), [cn[:, c * P:(c + 1) * P] for c in range(3)])
                    turn(("c", i, 1), [cn[:, c * P:(c + 1) * P] for c in range(3, 5)])

            pe.wait_ge(s_te["act"], EMPTIED[ROUND[("kf", T - 1, 1)]][1])
            attention("mla", p_rows, pT_sb, s_ms, s_e, s_pn, s_mpv, s_mo,
                      lambda h, t: (mqT_h[0:QK, h, t * P:(t + 1) * P], lambda a, b: mkT_h[0:QK, h, a:b]),
                      lambda h, j: v_mla[:, j, P * (h // 2):P * (h // 2 + 1)])

            pe.wait_ge(s_mo, 2 * HEADS)
            for i in range(T + 2):
                if i < T:
                    pe.wait_ge(s_msq, i + 1)
                    dst = begin(("stats", i, 0))
                    for c in range(2):
                        product(dst[:, c:c + 1], [(mix_sum[:, c, :], ones[:, 0:1])], s_t if c else None)
                    if i == 0:
                        pe.wait_ge(s_wos, DC)
                    else:
                        pe.wait_ge(s_mqo, i)
                    lhs = lambda c: mixT[:, c, i * P:(i + 1) * P]
                    halves(1, lambda k: lhs(k), lambda k, half: wo_sb[:, k, 512 * half:512 * half + 512], s_om, 4)
                    if i >= 2:
                        pe.wait_ge(s_moto, i - 1)
                    halves(2, lambda k: lhs(4 + k), lambda k, half: wo_sb[:, 4 + k, 512 * half:512 * half + 512], s_om, 4)
                if 1 <= i <= T:
                    pe.wait_ge(s_mqo, i)
                    for half in range(2):
                        turn(("mqT", i - 1, half), [mq_sb[:, (4 * half + c) * P:(4 * half + c + 1) * P] for c in range(4)])
                    if i == 1:
                        pe.wait_ge(s_mk1, 32)
                    else:
                        pe.wait_ge(s_h2, i - 1)
                    pe.wait_ge(s_te["act"], EMPTIED[ROUND[("mqT", i - 1, 1)]][1])
                    for h in range(MH):
                        product(pair(3)[:, MEM * h:MEM * (h + 1)],
                                [(mqT[:, 2 * h + c, :], mkT1[:, 2 * h + c, :]) for c in range(2)],
                                s_msc if h == MH - 1 else None)
                if i < T:
                    pe.wait_ge(s_h1, i + 1)
                    for half in range(2):
                        turn(("hT", i, half), [h1[:, i % 2, (4 * half + c) * P:(4 * half + c + 1) * P] for c in range(4)])
                    if i == 0:
                        pe.wait_ge(s_wmqs, DC)
                    pe.wait_ge(s_te["act"], EMPTIED[ROUND[("hT", i, 1)]][1])
                    halves(1, lambda k: h1T[:, k, :], lambda k, half: wmq_sb[:, k, 512 * half:512 * half + 512], s_mq)
                if 1 <= i <= T:
                    pe.wait_ge(s_mp, i)
                    for half in range(2):
                        turn(("pT", i - 1, half), [mp[:, 2 * half + c // 2, (c % 2) * P:(c % 2 + 1) * P] for c in range(4)])
                    pe.wait_ge(s_te["act"], EMPTIED[ROUND[("pT", i - 1, 1)]][1])
                    for c in range(DC):
                        h = c // 2
                        product(pair(2)[:, c * P:(c + 1) * P],
                                [(mv1[:, m, c * P:(c + 1) * P], mpT[:, 2 * h + m, :]) for m in range(MT)],
                                s_mot if c == DC - 1 else None)
                if i >= 2:
                    for half in range(2):
                        pe.wait_ge(s_tn, i - 1)
                        turn(("tT", i - 2, half), [tn[:, (4 * half + c) * P:(4 * half + c + 1) * P] for c in range(4)])
                    if i == 2:
                        pe.wait_ge(s_wr, 64)
                    pe.wait_ge(s_te["act"], EMPTIED[ROUND[("tT", i - 2, 1)]][1])
                    dst = begin(("router", i - 2, 0))
                    product(dst[:, 0:NG + NE], [(tT[:, k, :], wr[:, k, :]) for k in range(DC)], s_t)
                if 1 <= i <= T:
                    if i == 1:
                        pe.wait_ge(s_wmo, 16)
                    pe.wait_ge(s_moto, i)
                    pe.wait_ge(s_me, MH * i)
                    halves(3, lambda k: moT[:, k, :], lambda k, half: wmo_sb[:, k, 512 * half:512 * half + 512], s_mop)

            pe.wait_ge(s_rm, 4)
            dst = begin(("rank", 0, 0))
            marks = rt[4].rearrange("p t e -> p (t e)")
            pe.matmul(dst[:, 0:T * NE], before[:, :], marks, start=True, stop=True)
            pe.matmul(dst[:, T * NE:2 * T * NE], ones[:, :], marks, start=True, stop=True).then_inc(s_t, 1)
            dst = begin(("table", 0, 0))
            for c in range(2 * T):
                pe.wait_ge(s_ab, c + 1)
                mm = pe.matmul(dst[:, 0:TAB], onehot[:, c, :], token_at[:, c, :], start=(c == 0), stop=(c == 2 * T - 1))
            mm.then_inc(s_t, 1)

            pe.wait_ge(s_idx, 1)
            pe.wait_ge(s_plan, 1)
            n_it = pe.value_load(nitt[0:1, 0:1], min_val=NE // 2, max_val=SLOTS // 2)

            def rows_in(b, loads):
                pe.wait_ge(s_xg[b], loads)
                for half in range(2):
                    for c in range(4):
                        at = (4 * half + c) * P
                        mm = pe.transpose(bank(half)[:, c * P:(c + 1) * P], xg[:, b, at:at + P], ident[:, :])
                    mm.then_inc(s_xt, 1)

            def gate(s, b, loads):
                pe.wait_ge(s_xa, s + 1)
                pe.wait_ge(s_xb, s + 1)
                pe.wait_ge(s_wg[b], loads)
                product(bank(2), [(xT[:, b, c, :], wexp[b][0][:, c, :]) for c in range(DC)], s_gf)

            def up(b, loads):
                pe.wait_ge(s_wu[b], loads)
                product(bank(3), [(xT[:, b, c, :], wexp[b][1][:, c, :]) for c in range(DC)], s_uf)

            def hidden_in(s):
                pe.wait_ge(s_h, s + 1)
                for c in range(FC):
                    mm = pe.transpose(bank(0)[:, c * P:(c + 1) * P], hrow[:, c * P:(c + 1) * P], ident[:, :])
                mm.then_inc(s_ht, 1)

            def down(s, b, loads):
                pe.wait_ge(s_hto, s + 1)
                pe.wait_ge(s_wd[b], loads)
                pe.wait_ge(s_yo, s + 1)
                halves(2 + b, lambda c: hTe[:, c, :],
                       lambda c, half: wexp[b][2][:, c, 512 * half:512 * half + 512], s_y, FC)

            def slot(s, b, loads, down_loads, next_rows):
                pe.wait_ge(s_si, s)
                gate(s, b, loads)
                hidden_in(s - 1)
                up(b, loads)
                pe.wait_ge(s_hto, s)
                rows_in(1 - b, next_rows)
                down(s - 1, 1 - b, down_loads)

            rows_in(0, 16)
            gate(0, 0, 16)
            up(0, 16)
            rows_in(1, 16)
            slot(1, 1, 16, 16, 32)
            with pe.Fori(1, n_it) as k:
                slot(2 * k, 0, 16 * k + 16, 16 * k, 16 * k + 16)
                slot(2 * k + 1, 1, 16 * k + 16, 16 * k + 16, 16 * k + 32)
            pe.wait_ge(s_xa, 2 * n_it + 1)
            hidden_in(2 * n_it - 1)
            down(2 * n_it - 1, 1, 16 * n_it)


def prod_count(u):
    return sum(blocks(v) for v in range(u + 1))


_INS = ["x", "mem", "positions", "norm_mix_g", "w_in", "mla_q_norm_g", "w_uq", "mla_kv_norm_g", "w_ukv",
        "mla_qn_g", "mla_qr_g", "mla_kn_g", "mla_kr_g", "sb_out_g", "mla_out_g", "w_o", "norm_mem_g",
        "mem_src_g", "w_mq", "w_mkv", "mem_qhead_g", "mem_khead_g", "w_mo", "norm_moe_g", "w_group",
        "b_group", "w_router", "b_router", "w_gate", "w_up", "w_down"]


def kernel(**inputs):
    import numpy as _np
    import concourse.bacc as _bacc
    from concourse import mybir as _mybir
    from concourse.bass_utils import run_bass_kernel_spmd as _run

    nc = _bacc.Bacc("TRN2", target_bir_lowering=False, num_devices=1)
    arrays, args = {}, []
    for name in _INS:
        a = _np.ascontiguousarray(inputs[name])
        arrays[f"in_{name}"] = a
        args.append(nc.dram_tensor(f"in_{name}", a.shape, _mybir.dt.from_np(a.dtype), kind="ExternalInput").ap())
    out = nc.dram_tensor("layer_out", (1, SEQ, DM), F32, kind="ExternalOutput").ap()
    moe_layer(nc, *args, out)
    r = _run(nc, [arrays], core_ids=[0])
    return r.results[0]["layer_out"]
```

```python
import math

import numpy as np
import concourse.bass as bass
from concourse import mybir
from contextlib import ExitStack

F32 = mybir.dt.float32
F32R = mybir.dt.float32r
BF16 = mybir.dt.bfloat16
I32 = mybir.dt.int32
ACT = mybir.ActivationFunctionType
ALU = mybir.AluOpType
AX = mybir.AxisListType

P = 128
SEQ, DM, MEM = 1024, 1024, 256
T, DC, MT = SEQ // P, DM // P, MEM // P
EPS = 1e-6
HEADS, HD = 8, 64
PAIRS = HEADS // 2
NOPE, ROPE = 64, 32
QK = NOPE + ROPE
HALF = ROPE // 2
QR, KVR = 384, 256
SBW = HEADS * HD
MLA0 = 3 * SBW
MLAW = QR + KVR + ROPE
THETA = 10000.0
MH, MHD = 4, 256
NG, EG = 4, 4
NE, FF = NG * EG, 512
FC = FF // P
GRP = 4
UNITS = [(h, g) for g in (1, 0) for h in range(HEADS)]
SLOTS = (2 * SEQ) // P + NE
TAB = SLOTS + 2
PARTS = 4
BIG = 64.0


class Steps:

    def __init__(self, eng, own):
        self.eng, self.own, self.counts, self.last = eng, own, {}, None

    def __call__(self, ins, sem=None):
        sem = self.own if sem is None else sem
        self.counts[sem.name] = self.counts.get(sem.name, 0) + 1
        ins.then_inc(sem, 1)
        self.last = (sem, self.counts[sem.name])

    def settle(self):
        self.eng.wait_ge(*self.last)


def blocks(u):
    return GRP * (UNITS[u][1] + 1)


def transposition_rounds():
    rounds = []

    def add(kind, key, engine, n=2):
        for half in range(n):
            rounds.append(((kind, key, half), engine))

    for m in range(MT):
        add("mem", m, "dve")
    for j in range(4):
        for t in (2 * j, 2 * j + 1):
            add("x", t, "dve")
        if j in (1, 2):
            add("mk", j - 1, "dve")
    for u in range(2 * HEADS):
        add("sb", u, "act", blocks(u))
    for i in range(T + 2):
        if i >= 2:
            add("qf", i - 2, "act")
            add("kf", i - 2, "act")
        if i < T:
            add("c", i, "act")
    for u in range(2 * HEADS):
        add("mla", u, "act", blocks(u))
    for i in range(T + 2):
        if 1 <= i <= T:
            add("mqT", i - 1, "act")
        if i < T:
            add("stats", i, "dve", 1)
            add("hT", i, "act")
        if i >= 2:
            add("tT", i - 2, "act")
        if 1 <= i <= T:
            add("pT", i - 1, "act")
        if i >= 2:
            add("router", i - 2, "dve", 1)
    add("rank", 0, "dve", 1)
    add("table", 0, "dve", 1)
    return rounds


def moe_layer(nc, x, mem, positions, norm_mix_g, w_in, mla_q_norm_g, w_uq, mla_kv_norm_g, w_ukv,
              mla_qn_g, mla_qr_g, mla_kn_g, mla_kr_g, sb_out_g, mla_out_g, w_o, norm_mem_g,
              mem_src_g, w_mq, w_mkv, mem_qhead_g, mem_khead_g, w_mo, norm_moe_g, w_group, b_group,
              w_router, b_router, w_gate, w_up, w_down, out):
    ROUNDS = transposition_rounds()
    ROUND = {key: i for i, (key, _) in enumerate(ROUNDS)}
    EMPTIED = []
    seen = {"act": 0, "dve": 0}
    for _, engine in ROUNDS:
        seen[engine] += 1
        EMPTIED.append((engine, seen[engine]))

    x2, mem2, out2 = x[0], mem[0], out[0]
    mkT_dram = nc.dram_tensor("mkT_spill", [P, DC * MEM], F32).ap()
    mv_dram = nc.dram_tensor("mv_spill", [P, MT * DM], F32).ap()
    tn_dram = nc.dram_tensor("tn_rows", [SEQ, DM], F32).ap()
    y_dram = nc.dram_tensor("expert_rows", [SLOTS * P, DM], F32).ap()

    ctx = ExitStack()
    with ctx:
        def sem(name):
            return ctx.enter_context(nc.semaphore(name))

        def small(name, shape, dt=F32):
            return ctx.enter_context(nc.sbuf_tensor(name, shape, dt))

        ARENA = 50720
        arena = small("arena", [P, ARENA])
        base = nc.sbuf_base - 4 * ARENA

        def over(name, dt, at, *dims):
            assert at + math.prod(dims) <= ARENA
            return nc.alloc_sbuf_tensor_at(name, [P, *dims], dt, offset=base + 4 * at)

        psum = ctx.enter_context(nc.psum_tensor("psum", [P, 8, 512], F32))

        def cut(at, *dims):
            n = math.prod(dims)
            assert at + n <= ARENA
            v = arena[:, at:at + n]
            if len(dims) == 2:
                v = v.rearrange("p (a b) -> p a b", a=dims[0])
            elif len(dims) == 3:
                v = v.rearrange("p (a b c) -> p a b c", a=dims[0], b=dims[1])
            return v

        hnT = cut(0, DC, SEQ)
        mixT = cut(8192, DC, SEQ)
        XIN = 4
        xin = cut(8192, XIN, DM)
        mnT = cut(12288, DC, MEM)
        k_raw = cut(14336, MT, DM)
        w_mk = cut(16384, DC, DM)
        w_mv = cut(24576, DC, DM)
        w_qkv = cut(32768, DC, 3 * SBW)
        mv0 = cut(45056, MT, DM)
        mkT0 = cut(47104, DC, MEM)
        qz = cut(16384, HEADS, SEQ)
        kT = cut(24576, PAIRS, SEQ)
        v_sb = cut(28672, T, SBW)
        f_sb = cut(32768, 2, SEQ)
        g_sb = cut(34816, 2, SEQ)
        w_rows = cut(36864, 2, GRP, SEQ)
        wT_sb = cut(45056, 2, 512)
        fall = cut(46080, 2, SEQ + 1)
        zeros = cut(48640, 1)
        mqT_h = cut(16384, HEADS, SEQ)
        mkT_h = cut(24576, HEADS, SEQ)
        v_mla = cut(32768, T, SBW)
        w_c = (cut(12288, 6, MLAW), cut(48704, 2, MLAW))
        w_q = cut(36864, 3, HEADS * QK)
        w_kv = (cut(39168, 1, HEADS * P), cut(40960, 1, HEADS * P))
        cn = cut(46592, QR + KVR)
        cT = cut(47232, 5, P)
        qfs = (cut(47872, HEADS, QK), cut(43520, HEADS, QK))
        kfs = (cut(41984, HEADS, QK), cut(44288, HEADS, QK))
        sq = cut(42752, HEADS, QK)
        p_rows = cut(36864, 2, GRP, SEQ)
        pT_sb = cut(45056, 2, 512)
        wo_sb = cut(0, DC, DM)
        wmq_sb = cut(16384, DC, DM)
        wmo_sb = cut(24576, DC, DM)
        x_in = cut(32768, DM)
        h1 = cut(33792, 2, DM)
        h1T = cut(35840, DC, P)
        mq_sb = cut(36864, DM)
        mqT = cut(37888, DC, P)
        mp = cut(38912, MH, MEM)
        mpT = cut(39936, MH * MT, P)
        moT = cut(40960, DC, P)
        tn = cut(41984, DM)
        tT = cut(43008, DC, P)
        mix_sq = cut(44032, DC, P)
        moe_g = cut(45056, DM)
        mkT1 = cut(46080, DC, MEM)
        mv1 = cut(48128, MT, DM)
        junk = cut(50176, 544)
        junk_b = junk.bitcast(BF16)
        h2 = mixT
        stage = (over("gate_stage", F32, 16384, DC, FF), over("up_stage", F32, 20480, DC, FF),
                 over("down_stage", F32, 24576, FC, DM))
        split = ((over("gate_high", F32R, 0, DC, FF), over("gate_rest", F32R, 4096, DC, FF)),
                 (over("up_high", F32R, 28672, DC, FF), over("up_rest", F32R, 32768, DC, FF)),
                 (over("down_high", F32R, 36864, FC, DM), over("down_rest", F32R, 40960, FC, DM)))
        xg = cut(45056, DM)
        xT = (over("rows_high", F32R, 46080, DC, P), over("rows_rest", F32R, 47104, DC, P))
        hrow = cut(48128, FF)
        hTe = (over("hidden_high", F32R, 48992, FC, P), over("hidden_rest", F32R, 49504, FC, P))
        rt = [cut(40960 + P * i, T, NE) for i in range(12)]
        onehot = over("onehot", F32R, 42496, 2 * T, P)
        token_at = over("token_at", F32R, 44544, 2 * T, TAB)
        y1 = cut(16384, 2, DM)
        y2 = cut(18432, 2, DM)
        yo = cut(20480, 2, DM)

        ident = small("ident", [P, P])
        before = small("before", [P, P])
        ones = small("ones", [P, P])
        cos = small("cos", [P, T, HALF])
        sin = small("sin", [P, T, HALF])
        rtmp = small("rtmp", [P, 5, P])
        mix_sum = rtmp[:, 0:2, :]
        lane = rtmp[:, 2, :]
        slot_no = rtmp[:, 3, 0:TAB]
        ysb = (rtmp[:, 0:4, :].rearrange("p a b -> p (a b)"), cut(50016, 512))
        pos_i = small("pos_i", [P, T], I32)
        posf = small("posf", [P, T])
        invf = small("invf", [P, HALF])
        gx = small("gx", [P, DC])
        gmem = small("gmem", [P, DC])
        gcq = small("gcq", [P, 5])
        gq96 = small("gq96", [P, QK])
        gk96 = small("gk96", [P, QK])
        gmh = small("gmh", [P, 4])
        gmix = small("gmix", [P, DC])
        ghq = small("ghq", [P, DC])
        kr = small("kr", [P, ROPE])
        ms = small("ms", [P, MT + T])
        rr = small("rr", [P, MT + T])
        mst = small("mst", [P, 32])
        rst = small("rst", [P, 32])
        nwt = small("nwt", [P, 32])
        mx = small("mx", [P, 4])
        nb = small("nb", [P, 4])
        rs = small("rs", [P, 4])
        ri = small("ri", [P, 4])
        st2 = small("st2", [P, 2])
        r2 = small("r2", [P, 2])
        r1 = small("r1", [P, 2])
        singles = small("singles", [P, 4])
        m1 = singles[:, 0:1]
        m4 = small("m4", [P, MH])
        v4 = small("v4", [P, MH])
        sc = small("sc", [P, MH])
        mmx = small("mmx", [P, MH])
        mnb = small("mnb", [P, MH])
        mrs = small("mrs", [P, MH])
        mri = small("mri", [P, MH])
        m2 = singles[:, 1:2]
        rt2 = singles[:, 2:3]
        wr = small("wr", [P, DC, NG + NE])
        br = small("br", [P, NG + NE])
        lg = small("lg", [P, T, NG + NE])
        rsm = cut(48640, 16, T)
        esm = cut(48768, 8, NE)
        s4 = cut(48896, 3, T, EG)
        io4 = small("io4", [P, EG])
        io16 = small("io16", [P, NE])
        slotf = small("slotf", [P, SLOTS])
        posk = small("posk", [P, 2, T], I32)
        adr = small("adr", [P, 2, 2 * T], I32)
        adrf = small("adrf", [P, 2, 2 * T])
        tokf = small("tokf", [P, T])
        thr = small("thr", [P, T - 1])
        nums = small("nums", [P, 2 * NE], I32)
        eidt = small("eidt", [P, SLOTS], I32)
        newt = small("newt", [P, SLOTS], I32)
        ends_i = small("ends_i", [P, NE], I32)
        idx_all = small("idx_all", [P, TAB], I32)
        idx = small("idx", [P, 1], I32)
        tiny = singles[:, 3:4]
        slot_cmp = junk[:, 0:SLOTS * NE].rearrange("p (s e) -> p s e", s=SLOTS)

        s_gain = sem("gains_loaded")
        s_pos = sem("positions_loaded")
        s_gcol = sem("input_gains_loaded")
        s_ang = sem("angles_ready")
        s_rot = sem("rotary_tables_ready")
        s_const = sem("constants_made")
        s_xin = [sem(f"input_tile_loaded{i}") for i in range(XIN)]
        s_wmk = [sem(f"w_mk_loaded{i}") for i in range(2)]
        s_wmv = sem("w_mv_loaded")
        s_wqkv = sem("w_qkv_loaded")
        s_sq = sem("mean_square_ready")
        s_rr = sem("rstd_ready")
        s_xn = sem("input_tile_normed")
        s_t = sem("transposition_bank_full")
        s_te = {"act": sem("transposition_bank_emptied_by_act"), "dve": sem("transposition_bank_emptied_by_dve")}
        s_mkv = sem("mem_kv_product")
        s_mkvo = sem("mem_kv_copied")
        s_mkn = sem("mem_k_normed")
        s_spill = sem("mem_kv_spilled")
        s_mk1 = sem("mem_kv_reloaded")
        s_qz = sem("query_zeros")
        s_pr = sem("sb_projection_product")
        s_proA = sem("sb_projection_copied_by_act")
        s_proD = sem("sb_projection_copied_by_dve")
        s_s = sem("sb_scores_full")
        s_f = sem("sb_fail_ready")
        s_g = sem("sb_take_ready")
        s_fm = sem("sb_fail_masked")
        s_gm = sem("sb_take_masked")
        s_w = sem("sb_weights_ready")
        s_pv = sem("sb_value_product")
        s_o = sem("sb_output_copied")
        s_wc = sem("w_c_loaded")
        s_wuq = sem("w_uq_loaded")
        s_p1 = sem("mla_down_product")
        s_csq = sem("mla_down_squares")
        s_cr = sem("mla_down_rstd")
        s_ce = sem("mla_down_normed")
        s_kre = sem("mla_rope_key_taken")
        s_p3 = sem("mla_up_product")
        s_q3 = sem("mla_up_copied")
        s_qkf = sem("mla_heads_ready")
        s_ms = sem("mla_scores_full")
        s_nb = sem("mla_maximum_ready")
        s_e = sem("mla_exp_ready")
        s_pn = sem("mla_probabilities_ready")
        s_mpv = sem("mla_value_product")
        s_mo = sem("mla_output_copied")
        s_wo = sem("w_o_loaded")
        s_wmq = [sem(f"w_mq_loaded{c}") for c in range(DC)]
        s_wmo = sem("w_mo_loaded")
        s_wos = sem("w_o_scaled")
        s_wmqs = sem("w_mq_scaled")
        s_moeg = sem("moe_gain_loaded")
        s_x = sem("x_tile_loaded")
        s_msq = sem("mixed_squares")
        s_om = sem("mix_product")
        s_h1a = sem("sb_part_added")
        s_h1 = sem("h1_ready")
        s_h1q = sem("h1_mean_square")
        s_msc = sem("mem_scores_full")
        s_mnb = sem("mem_maximum_ready")
        s_me = sem("mem_exp_ready")
        s_mp = sem("mem_probabilities_ready")
        s_mq = sem("mem_query_product")
        s_mqo = sem("mem_query_copied")
        s_mqs = sem("mem_query_scale_ready")
        s_mot = sem("mem_output_product")
        s_moto = sem("mem_output_copied")
        s_mop = sem("mem_projection_product")
        s_h2 = sem("h2_ready")
        s_h2q = sem("h2_mean_square")
        s_tn = sem("moe_input_ready")
        s_tnd = sem("moe_input_stored")
        s_wr = sem("router_loaded")
        s_rm = sem("expert_choice_ready")
        s_lane = sem("table_numbers_made")
        s_ab = sem("token_marks_ready")
        s_idx = sem("token_table_ready")
        s_plan = sem("slot_plan_ready")
        s_st = [sem(f"{m}_loaded") for m in ("gate", "up", "down")]
        s_hi = [sem(f"{m}_high_ready") for m in ("gate", "up", "down")]
        s_hip = sem("down_high_step_by_pool")
        s_lo = [sem(f"{m}_rest_ready") for m in ("gate", "up", "down")]
        s_lop = [sem(f"{m}_rest_ready_by_pool") for m in ("gate", "up", "down")]
        s_go = sem("waits_carried")
        s_ic = sem("slot_indices_ready")
        s_xg = sem("slot_rows_gathered")
        s_xt = sem("slot_rows_transposed")
        s_xh = sem("slot_rows_high_ready")
        s_xl = sem("slot_rows_rest_ready")
        s_gf = sem("gate_product")
        s_ua = sem("up_product_first_half")
        s_ub = sem("up_product_second_half")
        s_si = sem("silu_ready")
        s_h = sem("expert_hidden_ready")
        s_ht = sem("expert_hidden_transposed")
        s_hth = sem("expert_hidden_high_ready")
        s_htl = sem("expert_hidden_rest_ready")
        s_y = sem("down_product")
        s_yo = sem("down_copied")
        s_ys = sem("expert_rows_stored")
        s_cg = [sem(f"chosen_rows_gathered{b}") for b in range(2)]
        s_co = sem("combined_ready")
        s_out = [sem(f"output_stored{b}") for b in range(2)]
        s_dve = sem("dve_own")
        s_act = sem("act_own")
        s_pool = sem("pool_own")

        block = ctx.enter_context(nc.Block())
        GAINS = 10

        def bank(i):
            return psum[:, i, :]

        def pair(i):
            return psum[:, 2 * i:2 * i + 2, :].rearrange("p a b -> p (a b)")

        @block.sync
        def _(sp):
            def rows(t):
                return slice(t * P, (t + 1) * P)

            def load_tile(n):
                src = mem2[rows(n), :] if n < MT else x2[rows(n - MT), :]
                if n >= XIN:
                    last = ROUND[("mem", n - XIN, 1)] if n - XIN < MT else ROUND[("x", n - XIN - MT, 1)]
                    sp.wait_ge(s_t, last + 1)
                sp.dma_start(xin[:, n % XIN, :], src).then_inc(s_xin[n % XIN], 16)

            def chunks(w, c0, c1):
                return w[:, c0:c1].rearrange("(k p) n -> p k n", p=P)

            def load(e, part, cond=None):
                src = (w_gate, w_up, w_down)[part][bass.ds(e, 1), :, :].rearrange("e (k p) n -> p (e k) n", p=P)
                sp.dma_start(stage[part][:, :, :], src, cond=cond).then_inc(s_st[part], 16)

            load_tile(0)
            load_tile(1)
            for i in range(2):
                sp.dma_start(w_mk[:, 4 * i:4 * i + 4, :], chunks(w_mkv, 0, DM)[:, 4 * i:4 * i + 4, :]).then_inc(s_wmk[i], 16)
            load_tile(2)
            load_tile(3)
            sp.dma_start(w_mv, chunks(w_mkv, DM, 2 * DM)).then_inc(s_wmv, 16)
            with nc.allow_non_contiguous_dma(reason="small gain vectors laid along the partitions"):
                for dst, src in ((gmh[:, 0:2], mem_qhead_g.rearrange("(c p) -> p c", p=P)),
                                 (gmh[:, 2:4], mem_khead_g.rearrange("(c p) -> p c", p=P)),
                                 (gcq[:, 0:3], mla_q_norm_g.rearrange("(c p) -> p c", p=P)),
                                 (gcq[:, 3:5], mla_kv_norm_g.rearrange("(c p) -> p c", p=P)),
                                 (gq96[:, 0:NOPE], mla_qn_g.partition_broadcast(P)),
                                 (gq96[:, NOPE:QK], mla_qr_g.partition_broadcast(P)),
                                 (gk96[:, 0:NOPE], mla_kn_g.partition_broadcast(P)),
                                 (gk96[:, NOPE:QK], mla_kr_g.partition_broadcast(P)),
                                 (gmix[:, 0:4], sb_out_g.rearrange("(c p) -> p c", p=P)),
                                 (gmix[:, 4:8], mla_out_g.rearrange("(c p) -> p c", p=P))):
                    sp.dma_start(dst, src).then_inc(s_gain, 16)
                sp.dma_start(ghq[:, :], norm_mem_g.rearrange("(c p) -> p c", p=P)).then_inc(s_pos, 16)
                sp.dma_start(pos_i[:, :], positions[0].rearrange("(t p) -> p t", p=P)).then_inc(s_pos, 16)
                sp.dma_start(wr[:, :, 0:NG], w_group.rearrange("(c p) e -> p c e", p=P)).then_inc(s_wr, 16)
                sp.dma_start(wr[:, :, NG:NG + NE], w_router.rearrange("(c p) e -> p c e", p=P)).then_inc(s_wr, 16)
                sp.dma_start(br[:, 0:NG], b_group.partition_broadcast(P)).then_inc(s_wr, 16)
                sp.dma_start(br[:, NG:NG + NE], b_router.partition_broadcast(P)).then_inc(s_wr, 16)
            for j in range(4):
                if j < 3:
                    load_tile(4 + 2 * j)
                    load_tile(5 + 2 * j)
                ks = slice(2 * j, 2 * j + 2)
                sp.dma_start(w_qkv[:, ks, :], chunks(w_in, 0, 3 * SBW)[:, ks, :]).then_inc(s_wqkv, 16)
            for b in range(2):
                c = (2 + b) * SEQ
                sp.dma_start(y_dram[c:c + SEQ, :], x2).then_inc(s_ys, 16)
            sp.wait_ge(s_mkvo, 4)
            sp.dma_start(mv_dram, mv0.rearrange("p a b -> p (a b)")).then_inc(s_spill, 16)
            sp.wait_ge(s_te["dve"], EMPTIED[ROUND[("mk", 1, 1)]][1])
            sp.dma_start(mkT_dram, mkT0.rearrange("p a b -> p (a b)")).then_inc(s_spill, 16)
            sp.wait_ge(s_pr, 12)
            sp.wait_ge(s_spill, 32)
            for part, at in zip(w_c, (0, 6)):
                sp.dma_start(part, chunks(w_in, MLA0, MLA0 + MLAW)[:, at:at + part.shape[1], :]).then_inc(s_wc, 16)
            for u in (2 * HEADS - 2, 2 * HEADS - 1):
                sp.wait_ge(s_t, ROUND[("sb", u, blocks(u) - 1)] + 1)
                if u % 2 == 0:
                    sp.dma_start(w_q, chunks(w_uq, 0, HEADS * QK)).then_inc(s_wuq, 16)
                sp.dma_start(w_kv[u % 2], chunks(w_ukv, 0, HEADS * P)[:, u % 2:u % 2 + 1, :]).then_inc(s_wuq, 16)
            sp.wait_ge(s_p1, T)
            sp.dma_start(wo_sb, chunks(w_o, 0, DM)).then_inc(s_wo, 16)
            sp.wait_ge(s_t, ROUND[("kf", T - 1, 1)] + 1)
            sp.wait_ge(s_spill, 32)
            sp.dma_start(mkT1.rearrange("p a b -> p (a b)"), mkT_dram).then_inc(s_mk1, 16)
            sp.dma_start(mv1.rearrange("p a b -> p (a b)"), mv_dram).then_inc(s_mk1, 16)
            for h in range(HEADS):
                sp.wait_ge(s_ms, GRP * (HEADS + h + 1))
                sp.dma_start(wmq_sb[:, h, :], w_mq[rows(h), :]).then_inc(s_wmq[h], 16)
                sp.dma_start(wmo_sb[:, h, :], w_mo[rows(h), :]).then_inc(s_wmo, 16)
            sp.wait_ge(s_mo, 2 * HEADS)
            sp.dma_start(x_in, x2[rows(0), :]).then_inc(s_x, 16)
            sp.dma_start(moe_g, norm_moe_g.partition_broadcast(P)).then_inc(s_moeg, 16)
            for i in range(T + 1):
                if i + 1 < T:
                    sp.wait_ge(s_h1a, i + 1)
                    sp.dma_start(x_in, x2[rows(i + 1), :]).then_inc(s_x, 16)
                if i >= 1:
                    sp.wait_ge(s_tn, i)
                    sp.dma_start(tn_dram[rows(i - 1), :], tn).then_inc(s_tnd, 16)
                if i == T - 1:
                    sp.wait_ge(s_mq, T)
                    load(0, 0)
                    load(0, 1)
            sp.wait_ge(s_mop, T)
            load(0, 2)
            sp.wait_ge(s_plan, 1)
            n_slots = sp.value_load(ends_i[0:1, NE - 1:NE], min_val=NE, max_val=SLOTS - 1)

            def next_weights(s, parts, e, new):
                for part in parts:
                    sp.wait_ge(s_lo[part], s)
                    sp.wait_ge(s_lop[part], s)
                    load(e, part, new > 0)

            def store(s, counts):
                for half in range(2):
                    sp.wait_ge(s_yo, counts[half])
                    sp.dma_start(y_dram[bass.ds(s * P, P), 512 * half:512 * half + 512], ysb[half]).then_inc(s_ys, 16)

            def plan(s):
                return (sp.value_load(eidt[0:1, bass.ds(s, 1)], min_val=0, max_val=NE - 1),
                        sp.value_load(newt[0:1, bass.ds(s, 1)], min_val=0, max_val=1))

            next_weights(1, range(3), *plan(1))
            last = sp.snap(n_slots - 1)
            with sp.Fori(0, last) as s:
                e, new = plan(s + 2)
                next_weights(s + 2, (0, 1), e, new)
                store(s, (2 * s + 1, 2 * s + 2))
                next_weights(s + 2, (2,), e, new)
            both = sp.snap(2 * n_slots)
            store(last, (both, both))
            for t in range(T):
                sp.wait_ge(s_co, t + 1)
                sp.dma_start(out2[rows(t), :], yo[:, t % 2, :]).then_inc(s_out[t % 2], 16)
            for b in range(2):
                sp.wait_ge(s_out[b], 16 * T // 2)

        @block.gpsimd
        def _(pool):
            do = Steps(pool, s_pool)
            INV = (np.float32(THETA) ** (-(np.arange(HALF, dtype=np.float32) * np.float32(2.0) / np.float32(ROPE)))).astype(np.float32)
            do(pool.memset(ident[:, :], 0.0))
            do(pool.memset(ones[:, :], 1.0))
            for j in range(HALF):
                do(pool.memset(invf[:, j:j + 1], float(INV[j])))
            do.settle()
            do(pool.affine_select(out=ident[:, :], in_=ident[:, :], compare_op=ALU.not_equal, fill=1.0,
                                  base=0, pattern=[[-1, P]], channel_multiplier=1))
            do(pool.affine_select(out=before[:, :], in_=ones[:, :], compare_op=ALU.is_gt, fill=0.0,
                                  base=0, pattern=[[1, P]], channel_multiplier=-1))
            do(pool.iota(nums[:, 0:NE], pattern=[[1, NE]], base=0, channel_multiplier=0))
            do(pool.iota(nums[:, NE:NE + T - 1], pattern=[[P, T - 1]], base=P, channel_multiplier=0))
            do(pool.iota(nums[:, NE + T:NE + 2 * T], pattern=[[P, T]], base=0, channel_multiplier=1))
            do(pool.iota(eidt[:, :], pattern=[[1, SLOTS]], base=0, channel_multiplier=0))
            do.settle()
            do(pool.tensor_copy(io16[:, :], nums[:, 0:NE]))
            do(pool.tensor_copy(io4[:, :], nums[:, 0:EG]))
            do(pool.tensor_copy(thr[:, :], nums[:, NE:NE + T - 1]))
            do(pool.tensor_copy(tokf[:, :], nums[:, NE + T:NE + 2 * T]))
            do(pool.tensor_copy(slotf[:, :], eidt[:, :]))
            do.settle()
            do(pool.memset(tiny[:, :], 0.0), s_const)

            pool.wait_ge(s_mkv, 4)
            pool.memset(qz[HD:P, 0:HEADS:2, :], 0.0).then_inc(s_qz, 1)
            pool.memset(qz[0:HD, 1:HEADS:2, :], 0.0).then_inc(s_qz, 1)
            pool.wait_ge(s_pr, 12)
            pool.wait_ge(s_spill, 32)
            for b in range(2):
                pool.memset(fall[:, b, SEQ:SEQ + 1], 1.0).then_inc(s_qz, 1)
            pool.memset(zeros, 0.0).then_inc(s_qz, 1)
            for u, (h, g) in enumerate(UNITS):
                for r in range(GRP):
                    n, t = GRP * u + r, GRP * g + r
                    for buf, full, masked, fill in ((f_sb, s_f, s_fm, 1.0), (g_sb, s_g, s_gm, 0.0)):
                        block_ = buf[:, n % 2, t * P:(t + 1) * P]
                        pool.wait_ge(full, n + 1)
                        pool.affine_select(out=block_, in_=block_, compare_op=ALU.is_gt, fill=fill, base=0,
                                           pattern=[[-1, P]], channel_multiplier=1).then_inc(masked, 1)

            pool.wait_ge(s_qkf, T)
            whole = rtmp[:, 4, :].bitcast(I32)
            do(pool.iota(whole, pattern=[[1, P]], base=0, channel_multiplier=0))
            do.settle()
            do(pool.tensor_copy(lane, whole), s_lane)
            do(pool.tensor_copy(slot_no, whole[:, 0:TAB]), s_lane)

            pool.wait_ge(s_pos, 32)
            for c in range(DC):
                pool.wait_ge(s_wmq[c], 16)
                pool.tensor_scalar(wmq_sb[:, c, :], wmq_sb[:, c, :], ghq[:, c:c + 1], None, ALU.mult).then_inc(s_wmqs, 1)

            for c in range(PARTS):
                k = slice(DC // PARTS * c, DC // PARTS * (c + 1))
                pool.wait_ge(s_hi[0], c + 1)
                ins = pool.tensor_tensor(split[0][1][:, k, :], stage[0][:, k, :], split[0][0][:, k, :].bitcast(F32),
                                         ALU.subtract)
                if c >= PARTS - 2:
                    ins.then_inc(s_lo[0] if c == PARTS - 2 else s_lop[0], 1)

            pool.wait_ge(s_idx, 1)
            pool.wait_ge(s_tnd, 16 * T)

            def pick(column):
                pool.tensor_copy(idx[:, :], idx_all[:, column]).then_inc(s_ic, 1)

            def fetch():
                pool.indirect_dma_start(out=xg, out_offset=None, in_=tn_dram,
                                        in_offset=bass.IndirectOffsetOnAxis(ap=idx[:, 0:1], axis=0)).then_inc(s_xg, 16)

            def rest(s, part, used=None):
                k = slice((DC if part < 2 else FC) * (PARTS - 1) // PARTS, None)
                high, low = split[part]
                if part == 2:
                    pool.wait_ge(s_st[part], 16 * s + 16)
                    if used is not None:
                        pool.wait_ge(*used)
                        pool.sem_inc(s_go, 1)
                    pool.tensor_copy(high[:, k, :], stage[part][:, k, :]).then_inc(s_hip, 1)
                    pool.wait_ge(s_hip, s + 1)
                else:
                    pool.wait_ge(s_hi[part], PARTS * (s + 1))
                pool.tensor_tensor(low[:, k, :], stage[part][:, k, :], high[:, k, :].bitcast(F32),
                                   ALU.subtract).then_inc(s_lop[part], 1)

            pick(slice(0, 1))
            pool.wait_ge(s_ic, 1)
            fetch()
            pool.wait_ge(s_xt, 2)
            pick(slice(1, 2))
            pool.wait_ge(s_ic, 2)
            fetch()
            for part in (1, 2):
                rest(0, part)
            pool.wait_ge(s_plan, 1)
            n_slots = pool.value_load(ends_i[0:1, NE - 1:NE], min_val=NE, max_val=SLOTS - 1)
            with pool.Fori(0, n_slots) as s:
                rest(s + 1, 0)
                column = pool.snap(s + 2)
                pool.wait_ge(s_xt, 2 * s + 4)
                pick(bass.ds(column, 1))
                pool.wait_ge(s_ic, s + 3)
                pool.sem_inc(s_go, 1)
                fetch()
                rest(s + 1, 1)
                rest(s + 1, 2, (s_y, s + 1))
            all_stored, all_fetched = pool.snap(32 * n_slots + 32), pool.snap(16 * n_slots + 32)
            all_split = pool.snap(n_slots + 1)
            pool.wait_ge(s_ys, all_stored)
            for part in range(2):
                pool.wait_ge(s_lo[part], all_split)
                pool.wait_ge(s_lop[part], all_split)
            pool.wait_ge(s_xg, all_fetched)
            pool.sem_inc(s_go, 1)
            for t in range(T):
                if t >= 2:
                    pool.wait_ge(s_co, t - 1)
                for j, buf in enumerate((y1, y2)):
                    pool.indirect_dma_start(out=buf[:, t % 2, :], out_offset=None, in_=y_dram,
                                            in_offset=bass.IndirectOffsetOnAxis(ap=posk[:, j, t:t + 1], axis=0)).then_inc(s_cg[t % 2], 16)

        @block.scalar
        def _(act):
            do = Steps(act, s_act)

            with nc.allow_non_contiguous_dma(reason="small gain vectors laid along the partitions"):
                for dst, src in ((gmem, mem_src_g), (gx, norm_mix_g)):
                    act.dma_start(dst[:, :], src.rearrange("(c p) -> p c", p=P)).then_inc(s_gcol, 16)

            def empty(key, dst, src):
                i = ROUND[key]
                act.wait_ge(s_t, i + 1)
                do(act.activation(dst, src, ACT.Copy), s_te["act"])

            def squares(n):
                act.wait_ge(s_xin[n % XIN], 16 * (n // XIN + 1))
                do(act.activation(junk_b[:, 0:DM], xin[:, n % XIN, :], ACT.Square, scale=DM ** -0.5,
                                  accum_out=ms[:, n:n + 1]), s_sq)
                do.settle()

            for j in range(-1, 4):
                for n in (2 * j + 2, 2 * j + 3):
                    squares(n)
                for n in (2 * j + 2, 2 * j + 3):
                    act.wait_ge(s_rr, n // 2 + 1)
                    do(act.activation(xin[:, n % XIN, :], xin[:, n % XIN, :], ACT.Copy, scale=rr[:, n:n + 1]), s_xn)
                if j < 0:
                    continue
                act.wait_ge(s_mkv, j + 1)
                src = pair(1 + j % 3)
                if j < 2:
                    for h in range(MH):
                        do(act.activation(junk_b[:, 0:MHD], src[:, MHD * h:MHD * (h + 1)], ACT.Square,
                                          scale=MHD ** -0.5, accum_out=mst[:, MH * j + h:MH * j + h + 1]))
                        do.settle()
                    do(act.activation(k_raw[:, j, :], src, ACT.Copy), s_mkvo)
                else:
                    do(act.activation(mv0[:, j - 2, :], src, ACT.Copy), s_mkvo)
            act.wait_ge(s_ang, 1)
            for dst, src in ((sin, rtmp[:, 0, :]), (cos, rtmp[:, 1, :])):
                do(act.activation(dst[:, :, :].rearrange("p a b -> p (a b)"), src, ACT.Sin), s_rot)

            for p in range(PAIRS):
                act.wait_ge(s_pr, 2 * p + 2)
                do(act.activation(kT[:, p, :], pair(1 + (4 + 2 * p + 1) % 3), ACT.Copy), s_proA)
            act.wait_ge(s_const, 1)
            do(act.activation(m2, tiny, ACT.Sigmoid))

            def take(u, r):
                g = UNITS[u][1]
                n, L = GRP * u + r, P * (GRP * g + r + 1)
                src = pair(1 + n % 2)[:, 0:L]
                act.wait_ge(s_s, n + 1)
                if n >= 2:
                    act.wait_ge(s_w, n - 1)
                do(act.activation(f_sb[:, n % 2, 0:L], src, ACT.Sigmoid, scale=-(HD ** -0.5)), s_f)
                do(act.activation(g_sb[:, n % 2, 0:L], src, ACT.Sigmoid, scale=HD ** -0.5), s_g)

            def spread(kind, bufs, u, j, s_done):
                i = ROUND[(kind, u, j)]
                first = ROUND[(kind, 0, 0)]
                lo = P * max(0, j - GRP * UNITS[u][1])
                if i - first >= 2:
                    act.wait_ge(s_done, i - first - 1)
                empty((kind, u, j), bufs[:, (i - first) % 2, lo:512], bank(i % 2)[:, lo:512])

            def attention(kind, bufs, s_done, one):
                act_units = 2 * HEADS
                for r in range(GRP):
                    one(0, r)
                one(1, 0)
                for u in range(act_units):
                    for j in range(blocks(u)):
                        spread(kind, bufs, u, j, s_done)
                        if u + 1 < act_units and j < GRP - 1:
                            one(u + 1, 1 + j)
                    if u + 2 < act_units:
                        one(u + 2, 0)

            act.wait_ge(s_proD, 8)
            attention("sb", wT_sb, s_pv, take)

            act.wait_ge(s_gain, 16 * GAINS)
            for i in range(T + 2):
                if i < T:
                    act.wait_ge(s_p1, i + 1)
                    for c, (a, b, src) in enumerate(((0, QR, bank(2)[:, 0:QR]), (QR, QR + KVR, bank(3)[:, 0:KVR]),
                                                     (0, ROPE, bank(3)[:, KVR:KVR + ROPE]))):
                        n = b - a
                        do(act.activation(junk_b[:, 0:n], src, ACT.Square, scale=n ** -0.5,
                                          accum_out=mst[:, c:c + 1]), s_csq if c == 2 else None)
                        do.settle()
                    act.wait_ge(s_cr, i + 1)
                    do(act.activation(cn[:, 0:QR], bank(2)[:, 0:QR], ACT.Copy, scale=rst[:, 0:1]))
                    act.wait_ge(s_kre, i + 1)
                    do(act.activation(cn[:, QR:QR + KVR], bank(3)[:, 0:KVR], ACT.Copy, scale=rst[:, 1:2]), s_ce)
                if i >= 2:
                    for kind, dst in (("qf", mqT_h), ("kf", mkT_h)):
                        for half in range(2):
                            key = (kind, i - 2, half)
                            empty(key, dst[0:QK, 4 * half:4 * half + 4, (i - 2) * P:(i - 1) * P],
                                  bank(ROUND[key] % 2)[0:QK, :].rearrange("p (a b) -> p a b", a=4))
                if 1 <= i <= T:
                    act.wait_ge(s_p3, i)
                    qf, kf = qfs[(i - 1) % 2], kfs[(i - 1) % 2]
                    if i >= 3:
                        act.wait_ge(s_t, ROUND[("kf", i - 3, 1)] + 1)
                    for half in range(2):
                        hs = slice(4 * half, 4 * half + 4)
                        src = bank(4 + half)[:, 0:4 * QK].rearrange("p (a b) -> p a b", a=4)
                        kv = bank(6 + half).rearrange("p (a b) -> p a b", a=4)
                        do(act.activation(qf[:, hs, :], src, ACT.Copy))
                        do(act.activation(kf[:, hs, 0:NOPE], kv[:, :, 0:NOPE], ACT.Copy))
                        do(act.activation(v_mla[:, i - 1, 4 * half * HD:(4 * half + 4) * HD].rearrange("p (a b) -> p a b", a=4),
                                          kv[:, :, NOPE:NOPE + HD], ACT.Copy), s_q3)
                if i < T:
                    for half, chunks_ in enumerate((range(3), range(3, 5))):
                        j = ROUND[("c", i, half)]
                        act.wait_ge(s_t, j + 1)
                        for c in chunks_:
                            at = (c - chunks_[0]) * P
                            do(act.activation(cT[:, c, :], bank(j % 2)[:, at:at + P], ACT.Copy, scale=gcq[:, c:c + 1]),
                               s_te["act"] if c == chunks_[-1] else None)

            def exps(u, r):
                n, g = GRP * u + r, UNITS[u][1]
                L = P * (GRP * g + r + 1)
                act.wait_ge(s_nb, n + 1)
                if u >= 2:
                    act.wait_ge(s_t, ROUND[("mla", u - 2, blocks(u - 2) - 1)] + 1)
                if n >= 4:
                    act.wait_ge(s_pn, n - 3)
                do(act.activation(p_rows[:, u % 2, r, 0:L], pair(1 + n % 2)[:, 0:L], ACT.Exp, scale=QK ** -0.5,
                                  bias=nb[:, n % 4:n % 4 + 1], accum_out=rs[:, n % 4:n % 4 + 1]), s_e)

            attention("mla", pT_sb, s_mpv, exps)

            def wide(key2, dst):
                for half in range(2):
                    key = (*key2, half)
                    empty(key, dst[:, 4 * half:4 * half + 4, :].rearrange("p a b -> p (a b)"), bank(ROUND[key] % 2))

            for i in range(T + 2):
                if 1 <= i <= T:
                    wide(("mqT", i - 1), mqT)
                if i < T:
                    act.wait_ge(s_h1, i + 1)
                    do(act.activation(junk_b[:, 0:DM], h1[:, i % 2, :], ACT.Square, scale=DM ** -0.5,
                                      accum_out=m1[:, 0:1]), s_h1q)
                    wide(("hT", i), h1T)
                if 1 <= i <= T:
                    act.wait_ge(s_mnb, i)
                    if i >= 2:
                        act.wait_ge(s_t, ROUND[("pT", i - 2, 1)] + 1)
                    for h in range(MH):
                        do(act.activation(mp[:, h, :], pair(3)[:, MEM * h:MEM * (h + 1)], ACT.Exp, scale=sc[:, h:h + 1],
                                          bias=mnb[:, h:h + 1], accum_out=mrs[:, h:h + 1]), s_me)
                if i >= 2:
                    wide(("tT", i - 2), tT)
                if 1 <= i <= T:
                    wide(("pT", i - 1), mpT)
                if i < T:
                    act.wait_ge(s_mq, i + 1)
                    for h in range(MH):
                        do(act.activation(junk_b[:, 0:MHD], pair(1)[:, MHD * h:MHD * (h + 1)], ACT.Square,
                                          scale=MHD ** -0.5, accum_out=m4[:, h:h + 1]))
                        do.settle()
                    do(act.activation(mq_sb, pair(1), ACT.Copy), s_mqo)
                if 1 <= i <= T:
                    for half in range(2):
                        act.wait_ge(s_mot, 2 * i - 1 + half)
                        do(act.activation(moT[:, 4 * half:4 * half + 4, :].rearrange("p a b -> p (a b)"),
                                          bank(4 + half), ACT.Copy), s_moto)
                    act.wait_ge(s_h2, i)
                    do(act.activation(junk_b[:, 0:DM].rearrange("p (a b) -> p a b", a=DC), h2[:, :, (i - 1) * P:i * P],
                                      ACT.Square, scale=DM ** -0.5, accum_out=m2[:, 0:1]), s_h2q)

            act.wait_ge(s_rm, 1)
            do(act.activation(s4[:, 2, :, :], s4[:, 1, :, :], ACT.Exp), s_rm)
            do(act.activation(rsm[:, 8, :], rsm[:, 7, :], ACT.Exp), s_rm)

            def high(s, part, used):
                n = (DC if part < 2 else FC) // PARTS
                act.wait_ge(s_st[part], 16 * s + 16)
                if used is not None:
                    act.wait_ge(used, s)
                for c in range(PARTS if part < 2 else PARTS - 1):
                    k = slice(n * c, n * c + n)
                    act.activation(split[part][0][:, k, :], stage[part][:, k, :], ACT.Copy).then_inc(s_hi[part], 1)

            def rows_high(s):
                for half in range(2):
                    act.wait_ge(s_xt, 2 * s + 1 + half)
                    act.activation(xT[0][:, 4 * half:4 * half + 4, :].rearrange("p a b -> p (a b)"), bank(half),
                                   ACT.Copy).then_inc(s_xh, 1)

            act.wait_ge(s_om, 2 * T)
            high(0, 0, None)
            act.wait_ge(s_mop, T)
            high(0, 1, None)
            high(0, 2, None)
            act.wait_ge(s_plan, 1)
            n_slots = act.value_load(ends_i[0:1, NE - 1:NE], min_val=NE, max_val=SLOTS - 1)
            act.wait_ge(s_ys, 32)
            rows_high(0)
            with act.Fori(0, n_slots) as s:
                act.wait_ge(s_gf, s + 1)
                act.activation(hrow, bank(2), ACT.Silu).then_inc(s_si, 1)
                high(s + 1, 0, s_gf)
                for half in range(2):
                    act.wait_ge(s_ht, 2 * s + 1 + half)
                    act.activation(hTe[0][:, 2 * half:2 * half + 2, :].rearrange("p a b -> p (a b)"),
                                   bank(5 - 2 * half)[:, 0:2 * P], ACT.Copy).then_inc(s_hth, 1)
                    if half == 0:
                        rows_high(s + 1)
                high(s + 1, 1, s_ub)
                act.wait_ge(s_y, s + 1)
                act.wait_ge(s_ys, 32 * s + 32)
                for half in range(2):
                    act.activation(ysb[half], bank(6 + half), ACT.Copy).then_inc(s_yo, 1)
                high(s + 1, 2, s_y)

        @block.vector
        def _(dve):
            do = Steps(dve, s_dve)

            def one(ins, sem_=None):
                do(ins, sem_)
                do.settle()

            def rsqrt(y, v, sem_=None):
                n = v.shape[-1]
                w = nwt[:, 0:n]
                one(dve.tensor_scalar(w.bitcast(I32), v.bitcast(I32), 1, None, ALU.logical_shift_right))
                one(dve.tensor_scalar(y.bitcast(I32), w.bitcast(I32), -1.0, float(0x5F3759DF), ALU.mult, ALU.add))
                for step in range(3):
                    one(dve.tensor_tensor(w, y, y, ALU.mult))
                    one(dve.tensor_tensor(w, w, v, ALU.mult))
                    one(dve.tensor_scalar(w, w, -0.5, 1.5, ALU.mult, ALU.add))
                    one(dve.tensor_tensor(y, y, w, ALU.mult), sem_ if step == 2 else None)

            def rotate(dst, src, t):
                n = src.shape[1]
                c = cos[:, t, :].unsqueeze(1).to_broadcast([P, n, HALF])
                s = sin[:, t, :].unsqueeze(1).to_broadcast([P, n, HALF])
                a, b = src[:, :, 0:HALF], src[:, :, HALF:ROPE]
                v = [rtmp[:, i, 0:n * HALF].rearrange("p (a b) -> p a b", a=n) for i in range(4)]
                do(dve.tensor_tensor(v[0], a, c, ALU.mult))
                do(dve.tensor_tensor(v[1], b, s, ALU.mult))
                do(dve.tensor_tensor(v[2], b, c, ALU.mult))
                one(dve.tensor_tensor(v[3], a, s, ALU.mult))
                do(dve.tensor_tensor(dst[:, :, 0:HALF], v[0], v[1], ALU.subtract))
                one(dve.tensor_tensor(dst[:, :, HALF:ROPE], v[2], v[3], ALU.add))


            def rstds(pair_):
                dve.wait_ge(s_sq, 2 * pair_ + 2)
                c = slice(2 * pair_, 2 * pair_ + 2)
                one(dve.tensor_scalar(ms[:, c], ms[:, c], EPS, None, ALU.add))
                rsqrt(rr[:, c], ms[:, c], s_rr)

            def turned(key, dst, gain):
                i = ROUND[key]
                n = dst.shape[1]
                dve.wait_ge(s_t, i + 1)
                do(dve.tensor_tensor(dst, bank(i % 2)[:, 0:n * P].rearrange("p (a b) -> p a b", a=n),
                                     gain.unsqueeze(2).to_broadcast([P, n, P]), ALU.mult), s_te["dve"])

            rstds(0)
            dve.wait_ge(s_gcol, 32)
            for m in range(MT):
                for half in range(2):
                    hs = slice(4 * half, 4 * half + 4)
                    turned(("mem", m, half), mnT[:, hs, m * P:(m + 1) * P], gmem[:, hs])

            for j in range(4):
                rstds(j + 1)
                for t in (2 * j, 2 * j + 1):
                    for half in range(2):
                        hs = slice(4 * half, 4 * half + 4)
                        turned(("x", t, half), hnT[:, hs, t * P:(t + 1) * P], gx[:, hs])
                if j in (0, 1):
                    dve.wait_ge(s_mkvo, j + 1)
                    c = slice(MH * j, MH * j + MH)
                    one(dve.tensor_scalar(mst[:, c], mst[:, c], EPS, None, ALU.add))
                    rsqrt(rst[:, c], mst[:, c])
                    kv = k_raw[:, j, :].rearrange("p (a b) -> p a b", a=MH)
                    do(dve.tensor_tensor(kv, kv, rst[:, c].unsqueeze(2).to_broadcast([P, MH, MHD]), ALU.mult), s_mkn)
                if j == 1:
                    dve.wait_ge(s_gain, 16 * GAINS)
                    one(dve.tensor_tensor(gmh[:, 0:2], gmh[:, 0:2], gmh[:, 2:4], ALU.mult))
                if j in (1, 2):
                    m = j - 1
                    for half in range(2):
                        key = ("mk", m, half)
                        dve.wait_ge(s_t, ROUND[key] + 1)
                        src = bank(ROUND[key] % 2).rearrange("p (h c m) -> p h c m", h=2, c=2)
                        for c in range(2):
                            dst = mkT0[:, 4 * half + c:4 * half + 4:2, m * P:(m + 1) * P]
                            do(dve.tensor_scalar(dst, src[:, :, c, :], gmh[:, c:c + 1], None, ALU.mult),
                               s_te["dve"] if c else None)

            dve.wait_ge(s_pos, 32)
            dve.wait_ge(s_const, 1)
            one(dve.tensor_copy(posf[:, :], pos_i[:, :]))
            ang, cyc, tmp = rtmp[:, 0, :], rtmp[:, 1, :], rtmp[:, 2, :]
            a3 = ang.rearrange("p (a b) -> p a b", a=T)
            one(dve.tensor_tensor(a3, posf[:, :].unsqueeze(2).to_broadcast([P, T, HALF]),
                                  invf[:, :].unsqueeze(1).to_broadcast([P, T, HALF]), ALU.mult))
            one(dve.tensor_scalar(tmp, ang, 1.0 / (2 * math.pi), None, ALU.mult))
            one(dve.tensor_copy(cyc.bitcast(I32), tmp))
            one(dve.tensor_copy(tmp, cyc.bitcast(I32)))
            TWO_PI = (6.28125, 0.0019350051879882812, 3.019916e-07)
            for part in TWO_PI:
                one(dve.scalar_tensor_tensor(out=ang, in0=tmp, scalar=-part, in1=ang, op0=ALU.mult, op1=ALU.add))
            PI = float(np.nextafter(np.float32(math.pi), np.float32(0)))

            def wrap(v, w, sem_=None):
                one(dve.tensor_scalar(w, v, PI, -2 * math.pi, ALU.is_gt, ALU.mult))
                one(dve.tensor_tensor(v, v, w, ALU.add))
                one(dve.tensor_scalar(w, v, -PI, 2 * math.pi, ALU.is_lt, ALU.mult))
                one(dve.tensor_tensor(v, v, w, ALU.add))
                one(dve.tensor_scalar(v, v, PI, -PI, ALU.min, ALU.max), sem_)

            wrap(ang, tmp)
            one(dve.tensor_scalar(cyc, ang, math.pi / 2, None, ALU.add))
            wrap(cyc, tmp, s_ang)

            dve.wait_ge(s_qz, 2)
            for p in range(PAIRS):
                dve.wait_ge(s_pr, 2 * p + 1)
                src = pair(1 + (4 + 2 * p) % 3)
                do(dve.tensor_copy(qz[0:HD, 2 * p, :], src[0:HD, :]))
                do(dve.tensor_copy(qz[HD:P, 2 * p + 1, :], src[HD:P, :]), s_proD)
            for c in range(4):
                dve.wait_ge(s_pr, 9 + c)
                do(dve.tensor_copy(v_sb[:, 2 * c:2 * c + 2, :].rearrange("p a b -> p (a b)"),
                                   pair(1 + (12 + c) % 3)), s_proD)

            def out_rows(u, s_prod, s_copied, chunk0):
                h, g = UNITS[u]
                rows = slice(HD * (h % 2), HD * (h % 2) + HD)
                dve.wait_ge(s_prod, prod_count(u))
                do(dve.tensor_copy(mixT[rows, chunk0 + h // 2, 512 * g:512 * (g + 1)], bank(6 + u % 2)[rows, :]), s_copied)

            dve.wait_ge(s_qz, 5)
            for u in range(2 * HEADS):
                g = UNITS[u][1]
                for r in range(GRP):
                    n, L = GRP * u + r, P * (GRP * g + r + 1)
                    dve.wait_ge(s_fm, n + 1)
                    b = n % 2
                    one(dve.tensor_tensor_scan(fall[:, b, SEQ - L:SEQ][:, ::-1], f_sb[:, b, 0:L][:, ::-1],
                                               zeros.to_broadcast([P, L]), 1.0, ALU.mult, ALU.add))
                    dve.wait_ge(s_gm, n + 1)
                    if u >= 2 and r == 0:
                        dve.wait_ge(s_t, ROUND[("sb", u - 2, blocks(u - 2) - 1)] + 1)
                    do(dve.tensor_tensor(w_rows[:, u % 2, r, 0:L], g_sb[:, b, 0:L],
                                         fall[:, b, SEQ - L + 1:SEQ + 1], ALU.mult), s_w)
                if u >= 1:
                    out_rows(u - 1, s_pv, s_o, 0)
            out_rows(2 * HEADS - 1, s_pv, s_o, 0)

            one(dve.tensor_tensor(gk96[:, 0:NOPE], gk96[:, 0:NOPE], gq96[:, 0:NOPE], ALU.mult))

            def mla_down(i):
                dve.wait_ge(s_csq, i + 1)
                one(dve.tensor_scalar(mst[:, 0:3], mst[:, 0:3], EPS, None, ALU.add))
                rsqrt(rst[:, 0:3], mst[:, 0:3], s_cr)
                one(dve.scalar_tensor_tensor(out=kr[:, :], in0=bank(3)[:, KVR:KVR + ROPE], scalar=rst[:, 2:3],
                                             in1=gk96[:, NOPE:QK], op0=ALU.mult, op1=ALU.mult), s_kre)

            def mla_heads(t):
                dve.wait_ge(s_q3, 2 * t + 2)
                qf, kf = qfs[t % 2], kfs[t % 2]
                do(dve.tensor_tensor(sq, qf, qf, ALU.mult))
                do.settle()
                do(dve.tensor_reduce(mst[:, 8:16], sq[:, :, 0:NOPE], AX.X, ALU.add))
                one(dve.tensor_reduce(mst[:, 16:24], sq[:, :, NOPE:QK], AX.X, ALU.add))
                one(dve.tensor_tensor(sq[:, :, 0:NOPE], kf[:, :, 0:NOPE], kf[:, :, 0:NOPE], ALU.mult))
                one(dve.tensor_reduce(mst[:, 24:32], sq[:, :, 0:NOPE], AX.X, ALU.add))
                do(dve.tensor_scalar(mst[:, 8:16], mst[:, 8:16], 1.0 / NOPE, EPS, ALU.mult, ALU.add))
                do(dve.tensor_scalar(mst[:, 16:24], mst[:, 16:24], 1.0 / ROPE, EPS, ALU.mult, ALU.add))
                one(dve.tensor_scalar(mst[:, 24:32], mst[:, 24:32], 1.0 / NOPE, EPS, ALU.mult, ALU.add))
                rsqrt(rst[:, 8:32], mst[:, 8:32])

                def spread(c, n):
                    return rst[:, c:c + HEADS].unsqueeze(2).to_broadcast([P, HEADS, n])

                do(dve.tensor_tensor(qf[:, :, 0:NOPE], qf[:, :, 0:NOPE], spread(8, NOPE), ALU.mult))
                do(dve.tensor_tensor(qf[:, :, NOPE:QK], qf[:, :, NOPE:QK], spread(16, ROPE), ALU.mult))
                one(dve.tensor_tensor(kf[:, :, 0:NOPE], kf[:, :, 0:NOPE], spread(24, NOPE), ALU.mult))
                do(dve.tensor_tensor(qf[:, :, NOPE:QK], qf[:, :, NOPE:QK],
                                     gq96[:, NOPE:QK].unsqueeze(1).to_broadcast([P, HEADS, ROPE]), ALU.mult))
                one(dve.tensor_tensor(kf[:, :, 0:NOPE], kf[:, :, 0:NOPE],
                                      gk96[:, 0:NOPE].unsqueeze(1).to_broadcast([P, HEADS, NOPE]), ALU.mult))
                rotate(qf[:, :, NOPE:QK], qf[:, :, NOPE:QK], t)
                do(dve.tensor_copy(kf[:, :, NOPE:QK], krs[:, t % 2, :].unsqueeze(1).to_broadcast([P, HEADS, ROPE])), s_qkf)

            krs = rtmp[:, 4, 0:2 * ROPE].rearrange("p (a b) -> p a b", a=2)
            for i in range(T + 1):
                if i < T:
                    mla_down(i)
                    rotate(krs[:, i % 2, :].unsqueeze(1), kr[:, :].unsqueeze(1), i)
                if i >= 1:
                    mla_heads(i - 1)

            def maximum(n):
                u, r = divmod(n, GRP)
                t = GRP * UNITS[u][1] + r
                L = P * (t + 1)
                src = pair(1 + n % 2)
                dve.wait_ge(s_ms, n + 1)
                one(dve.memset(src[0:64, L - 64:L], -1e30))
                one(dve.tensor_reduce(mx[:, n % 4:n % 4 + 1], src[:, 0:L], AX.X, ALU.max))
                do(dve.tensor_scalar(nb[:, n % 4:n % 4 + 1], mx[:, n % 4:n % 4 + 1], -(QK ** -0.5), None, ALU.mult), s_nb)

            def scale_rows(n):
                u, r = divmod(n, GRP)
                L = P * (GRP * UNITS[u][1] + r + 1)
                dve.wait_ge(s_e, n + 1)
                one(dve.reciprocal(ri[:, n % 4:n % 4 + 1], rs[:, n % 4:n % 4 + 1]))
                row = p_rows[:, u % 2, r, 0:L]
                do(dve.tensor_scalar(row, row, ri[:, n % 4:n % 4 + 1], None, ALU.mult), s_pn)

            for n in range(8 * HEADS):
                maximum(n)
                if n % GRP >= 1:
                    scale_rows(n - 1)
                if n % GRP == GRP - 1:
                    scale_rows(n)
                if n >= 8 and n % 4 == 3:
                    out_rows(n // 4 - 2, s_mpv, s_mo, 4)
                if n < GRP * HEADS and n % 4 == 1:
                    c = n // 4
                    dve.wait_ge(s_wo, 16)
                    do(dve.tensor_scalar(wo_sb[:, c, :], wo_sb[:, c, :], gmix[:, c:c + 1], None, ALU.mult), s_wos)
            for u in range(2 * HEADS - 2, 2 * HEADS):
                out_rows(u, s_mpv, s_mo, 4)

            def mixed_squares(i):
                m = mixT[:, :, i * P:(i + 1) * P]
                one(dve.tensor_tensor(mix_sq, m, m, ALU.mult))
                do(dve.tensor_reduce(mix_sum, mix_sq.rearrange("p (g c) t -> p g t c", g=2), AX.X, ALU.add), s_msq)

            dve.wait_ge(s_mo, 2 * HEADS)
            mixed_squares(0)
            dve.wait_ge(s_moeg, 16)
            for i in range(T + 2):
                if i < T:
                    i_ = ROUND[("stats", i, 0)]
                    dve.wait_ge(s_t, i_ + 1)
                    one(dve.tensor_scalar(st2[:, :], bank(i_ % 2)[:, 0:2], 1.0 / SBW, EPS, ALU.mult, ALU.add), s_te["dve"])
                    rsqrt(r2[:, :], st2[:, :])
                    dve.wait_ge(s_x, 16 * (i + 1))
                    dve.wait_ge(s_om, 2 * i + 1)
                    one(dve.scalar_tensor_tensor(out=h1[:, i % 2, :], in0=pair(1), scalar=r2[:, 0:1], in1=x_in,
                                                 op0=ALU.mult, op1=ALU.add), s_h1a)
                    dve.wait_ge(s_om, 2 * i + 2)
                    one(dve.scalar_tensor_tensor(out=h1[:, i % 2, :], in0=pair(2), scalar=r2[:, 1:2], in1=h1[:, i % 2, :],
                                                 op0=ALU.mult, op1=ALU.add), s_h1)
                if i + 1 < T:
                    mixed_squares(i + 1)
                if 1 <= i <= T:
                    dve.wait_ge(s_msc, i)
                    one(dve.tensor_reduce(mmx[:, :], pair(3).rearrange("p (a b) -> p a b", a=MH), AX.X, ALU.max))
                    one(dve.tensor_tensor(mmx[:, :], mmx[:, :], sc[:, :], ALU.mult))
                    do(dve.tensor_scalar(mnb[:, :], mmx[:, :], -1.0, None, ALU.mult), s_mnb)
                if i < T:
                    dve.wait_ge(s_h1q, i + 1)
                    one(dve.tensor_scalar(r1[:, 1:2], m1[:, :], EPS, None, ALU.add))
                    rsqrt(r1[:, 0:1], r1[:, 1:2])
                    one(dve.tensor_tensor(r1[:, 1:2], r1[:, 0:1], r1[:, 0:1], ALU.mult))
                if 1 <= i <= T:
                    dve.wait_ge(s_me, MH * i)
                    one(dve.reciprocal(mri[:, :], mrs[:, :]))
                    do(dve.tensor_tensor(mp, mp, mri[:, :].unsqueeze(2).to_broadcast([P, MH, MEM]), ALU.mult), s_mp)
                if i < T:
                    dve.wait_ge(s_mqo, i + 1)
                    one(dve.tensor_scalar(v4[:, :], m4[:, :], r1[:, 1:2], EPS, ALU.mult, ALU.add))
                    rsqrt(sc[:, :], v4[:, :])
                    one(dve.tensor_scalar(sc[:, :], sc[:, :], r1[:, 0:1], MHD ** -0.5, ALU.mult, ALU.mult), s_mqs)
                if i >= 2:
                    j = ROUND[("router", i - 2, 0)]
                    dve.wait_ge(s_t, j + 1)
                    if i == 2:
                        dve.wait_ge(s_wr, 64)
                    do(dve.tensor_tensor(lg[:, i - 2, :], bank(j % 2)[:, 0:NG + NE], br[:, :], ALU.add), s_te["dve"])
                if 1 <= i <= T:
                    dve.wait_ge(s_mop, i)
                    h2v = h2[:, :, (i - 1) * P:i * P]
                    one(dve.tensor_tensor(h2v, pair(3).rearrange("p (a b) -> p a b", a=DC),
                                          h1[:, (i - 1) % 2, :].rearrange("p (a b) -> p a b", a=DC), ALU.add), s_h2)
                    dve.wait_ge(s_h2q, i)
                    one(dve.tensor_scalar(m2[:, :], m2[:, :], EPS, None, ALU.add))
                    rsqrt(rt2[:, :], m2[:, :])
                    if i >= 2:
                        dve.wait_ge(s_t, ROUND[("tT", i - 2, 1)] + 1)
                        dve.wait_ge(s_tnd, 16 * (i - 1))
                    do(dve.scalar_tensor_tensor(out=tn.rearrange("p (a b) -> p a b", a=DC), in0=h2v, scalar=rt2[:, 0:1],
                                                in1=moe_g.rearrange("p (a b) -> p a b", a=DC), op0=ALU.mult, op1=ALU.mult), s_tn)

            do.settle()
            gl = lg[:, :, 0:NG]
            el = lg[:, :, NG:NG + NE].rearrange("p t (g e) -> p t g e", g=NG)

            def over(v, n):
                return v.unsqueeze(2).to_broadcast([P, T, n])

            def along(v, n=T):
                return v.unsqueeze(1).to_broadcast([P, n, v.shape[-1]])

            def first_of(best, values, index):
                eq = s4[:, 0, :, :]
                one(dve.tensor_tensor(eq, values, over(best, EG), ALU.is_equal))
                one(dve.tensor_scalar(eq, eq, -BIG, BIG, ALU.mult, ALU.add))
                one(dve.tensor_tensor(eq, eq, along(io4[:, :]), ALU.add))
                one(dve.tensor_reduce(index, eq, AX.X, ALU.min))

            gmax, gid, top1, i1, top2, i2 = (rsm[:, c, :] for c in range(6))
            one(dve.tensor_reduce(gmax, gl, AX.X, ALU.max))
            one(dve.tensor_tensor(s4[:, 1, :, :], gl, over(gmax, NG), ALU.subtract))
            first_of(gmax, gl, gid)
            oh, sel = s4[:, 0, :, :], rt[0][:, :, 0:EG]
            one(dve.tensor_tensor(oh, along(io4[:, :]), over(gid, NG), ALU.is_equal))
            for g in range(NG):
                dst = rt[1][:, :, 0:EG] if g else sel
                one(dve.tensor_tensor(dst, el[:, :, g, :], oh[:, :, g:g + 1].to_broadcast([P, T, EG]), ALU.mult))
                if g:
                    one(dve.tensor_tensor(sel, sel, rt[1][:, :, 0:EG], ALU.add))
            one(dve.tensor_reduce(top1, sel, AX.X, ALU.max))
            first_of(top1, sel, i1)
            one(dve.tensor_tensor(oh, along(io4[:, :]), over(i1, EG), ALU.is_equal))
            one(dve.tensor_scalar(oh, oh, -3e38, None, ALU.mult))
            one(dve.tensor_tensor(sel, sel, oh, ALU.add))
            one(dve.tensor_reduce(top2, sel, AX.X, ALU.max))
            first_of(top2, sel, i2)
            one(dve.tensor_tensor(rsm[:, 7, :], top2, top1, ALU.subtract), s_rm)
            for c in (3, 5):
                one(dve.scalar_tensor_tensor(out=rsm[:, c, :], in0=gid, scalar=float(EG), in1=rsm[:, c, :],
                                             op0=ALU.mult, op1=ALU.add))
            one(dve.tensor_tensor(rt[2], along(io16[:, :]), over(i1, NE), ALU.is_equal))
            one(dve.tensor_tensor(rt[3], along(io16[:, :]), over(i2, NE), ALU.is_equal))
            one(dve.tensor_tensor(rt[4], rt[2], rt[3], ALU.add), s_rm)
            dve.wait_ge(s_rm, 4)
            one(dve.tensor_reduce(rsm[:, 9, :], s4[:, 2, :, :], AX.X, ALU.add))
            one(dve.tensor_scalar(rsm[:, 10, :], rsm[:, 8, :], 1.0, None, ALU.add))
            one(dve.tensor_tensor(rsm[:, 9, :], rsm[:, 9, :], rsm[:, 10, :], ALU.mult))
            one(dve.reciprocal(rsm[:, 11, :], rsm[:, 9, :]))
            one(dve.tensor_tensor(rsm[:, 12, :], rsm[:, 11, :], rsm[:, 8, :], ALU.mult))
            j = ROUND[("rank", 0, 0)]
            dve.wait_ge(s_t, j + 1)
            one(dve.tensor_copy(rt[5].rearrange("p t e -> p (t e)"), bank(j % 2)[:, 0:T * NE]))
            one(dve.tensor_copy(rt[6].rearrange("p t e -> p (t e)"), bank(j % 2)[:, T * NE:2 * T * NE]), s_te["dve"])
            tiles, ends = esm[:, 1, :], esm[:, 2, :]
            a, b_ = rt[6], rt[7]
            for step in (1, 2, 4):
                do(dve.tensor_copy(b_[:, 0:step, :], a[:, 0:step, :]))
                one(dve.tensor_tensor(b_[:, step:T, :], a[:, step:T, :], a[:, 0:T - step, :], ALU.add))
                a, b_ = b_, a
            do(dve.tensor_tensor(rt[5][:, 1:T, :], rt[5][:, 1:T, :], a[:, 0:T - 1, :], ALU.add))
            over_ = rt[0][:, 0:T - 1, :].rearrange("p c e -> p e c")
            one(dve.tensor_tensor(over_, a[:, T - 1, :].unsqueeze(2).to_broadcast([P, NE, T - 1]),
                                  along(thr[:, :], NE), ALU.is_gt))
            one(dve.tensor_reduce(tiles, over_, AX.X, ALU.add))
            one(dve.tensor_scalar(tiles, tiles, 1.0, None, ALU.add))
            one(dve.tensor_tensor_scan(ends, ones[:, 0:NE], tiles, 0.0, ALU.mult, ALU.add))
            one(dve.tensor_tensor(esm[:, 3, :], ends, tiles, ALU.subtract))
            one(dve.tensor_scalar(esm[:, 3, :], esm[:, 3, :], float(P), None, ALU.mult))
            one(dve.tensor_tensor(rt[5], rt[5], along(esm[:, 3, :]), ALU.add))
            do(dve.tensor_tensor(rt[6], rt[5], rt[2], ALU.mult))
            one(dve.tensor_tensor(rt[7], rt[5], rt[3], ALU.mult))
            do(dve.tensor_reduce(rsm[:, 13, :], rt[6], AX.X, ALU.add))
            one(dve.tensor_reduce(rsm[:, 14, :], rt[7], AX.X, ALU.add))
            flat = posk[:, :, :].rearrange("p c t -> p (c t)")
            one(dve.tensor_copy(flat, rsm[:, 13:15, :].rearrange("p c t -> p (c t)")))
            do(dve.tensor_scalar(adr[:, 0, :], flat, P - 1, None, ALU.bitwise_and))
            one(dve.tensor_scalar(adr[:, 1, :], flat, 7, None, ALU.logical_shift_right))
            one(dve.tensor_copy(adrf[:, :, :], adr[:, :, :]))
            dve.wait_ge(s_lane, 2)
            dve.wait_ge(s_tnd, 16 * T)
            one(dve.tensor_tensor(token_at[:, :, :], slot_no.unsqueeze(1).to_broadcast([P, 2 * T, TAB]),
                                  adrf[:, 1, :].unsqueeze(2).to_broadcast([P, 2 * T, TAB]), ALU.is_equal))
            t4 = token_at[:, :, :].rearrange("p (c t) s -> p c t s", c=2)
            one(dve.tensor_tensor(t4, t4.bitcast(F32), tokf[:, :].unsqueeze(1).unsqueeze(3).to_broadcast([P, 2, T, TAB]), ALU.mult))
            for c in range(4):
                v = slice(c * T // 2, (c + 1) * T // 2)
                do(dve.tensor_tensor(onehot[:, v, :], lane.unsqueeze(1).to_broadcast([P, T // 2, P]),
                                     adrf[:, 0, v].unsqueeze(2).to_broadcast([P, T // 2, P]), ALU.is_equal), s_ab)
            j = ROUND[("table", 0, 0)]
            dve.wait_ge(s_t, j + 1)
            one(dve.tensor_copy(idx_all[:, :], bank(j % 2)[:, 0:TAB]), s_idx)
            one(dve.tensor_tensor(slot_cmp, slotf[:, :].unsqueeze(2).to_broadcast([P, SLOTS, NE]), along(ends, SLOTS), ALU.is_ge))
            one(dve.tensor_reduce(junk[:, 512:512 + SLOTS], slot_cmp, AX.X, ALU.add))
            one(dve.tensor_scalar(junk[:, 512:512 + SLOTS], junk[:, 512:512 + SLOTS], float(NE - 1), None, ALU.min))
            one(dve.tensor_copy(eidt[:, :], junk[:, 512:512 + SLOTS]))
            one(dve.tensor_tensor(newt[:, 1:SLOTS], junk[:, 513:512 + SLOTS], junk[:, 512:511 + SLOTS], ALU.not_equal))
            one(dve.tensor_copy(ends_i[:, :], ends), s_plan)

            def rest(s, part, steps):
                n = (DC if part < 2 else FC) // PARTS
                for c in steps:
                    k = slice(n * c, n * c + n)
                    dve.wait_ge(s_hi[part], (PARTS if part < 2 else PARTS - 1) * s + c + 1)
                    ins = dve.tensor_tensor(split[part][1][:, k, :], stage[part][:, k, :],
                                            split[part][0][:, k, :].bitcast(F32), ALU.subtract)
                    if c == PARTS - 2:
                        ins.then_inc(s_lo[part], 1)

            def rows_rest(s):
                for half in range(2):
                    v = slice(4 * half, 4 * half + 4)
                    dve.wait_ge(s_xh, 2 * s + 1 + half)
                    dve.tensor_tensor(xT[1][:, v, :], bank(half).rearrange("p (a b) -> p a b", a=4),
                                      xT[0][:, v, :].bitcast(F32), ALU.subtract).then_inc(s_xl, 1)

            rows_rest(0)
            for part in (1, 2):
                rest(0, part, range(PARTS - 1))
            n_slots = dve.value_load(ends_i[0:1, NE - 1:NE], min_val=NE, max_val=SLOTS - 1)
            with dve.Fori(0, n_slots) as s:
                rest(s + 1, 0, (0,))
                for half, (full, count) in enumerate(((s_ua, s + 1), (s_ub, s + 1))):
                    cols = slice(256 * half, 256 * half + 256)
                    if half == 0:
                        dve.wait_ge(s_si, s + 1)
                    dve.wait_ge(full, count)
                    dve.tensor_tensor(hrow[:, cols], hrow[:, cols], bank(3 + half)[:, 0:256], ALU.mult).then_inc(s_h, 1)
                    if half == 0:
                        rest(s + 1, 0, (1, 2))
                for half in range(2):
                    v = slice(2 * half, 2 * half + 2)
                    dve.wait_ge(s_hth, 2 * s + 1 + half)
                    dve.tensor_tensor(hTe[1][:, v, :], bank(5 - 2 * half)[:, 0:2 * P].rearrange("p (a b) -> p a b", a=2),
                                      hTe[0][:, v, :].bitcast(F32), ALU.subtract).then_inc(s_htl, 1)
                    if half == 0:
                        rows_rest(s + 1)
                rest(s + 1, 1, range(PARTS - 1))
                rest(s + 1, 2, range(PARTS - 1))

            for t in range(T):
                dve.wait_ge(s_cg[t % 2], 32 * (t // 2 + 1))
                if t >= 2:
                    dve.wait_ge(s_out[t % 2], 16 * (t // 2))
                o3 = yo[:, t % 2, :].rearrange("p (a b) -> p a b", a=DC)
                one(dve.scalar_tensor_tensor(out=o3, in0=y1[:, t % 2, :].rearrange("p (a b) -> p a b", a=DC),
                                             scalar=rsm[:, 11, t:t + 1], in1=h2[:, :, t * P:(t + 1) * P], op0=ALU.mult, op1=ALU.add))
                one(dve.scalar_tensor_tensor(out=yo[:, t % 2, :], in0=y2[:, t % 2, :], scalar=rsm[:, 12, t:t + 1],
                                             in1=yo[:, t % 2, :], op0=ALU.mult, op1=ALU.add), s_co)

        @block.tensor
        def _(pe):
            def begin(key):
                i = ROUND[key]
                if i >= 2:
                    engine, count = EMPTIED[i - 2]
                    pe.wait_ge(s_te[engine], count)
                return bank(i % 2)

            def turn(key, blocks):
                dst = begin(key)
                at = 0
                for src in blocks:
                    rows = src.shape[-1]
                    mm = pe.transpose(dst[0:rows, at:at + P], src, ident[:, :])
                    at += P
                mm.then_inc(s_t, 1)

            def product(dst, pairs_, sem_=None):
                n = len(pairs_)
                for i, (a, b) in enumerate(pairs_):
                    mm = pe.matmul(dst, a, b, start=(i == 0), stop=(i == n - 1))
                if sem_ is not None:
                    mm.then_inc(sem_, 1)

            def halves(pair_, lhs, rhs, sem_, n=DC):
                for half in range(2):
                    product(bank(2 * pair_ + half), [(lhs(k), rhs(k, half)) for k in range(n)],
                            sem_ if half else None)

            pe.wait_ge(s_const, 1)
            for m in range(MT):
                pe.wait_ge(s_xn, m + 1)
                for half in range(2):
                    turn(("mem", m, half), [xin[:, m, (4 * half + c) * P:(4 * half + c + 1) * P] for c in range(4)])
            pe.wait_ge(s_te["dve"], EMPTIED[ROUND[("mem", 1, 1)]][1])
            for j in range(4):
                m = j % 2
                w = w_mk if j < 2 else w_mv
                if j == 3:
                    pe.wait_ge(s_mkvo, 1)
                for half in range(2):
                    if j == 2 and half == 0:
                        pe.wait_ge(s_wmv, 16)
                    for k in range(DC):
                        if j == 0 and half == 0 and k % 4 == 0:
                            pe.wait_ge(s_wmk[k // 4], 16)
                        mm = pe.matmul(bank(2 * (1 + j % 3) + half), mnT[:, k, m * P:(m + 1) * P],
                                       w[:, k, 512 * half:512 * half + 512], start=(k == 0), stop=(k == DC - 1))
                mm.then_inc(s_mkv, 1)
                for t in (2 * j, 2 * j + 1):
                    pe.wait_ge(s_xn, MT + t + 1)
                    for half in range(2):
                        turn(("x", t, half), [xin[:, (MT + t) % XIN, (4 * half + c) * P:(4 * half + c + 1) * P] for c in range(4)])
                if j in (1, 2):
                    pe.wait_ge(s_mkn, j)
                    for half in range(2):
                        turn(("mk", j - 1, half), [k_raw[:, j - 1, (4 * half + c) * P:(4 * half + c + 1) * P] for c in range(4)])

            pe.wait_ge(s_te["dve"], EMPTIED[ROUND[("x", T - 1, 1)]][1])
            pe.wait_ge(s_wqkv, 64)

            def projection_free(use):
                if use < 3 + 4 and use - 3 < 4:
                    pe.wait_ge(s_mkvo, use - 3 + 1)
                else:
                    o = use - 3 - 4
                    if o < 8:
                        pe.wait_ge(s_proA if o % 2 else s_proD, o // 2 + 1)
                    else:
                        pe.wait_ge(s_proD, 4 + o - 8 + 1)

            for p in range(PAIRS):
                for c in range(2):
                    use = 4 + 2 * p + c
                    projection_free(use)
                    col = c * SBW + p * P
                    halves(1 + use % 3, lambda k: w_qkv[:, k, col:col + P],
                           lambda k, half: hnT[:, k, 512 * half:512 * half + 512], s_pr)
            for c in range(4):
                use = 12 + c
                projection_free(use)
                for half in range(2):
                    t = 2 * c + half
                    product(bank(2 * (1 + use % 3) + half),
                            [(hnT[:, k, t * P:(t + 1) * P], w_qkv[:, k, 2 * SBW:3 * SBW]) for k in range(DC)],
                            s_pr if half else None)

            def attention(kind, rows, bufs, s_full, s_free, s_ready, s_prod, s_copied, scores, value):
                first = ROUND[(kind, 0, 0)]

                def weigh(u, j):
                    i = ROUND[(kind, u, j)]
                    h, g = UNITS[u]
                    lo = P * max(0, j - GRP * g)
                    pe.wait_ge(s_te["act"], EMPTIED[i][1])
                    if j == 0 and u >= 2:
                        pe.wait_ge(s_copied, u - 1)
                    pe.matmul(bank(6 + u % 2)[:, lo:512], value(h, j), bufs[:, (i - first) % 2, lo:512],
                              start=(j == 0), stop=(j == GRP * g + 3)).then_inc(s_prod, 1)

                def score(n):
                    u, r = divmod(n, GRP)
                    h, g = UNITS[u]
                    t = GRP * g + r
                    L = P * (t + 1)
                    if n >= 2:
                        pe.wait_ge(s_free, n - 1)
                    lhs, rhs = scores(h, t)
                    for at in range(0, L, 512):
                        end = min(L, at + 512)
                        mm = pe.matmul(pair(1 + n % 2)[:, at:end], lhs, rhs(at, end), start=True, stop=True)
                    mm.then_inc(s_full, 1)

                for n in range(GRP + 1):
                    score(n)
                for u in range(2 * HEADS):
                    g, nj = UNITS[u][1], blocks(u)
                    for j in range(nj):
                        if u + 1 < 2 * HEADS and j < GRP - 1:
                            score(GRP * (u + 1) + 1 + j)
                        pe.wait_ge(s_ready, GRP * (u + 1))
                        r0 = max(0, j - GRP * g)
                        dst = begin((kind, u, j))
                        for r in range(r0, GRP):
                            mm = pe.transpose(dst[:, r * P:(r + 1) * P], rows[:, u % 2, r, j * P:(j + 1) * P], ident[:, :])
                        mm.then_inc(s_t, 1)
                        if j >= 1:
                            weigh(u, j - 1)
                    if u + 2 < 2 * HEADS:
                        score(GRP * (u + 2))
                    weigh(u, nj - 1)

            pe.wait_ge(s_proA, 4)
            pe.wait_ge(s_proD, 8)
            attention("sb", w_rows, wT_sb, s_s, s_g, s_w, s_pv, s_o,
                      lambda h, t: (qz[:, h, t * P:(t + 1) * P], lambda a, b: kT[:, h // 2, a:b]),
                      lambda h, j: v_sb[:, j, P * (h // 2):P * (h // 2 + 1)])

            pe.wait_ge(s_o, 2 * HEADS)
            pe.wait_ge(s_g, 8 * HEADS)
            for i in range(T + 2):
                if i < T:
                    if i == 0:
                        pe.wait_ge(s_wc, 32)
                    else:
                        pe.wait_ge(s_ce, i)
                        pe.wait_ge(s_kre, i)
                    lhs = [hnT[:, k, i * P:(i + 1) * P] for k in range(DC)]
                    wc = [w_c[k // 6][:, k % 6, :] for k in range(DC)]
                    product(bank(2)[:, 0:QR], [(lhs[k], wc[k][:, 0:QR]) for k in range(DC)])
                    product(bank(3)[:, 0:KVR + ROPE], [(lhs[k], wc[k][:, QR:MLAW]) for k in range(DC)], s_p1)
                if 1 <= i <= T:
                    if i == 1:
                        pe.wait_ge(s_wuq, 48)
                    else:
                        pe.wait_ge(s_q3, 2 * (i - 1))
                    pe.wait_ge(s_te["act"], EMPTIED[ROUND[("c", i - 1, 1)]][1])
                    for half in range(2):
                        product(bank(4 + half)[:, 0:4 * QK],
                                [(cT[:, k, :], w_q[:, k, 4 * QK * half:4 * QK * (half + 1)]) for k in range(3)])
                    for half in range(2):
                        product(bank(6 + half), [(cT[:, 3 + k, :], w_kv[k][:, 0, 512 * half:512 * half + 512]) for k in range(2)],
                                s_p3 if half else None)
                if i >= 2:
                    pe.wait_ge(s_qkf, i - 1)
                    for kind, src in (("qf", qfs[i % 2]), ("kf", kfs[i % 2])):
                        for half in range(2):
                            turn((kind, i - 2, half), [src[:, 4 * half + c, :] for c in range(4)])
                if i < T:
                    pe.wait_ge(s_ce, i + 1)
                    turn(("c", i, 0), [cn[:, c * P:(c + 1) * P] for c in range(3)])
                    turn(("c", i, 1), [cn[:, c * P:(c + 1) * P] for c in range(3, 5)])

            pe.wait_ge(s_te["act"], EMPTIED[ROUND[("kf", T - 1, 1)]][1])
            attention("mla", p_rows, pT_sb, s_ms, s_e, s_pn, s_mpv, s_mo,
                      lambda h, t: (mqT_h[0:QK, h, t * P:(t + 1) * P], lambda a, b: mkT_h[0:QK, h, a:b]),
                      lambda h, j: v_mla[:, j, P * (h // 2):P * (h // 2 + 1)])

            def share(pair_, half, ks, lhs, w, sem_=None, ready=None):
                if ready is not None:
                    pe.wait_ge(*ready)
                for k in ks:
                    mm = pe.matmul(bank(2 * pair_ + half), lhs[:, k, :], w[:, k, 512 * half:512 * half + 512],
                                   start=(k == 0), stop=(k == DC - 1))
                if sem_ is not None:
                    mm.then_inc(sem_, 1)

            low, high_ = range(4), range(4, DC)
            pe.wait_ge(s_e, 8 * HEADS)
            for i in range(T + 2):
                if 1 <= i <= T:
                    pe.wait_ge(s_mqo, i)
                    for half in range(2):
                        turn(("mqT", i - 1, half), [mq_sb[:, (4 * half + c) * P:(4 * half + c + 1) * P] for c in range(4)])
                if i < T:
                    if i == 0:
                        pe.wait_ge(s_wos, DC)
                    else:
                        pe.wait_ge(s_mqo, i)
                    lhs = lambda c: mixT[:, c, i * P:(i + 1) * P]
                    halves(1, lambda k: lhs(k), lambda k, half: wo_sb[:, k, 512 * half:512 * half + 512], s_om, 4)
                    pe.wait_ge(s_msq, i + 1)
                    dst = begin(("stats", i, 0))
                    for c in range(2):
                        product(dst[:, c:c + 1], [(mix_sum[:, c, :], ones[:, 0:1])], s_t if c else None)
                    if i >= 2:
                        pe.wait_ge(s_moto, 2 * (i - 1))
                    halves(2, lambda k: lhs(4 + k), lambda k, half: wo_sb[:, 4 + k, 512 * half:512 * half + 512], s_om, 4)
                if 1 <= i <= T:
                    if i == 1:
                        pe.wait_ge(s_mk1, 32)
                    else:
                        pe.wait_ge(s_h2, i - 1)
                    pe.wait_ge(s_te["act"], EMPTIED[ROUND[("mqT", i - 1, 1)]][1])
                    for h in range(MH):
                        product(pair(3)[:, MEM * h:MEM * (h + 1)],
                                [(mqT[:, 2 * h + c, :], mkT1[:, 2 * h + c, :]) for c in range(2)],
                                s_msc if h == MH - 1 else None)
                if i < T:
                    pe.wait_ge(s_h1, i + 1)
                    for half in range(2):
                        turn(("hT", i, half), [h1[:, i % 2, (4 * half + c) * P:(4 * half + c + 1) * P] for c in range(4)])
                    if i == 0:
                        pe.wait_ge(s_wmqs, DC)
                    share(1, 0, low, h1T, wmq_sb, ready=(s_te["act"], EMPTIED[ROUND[("hT", i, 0)]][1]))
                    share(1, 0, high_, h1T, wmq_sb, ready=(s_te["act"], EMPTIED[ROUND[("hT", i, 1)]][1]))
                if i >= 2:
                    pe.wait_ge(s_tn, i - 1)
                    for half in range(2):
                        turn(("tT", i - 2, half), [tn[:, (4 * half + c) * P:(4 * half + c + 1) * P] for c in range(4)])
                if i < T:
                    share(1, 1, low, h1T, wmq_sb)
                if 1 <= i <= T:
                    pe.wait_ge(s_mp, i)
                    for half in range(2):
                        turn(("pT", i - 1, half), [mp[:, 2 * half + c // 2, (c % 2) * P:(c % 2 + 1) * P] for c in range(4)])
                if i < T:
                    share(1, 1, high_, h1T, wmq_sb, sem_=s_mq)
                if i >= 2:
                    if i == 2:
                        pe.wait_ge(s_wr, 64)
                    pe.wait_ge(s_te["act"], EMPTIED[ROUND[("tT", i - 2, 1)]][1])
                    dst = begin(("router", i - 2, 0))
                    product(dst[:, 0:NG + NE], [(tT[:, k, :], wr[:, k, :]) for k in range(DC)], s_t)
                if 1 <= i <= T:
                    pe.wait_ge(s_te["act"], EMPTIED[ROUND[("pT", i - 1, 1)]][1])
                    for c in range(DC):
                        h = c // 2
                        product(pair(2)[:, c * P:(c + 1) * P],
                                [(mv1[:, m, c * P:(c + 1) * P], mpT[:, 2 * h + m, :]) for m in range(MT)],
                                s_mot if c % 4 == 3 else None)
                    if i == 1:
                        pe.wait_ge(s_wmo, 16 * DC)
                    pe.wait_ge(s_me, MH * i)
                    share(3, 0, low, moT, wmo_sb, ready=(s_moto, 2 * i - 1))
                    share(3, 0, high_, moT, wmo_sb, ready=(s_moto, 2 * i))
                    share(3, 1, range(DC), moT, wmo_sb, sem_=s_mop)

            pe.wait_ge(s_rm, 4)
            dst = begin(("rank", 0, 0))
            marks = rt[4].rearrange("p t e -> p (t e)")
            pe.matmul(dst[:, 0:T * NE], before[:, :], marks, start=True, stop=True)
            pe.matmul(dst[:, T * NE:2 * T * NE], ones[:, :], marks, start=True, stop=True).then_inc(s_t, 1)
            dst = begin(("table", 0, 0))
            for c in range(2 * T):
                if c % (T // 2) == 0:
                    pe.wait_ge(s_ab, c // (T // 2) + 1)
                mm = pe.matmul(dst[:, 0:TAB], onehot[:, c, :], token_at[:, c, :], start=(c == 0), stop=(c == 2 * T - 1))
            mm.then_inc(s_t, 1)

            def split_product(dst, n, lhs, rhs, sem_=None, ks=None):
                for k in (range(n) if ks is None else ks):
                    for i, (a, b) in enumerate(((0, 0), (0, 1), (1, 0))):
                        mm = pe.matmul(dst, lhs(a, k), rhs(b, k), start=(k == 0 and i == 0), stop=(k == n - 1 and i == 2))
                if sem_ is not None:
                    mm.then_inc(sem_, 1)

            def rows_in(s):
                pe.wait_ge(s_xg, 16 * s + 16)
                for half in range(2):
                    for c in range(4):
                        at = (4 * half + c) * P
                        mm = pe.transpose(bank(half)[:, c * P:(c + 1) * P], xg[:, at:at + P], ident[:, :])
                    mm.then_inc(s_xt, 1)

            def weights(s, part):
                pe.wait_ge(s_lo[part], s + 1)
                pe.wait_ge(s_lop[part], s + 1)

            pe.wait_ge(s_idx, 1)
            pe.wait_ge(s_plan, 1)
            n_slots = pe.value_load(ends_i[0:1, NE - 1:NE], min_val=NE, max_val=SLOTS - 1)
            rows_in(0)
            with pe.Fori(0, n_slots) as s:
                pe.wait_ge(s_xl, 2 * s + 2)
                weights(s, 0)
                rows = lambda a, k: xT[a][:, k, :]
                split_product(bank(2), DC, rows, lambda b, k: split[0][b][:, k, :], s_gf)
                weights(s, 1)
                for half, full in enumerate((s_ua, s_ub)):
                    cols = slice(256 * half, 256 * half + 256)
                    split_product(bank(3 + half)[:, 0:256], DC, rows, lambda b, k: split[1][b][:, k, cols], full)
                for half in range(2):
                    pe.wait_ge(s_h, 2 * s + 1 + half)
                    for c in range(2):
                        at = (2 * half + c) * P
                        mm = pe.transpose(bank(5 - 2 * half)[:, c * P:(c + 1) * P], hrow[:, at:at + P], ident[:, :])
                    mm.then_inc(s_ht, 1)
                    if half == 0:
                        rows_in(s + 1)
                weights(s, 2)
                for part in range(2):
                    pe.wait_ge(s_htl, 2 * s + 1 + part)
                    for half in range(2):
                        split_product(bank(6 + half), FC, lambda a, k: hTe[a][:, k, :],
                                      lambda b, k: split[2][b][:, k, 512 * half:512 * half + 512],
                                      s_y if part and half else None, range(2 * part, 2 * part + 2))


def prod_count(u):
    return sum(blocks(v) for v in range(u + 1))


_INS = ["x", "mem", "positions", "norm_mix_g", "w_in", "mla_q_norm_g", "w_uq", "mla_kv_norm_g", "w_ukv",
        "mla_qn_g", "mla_qr_g", "mla_kn_g", "mla_kr_g", "sb_out_g", "mla_out_g", "w_o", "norm_mem_g",
        "mem_src_g", "w_mq", "w_mkv", "mem_qhead_g", "mem_khead_g", "w_mo", "norm_moe_g", "w_group",
        "b_group", "w_router", "b_router", "w_gate", "w_up", "w_down"]


def kernel(**inputs):
    import numpy as _np
    import concourse.bacc as _bacc
    from concourse import mybir as _mybir
    from concourse.bass_utils import run_bass_kernel_spmd as _run

    nc = _bacc.Bacc("TRN2", target_bir_lowering=False, num_devices=1)
    arrays, args = {}, []
    for name in _INS:
        a = _np.ascontiguousarray(inputs[name])
        arrays[f"in_{name}"] = a
        args.append(nc.dram_tensor(f"in_{name}", a.shape, _mybir.dt.from_np(a.dtype), kind="ExternalInput").ap())
    out = nc.dram_tensor("layer_out", (1, SEQ, DM), F32, kind="ExternalOutput").ap()
    moe_layer(nc, *args, out)
    r = _run(nc, [arrays], core_ids=[0])
    return r.results[0]["layer_out"]
```
